# Optimizing a Trainium2 kernel written in Bass

```python
import math
import jax, jax.numpy as jnp
from jax import lax
import numpy as np

D_MODEL = 1024
BATCH = 1
SEQ = 512
DEPTH = 2

CHUNK = 64
N_EVEN = (DEPTH + 1) // 2
N_ODD = DEPTH // 2
EPS = 1e-6
LN_EPS = 1e-5
ROPE_THETA = 10000.0

CONV_DIM = D_MODEL
CONV_WIDTH = 31
RWKV_HEAD = 64
RWKV_HEADS = D_MODEL // RWKV_HEAD
RWKV_DIM = RWKV_HEADS * RWKV_HEAD
LORA_DIM = 64
GN_EPS = 64e-5
ATT_HEADS = 16
ATT_HEAD_DIM = 128
ATT_DIM = ATT_HEADS * ATT_HEAD_DIM
IDX_HEADS = 8
IDX_HEAD_DIM = 64
TOPK_MAX = 256
Q_BLOCK = 128

EVEN_SIZES = (CONV_DIM, CONV_DIM, CONV_DIM,
              RWKV_DIM, RWKV_DIM, RWKV_DIM,
              LORA_DIM, LORA_DIM, RWKV_DIM)
EVEN_COLS = sum(EVEN_SIZES)
EVEN_OUT = CONV_DIM + RWKV_DIM
ODD_SIZES = (ATT_DIM, ATT_HEAD_DIM, ATT_HEAD_DIM,
             IDX_HEADS * IDX_HEAD_DIM, IDX_HEAD_DIM, IDX_HEADS,
             ATT_DIM)
ODD_COLS = sum(ODD_SIZES)


def split_cols(z, sizes):
    idx = np.cumsum(sizes)[:-1].tolist()
    return jnp.split(z, idx, axis=-1)

def rms_norm(x, g):
    xf = x.astype(jnp.float32)
    y = xf * lax.rsqrt(jnp.mean(xf * xf, axis=-1, keepdims=True) + EPS)
    return (y * g.astype(jnp.float32)).astype(x.dtype)

def layer_norm(x, w, b, eps):
    xf = x.astype(jnp.float32)
    mu = jnp.mean(xf, axis=-1, keepdims=True)
    var = jnp.mean(jnp.square(xf - mu), axis=-1, keepdims=True)
    y = (xf - mu) * lax.rsqrt(var + eps)
    return (y * w.astype(jnp.float32) + b.astype(jnp.float32)).astype(x.dtype)

def rope(x, pos):
    d = x.shape[-1]
    inv = ROPE_THETA ** (-jnp.arange(0, d, 2, dtype=jnp.float32) / d)
    ang = pos.astype(jnp.float32)[..., None] * inv
    cos = jnp.cos(ang)[:, :, None, :]
    sin = jnp.sin(ang)[:, :, None, :]
    xf = x.astype(jnp.float32)
    x1, x2 = jnp.split(xf, 2, axis=-1)
    out = jnp.concatenate([x1 * cos - x2 * sin, x2 * cos + x1 * sin], axis=-1)
    return out.astype(x.dtype)

def token_shift(z):
    return jnp.pad(z[:, :-1], ((0, 0), (1, 0), (0, 0)))

def conformer_conv(val, glu, conv_w, conv_vec):
    u = val * jax.nn.sigmoid(glu)
    y = lax.conv_general_dilated(u, conv_w.astype(u.dtype), window_strides=(1,),
                                 padding=[(CONV_WIDTH - 1, 0)],
                                 dimension_numbers=('NWC', 'WIO', 'NWC'),
                                 feature_group_count=CONV_DIM)
    y = y + conv_vec[0]
    y = layer_norm(y, conv_vec[1], conv_vec[2], LN_EPS)
    return jax.nn.silu(y)

def rwkv7_step(state, inp):
    r_t, w_t, k_t, v_t, kk_t, a_t = inp
    sa = jnp.einsum('bhvk,bhk->bhv', state, -kk_t)
    state = (state * w_t[:, :, None, :]
             + sa[..., None] * (kk_t * a_t)[:, :, None, :]
             + v_t[..., None] * k_t[:, :, None, :])
    y = jnp.einsum('bhvk,bhk->bhv', state, r_t)
    return state, y

def rwkv7_mix(r, k, v, wd, ad, mu_rkv, mu_lora, vec, w_up, a_up, r_k):
    B, S, _ = r.shape
    f32 = jnp.float32
    lerp = lambda z, mu: z + (token_shift(z) - z) * mu
    r = lerp(r, mu_rkv[0]).astype(f32)
    k = lerp(k, mu_rkv[1]).astype(f32)
    v = lerp(v, mu_rkv[2]).astype(f32)
    wd = lerp(wd, mu_lora[0]).astype(f32)
    ad = lerp(ad, mu_lora[1]).astype(f32)
    vec = vec.astype(f32)
    w0, a0, k_k, k_a, lnx_w, lnx_b = vec[0], vec[1], vec[2], vec[3], vec[4], vec[5]
    w_log = -jax.nn.softplus(-(w0 + jnp.tanh(wd) @ w_up.astype(f32))) - 0.5
    decay = jnp.exp(-jnp.exp(w_log))
    a = jax.nn.sigmoid(a0 + ad @ a_up.astype(f32))
    heads = lambda t: t.reshape(B, S, RWKV_HEADS, RWKV_HEAD)
    kk = heads(k * k_k)
    kk = kk / jnp.maximum(jnp.sqrt(jnp.sum(kk * kk, axis=-1, keepdims=True)), 1e-12)
    k = k * (1.0 + (a - 1.0) * k_a)
    r_h, w_h, k_h, v_h, a_h = heads(r), heads(decay), heads(k), heads(v), heads(a)
    xs = tuple(jnp.moveaxis(t, 1, 0) for t in (r_h, w_h, k_h, v_h, kk, a_h))
    state0 = jnp.zeros((B, RWKV_HEADS, RWKV_HEAD, RWKV_HEAD), f32)
    _, y = lax.scan(rwkv7_step, state0, xs)
    y = jnp.moveaxis(y, 0, 1)
    mu = jnp.mean(y, axis=-1, keepdims=True)
    var = jnp.mean(jnp.square(y - mu), axis=-1, keepdims=True)
    y = ((y - mu) * lax.rsqrt(var + GN_EPS)).reshape(B, S, RWKV_DIM) * lnx_w + lnx_b
    bonus = jnp.sum(r_h * k_h * r_k.astype(f32), axis=-1, keepdims=True) * v_h
    return y + bonus.reshape(B, S, RWKV_DIM)

def dsa_attention(q, k, v, qi, ki, wi, positions):
    B, S = positions.shape
    k_sel = min(TOPK_MAX, S // 4)
    nb = S // Q_BLOCK
    chunk_id = positions // CHUNK
    kf = ki.astype(jnp.float32)

    def to_blocks(t):
        return jnp.moveaxis(t.reshape((B, nb, Q_BLOCK) + t.shape[2:]), 1, 0)

    def block(args):
        qb, qib, wib, cqb = args
        idx_logits = jnp.einsum('bqhd,bsd->bqhs', qib.astype(jnp.float32), kf) * (IDX_HEAD_DIM ** -0.5)
        score = jnp.einsum('bqh,bqhs->bqs', wib.astype(jnp.float32) * (IDX_HEADS ** -0.5),
                           jax.nn.relu(idx_logits))
        adm = chunk_id[:, None, :] <= cqb[:, :, None]
        score = jnp.where(adm, score, -jnp.inf)
        top_val, top_idx = lax.top_k(score, k_sel)
        valid = jnp.isfinite(top_val)
        kg = jax.vmap(lambda kb, ib: kb[ib])(k, top_idx)
        vg = jax.vmap(lambda vb, ib: vb[ib])(v, top_idx)
        logits = jnp.einsum('bqhd,bqkd->bqhk', qb, kg).astype(jnp.float32) * (ATT_HEAD_DIM ** -0.5)
        logits = jnp.where(valid[:, :, None, :], logits, -jnp.inf)
        p = jax.nn.softmax(logits, axis=-1).astype(v.dtype)
        return jnp.einsum('bqhk,bqkd->bqhd', p, vg)

    o = lax.map(block, (to_blocks(q), to_blocks(qi), to_blocks(wi), to_blocks(chunk_id)))
    return jnp.moveaxis(o, 0, 1).reshape(B, S, ATT_DIM)

def first_inputs(seed: int = 0) -> dict:
    key = jax.random.key(seed)
    ks = jax.random.split(key, 24)
    nrm = lambda k, shape, s: jax.random.normal(k, shape, jnp.float32) * s
    x = nrm(ks[0], (BATCH, SEQ, D_MODEL), 1.0)
    c = nrm(ks[1], (BATCH, D_MODEL), 1.0)
    offsets = jax.random.randint(ks[2], (BATCH,), 0, 64, dtype=jnp.int32) * CHUNK
    positions = offsets[:, None] + jnp.arange(SEQ, dtype=jnp.int32)[None, :]
    ada_w = nrm(ks[3], (DEPTH, D_MODEL, 3 * D_MODEL), 0.5 * D_MODEL ** -0.5)
    ada_b = nrm(ks[4], (DEPTH, 3 * D_MODEL), 0.02)
    norm_g = 1.0 + nrm(ks[5], (DEPTH, D_MODEL), 0.05)
    final_g = 1.0 + nrm(ks[6], (D_MODEL,), 0.05)
    even_w_in = nrm(ks[7], (N_EVEN, D_MODEL, EVEN_COLS), D_MODEL ** -0.5)
    even_w_out = nrm(ks[8], (N_EVEN, EVEN_OUT, D_MODEL), EVEN_OUT ** -0.5)
    conv_w = nrm(ks[9], (N_EVEN, CONV_WIDTH, 1, CONV_DIM), CONV_WIDTH ** -0.5)
    kc = jax.random.split(ks[10], 3)
    conv_vec = jnp.stack([nrm(kc[0], (N_EVEN, CONV_DIM), 0.02),
                          1.0 + nrm(kc[1], (N_EVEN, CONV_DIM), 0.05),
                          nrm(kc[2], (N_EVEN, CONV_DIM), 0.02)], axis=1)
    rwkv_mu_rkv = jax.random.uniform(ks[11], (N_EVEN, 3, RWKV_DIM), jnp.float32)
    rwkv_mu_lora = jax.random.uniform(ks[12], (N_EVEN, 2, LORA_DIM), jnp.float32)
    kv = jax.random.split(ks[13], 6)
    rwkv_vec = jnp.stack([
        jax.random.uniform(kv[0], (N_EVEN, RWKV_DIM), jnp.float32, -4.0, 1.0),
        nrm(kv[1], (N_EVEN, RWKV_DIM), 0.1),
        0.85 + nrm(kv[2], (N_EVEN, RWKV_DIM), 0.05),
        1.0 + nrm(kv[3], (N_EVEN, RWKV_DIM), 0.05),
        1.0 + nrm(kv[4], (N_EVEN, RWKV_DIM), 0.05),
        nrm(kv[5], (N_EVEN, RWKV_DIM), 0.02)], axis=1)
    rwkv_w_up = nrm(ks[14], (N_EVEN, LORA_DIM, RWKV_DIM), 0.5 * LORA_DIM ** -0.5)
    rwkv_a_up = nrm(ks[15], (N_EVEN, LORA_DIM, RWKV_DIM), 0.5 * LORA_DIM ** -0.5)
    rwkv_r_k = nrm(ks[16], (N_EVEN, RWKV_HEADS, RWKV_HEAD), 0.1)
    odd_w_in = nrm(ks[17], (N_ODD, D_MODEL, ODD_COLS), D_MODEL ** -0.5)
    odd_w_out = nrm(ks[18], (N_ODD, ATT_DIM, D_MODEL), ATT_DIM ** -0.5)
    return {"x": x, "c": c, "positions": positions, "ada_w": ada_w, "ada_b": ada_b,
            "norm_g": norm_g, "final_g": final_g, "even_w_in": even_w_in,
            "even_w_out": even_w_out, "conv_w": conv_w, "conv_vec": conv_vec,
            "rwkv_mu_rkv": rwkv_mu_rkv, "rwkv_mu_lora": rwkv_mu_lora, "rwkv_vec": rwkv_vec,
            "rwkv_w_up": rwkv_w_up, "rwkv_a_up": rwkv_a_up, "rwkv_r_k": rwkv_r_k,
            "odd_w_in": odd_w_in, "odd_w_out": odd_w_out}

def first_block(x, c, positions, ada_w, ada_b, norm_g, final_g, even_w_in, even_w_out,
              conv_w, conv_vec, rwkv_mu_rkv, rwkv_mu_lora, rwkv_vec, rwkv_w_up, rwkv_a_up,
              rwkv_r_k, odd_w_in, odd_w_out):
    B, S, _ = x.shape
    cond = jax.nn.silu(c)
    for l in range(DEPTH):
        mod = cond @ ada_w[l] + ada_b[l]
        shift, scale, gate = jnp.split(mod, 3, axis=-1)
        h = rms_norm(x, norm_g[l]) * (1.0 + scale[:, None, :]) + shift[:, None, :]
        j = l // 2
        if l % 2 == 0:
            z = h @ even_w_in[j]
            a_val, a_glu, a_gate, r, k, v, wd, ad, b_gate = split_cols(z, EVEN_SIZES)
            ya = conformer_conv(a_val, a_glu, conv_w[j], conv_vec[j]) * jax.nn.silu(a_gate)
            yb = rwkv7_mix(r, k, v, wd, ad, rwkv_mu_rkv[j], rwkv_mu_lora[j], rwkv_vec[j],
                           rwkv_w_up[j], rwkv_a_up[j], rwkv_r_k[j]).astype(h.dtype)
            yb = yb * jax.nn.silu(b_gate)
            out = jnp.concatenate([ya, yb], axis=-1) @ even_w_out[j]
        else:
            z = h @ odd_w_in[j]
            q, k, v, qi, ki, wi, g = split_cols(z, ODD_SIZES)
            q = rope(q.reshape(B, S, ATT_HEADS, ATT_HEAD_DIM), positions)
            k = rope(k[:, :, None, :], positions)[:, :, 0, :]
            qi = rope(qi.reshape(B, S, IDX_HEADS, IDX_HEAD_DIM), positions)
            ki = rope(ki[:, :, None, :], positions)[:, :, 0, :]
            o = dsa_attention(q, k, v, qi, ki, wi, positions)
            out = (o * jax.nn.silu(g)) @ odd_w_out[j]
        x = x + gate[:, None, :] * out
    return rms_norm(x, final_g)


N_MIXERS = 2
N_LRU_LAYERS = (DEPTH + 1) // 2
N_FOX_LAYERS = DEPTH // 2
LRU_WIDTH = 1536
LRU_BLOCKS = 12
LRU_BLOCK_W = LRU_WIDTH // LRU_BLOCKS
CONV_WIDTH_2 = 4
LRU_C = 8.0
FOX_HEADS = 16
FOX_HEAD_DIM = 64
FOX_WIDTH = FOX_HEADS * FOX_HEAD_DIM
NEG_INF = -1e30


def rms_norm_2(x, g):
    xf = x.astype(jnp.float32)
    y = xf * lax.rsqrt(jnp.mean(xf * xf, axis=-1, keepdims=True) + EPS)
    return (y * g.astype(jnp.float32)).astype(x.dtype)

def causal_depthwise_conv(x, w, b):
    c = x.shape[-1]
    y = lax.conv_general_dilated(
        x, w[:, None, :].astype(x.dtype), window_strides=(1,),
        padding=[(CONV_WIDTH_2 - 1, 0)],
        dimension_numbers=("NWC", "WIO", "NWC"),
        feature_group_count=c)
    return y + b.astype(x.dtype)

def block_diag_linear(x, w, b):
    bsz, s, _ = x.shape
    xb = x.reshape(bsz, s, LRU_BLOCKS, LRU_BLOCK_W)
    y = jnp.einsum("bsnc,ncd->bsnd", xb, w.astype(x.dtype))
    return y.reshape(bsz, s, LRU_WIDTH) + b.astype(x.dtype)

def lru_mixer(h, w_in, conv_w, conv_b, wa, ba, wx, bx, a_param, w_out):
    u = h @ w_in.astype(h.dtype)
    xb, gate = u[..., :LRU_WIDTH], u[..., LRU_WIDTH:]
    xc = causal_depthwise_conv(xb, conv_w, conv_b)
    r = jax.nn.sigmoid(block_diag_linear(xc, wa, ba).astype(jnp.float32))
    i = jax.nn.sigmoid(block_diag_linear(xc, wx, bx).astype(jnp.float32))
    log_a = -LRU_C * r * jax.nn.softplus(-a_param.astype(jnp.float32))
    a = jnp.exp(log_a)
    mult = jnp.sqrt(-jnp.expm1(2.0 * log_a))
    bterm = mult * (i * xc.astype(jnp.float32))

    def combine(lhs, rhs):
        a1, b1 = lhs
        a2, b2 = rhs
        return a1 * a2, a2 * b1 + b2

    _, hs = lax.associative_scan(combine, (a, bterm), axis=1)
    y = hs.astype(h.dtype) * jax.nn.silu(gate)
    return y @ w_out.astype(h.dtype)

def fox_mixer(h, w_in, b_f, w_out):
    bsz, s, _ = h.shape
    u = h @ w_in.astype(h.dtype)
    q = u[..., 0 * FOX_WIDTH:1 * FOX_WIDTH].reshape(bsz, s, FOX_HEADS, FOX_HEAD_DIM)
    k = u[..., 1 * FOX_WIDTH:2 * FOX_WIDTH].reshape(bsz, s, FOX_HEADS, FOX_HEAD_DIM)
    v = u[..., 2 * FOX_WIDTH:3 * FOX_WIDTH].reshape(bsz, s, FOX_HEADS, FOX_HEAD_DIM)
    gate = u[..., 3 * FOX_WIDTH:4 * FOX_WIDTH]
    f_logit = u[..., 4 * FOX_WIDTH:].astype(jnp.float32) + b_f.astype(jnp.float32)
    cum = jnp.cumsum(jax.nn.log_sigmoid(f_logit), axis=1)
    ck = jnp.transpose(cum, (0, 2, 1))
    scale = 1.0 / math.sqrt(FOX_HEAD_DIM)
    n_blocks = s // Q_BLOCK
    qb = jnp.transpose(q.reshape(bsz, n_blocks, Q_BLOCK, FOX_HEADS, FOX_HEAD_DIM), (1, 0, 2, 3, 4))
    cqb = jnp.transpose(cum.reshape(bsz, n_blocks, Q_BLOCK, FOX_HEADS), (1, 0, 3, 2))
    starts = jnp.arange(n_blocks, dtype=jnp.int32) * Q_BLOCK
    kpos = jnp.arange(s, dtype=jnp.int32)
    kf = k.astype(jnp.float32)
    vf = v.astype(jnp.float32)

    def one_block(args):
        q_blk, cq_blk, start = args
        qpos = start + jnp.arange(Q_BLOCK, dtype=jnp.int32)
        logits = jnp.einsum("bqhd,bkhd->bhqk", q_blk.astype(jnp.float32), kf) * scale
        logits = logits + (cq_blk[..., :, None] - ck[:, :, None, :])
        mask = kpos[None, :] <= qpos[:, None]
        logits = jnp.where(mask[None, None], logits, NEG_INF)
        p = jax.nn.softmax(logits, axis=-1)
        return jnp.einsum("bhqk,bkhd->bqhd", p, vf)

    o = lax.map(one_block, (qb, cqb, starts))
    o = jnp.transpose(o, (1, 0, 2, 3, 4)).reshape(bsz, s, FOX_WIDTH).astype(h.dtype)
    y = o * jax.nn.silu(gate)
    return y @ w_out.astype(h.dtype)

def second_inputs(seed: int = 0) -> dict:
    key = jax.random.key(seed)
    ks = jax.random.split(key, 16)
    f32 = jnp.float32
    nl, nf = N_LRU_LAYERS, N_FOX_LAYERS
    x = jax.random.normal(ks[0], (BATCH, SEQ, D_MODEL), f32)
    norm_g = 1.0 + 0.05 * jax.random.normal(ks[1], (DEPTH, D_MODEL), f32)
    final_g = 1.0 + 0.05 * jax.random.normal(ks[2], (D_MODEL,), f32)
    lru_w_in = jax.random.normal(ks[3], (nl, D_MODEL, 2 * LRU_WIDTH), f32) * D_MODEL ** -0.5
    lru_conv_w = jax.random.normal(ks[4], (nl, CONV_WIDTH_2, LRU_WIDTH), f32) * CONV_WIDTH_2 ** -0.5
    lru_conv_b = 0.02 * jax.random.normal(ks[5], (nl, LRU_WIDTH), f32)
    lru_wa = jax.random.normal(ks[6], (nl, LRU_BLOCKS, LRU_BLOCK_W, LRU_BLOCK_W), f32) * LRU_BLOCK_W ** -0.5
    lru_ba = 0.02 * jax.random.normal(ks[7], (nl, LRU_WIDTH), f32)
    lru_wx = jax.random.normal(ks[8], (nl, LRU_BLOCKS, LRU_BLOCK_W, LRU_BLOCK_W), f32) * LRU_BLOCK_W ** -0.5
    lru_bx = 0.02 * jax.random.normal(ks[9], (nl, LRU_WIDTH), f32)
    a_c = jax.random.uniform(ks[10], (nl, LRU_WIDTH), f32, minval=0.9, maxval=0.999)
    a0 = a_c ** (1.0 / LRU_C)
    lru_a_param = jnp.log(a0) - jnp.log1p(-a0)
    lru_w_out = jax.random.normal(ks[11], (nl, LRU_WIDTH, D_MODEL), f32) * LRU_WIDTH ** -0.5
    fox_w_in = jax.random.normal(ks[12], (nf, D_MODEL, 4 * FOX_WIDTH + FOX_HEADS), f32) * D_MODEL ** -0.5
    fox_b_f = 3.0 + 0.5 * jax.random.normal(ks[13], (nf, FOX_HEADS), f32)
    fox_w_out = jax.random.normal(ks[14], (nf, FOX_WIDTH, D_MODEL), f32) * FOX_WIDTH ** -0.5
    return {"x": x, "norm_g": norm_g, "final_g": final_g,
            "lru_w_in": lru_w_in, "lru_conv_w": lru_conv_w, "lru_conv_b": lru_conv_b,
            "lru_wa": lru_wa, "lru_ba": lru_ba, "lru_wx": lru_wx, "lru_bx": lru_bx,
            "lru_a_param": lru_a_param, "lru_w_out": lru_w_out,
            "fox_w_in": fox_w_in, "fox_b_f": fox_b_f, "fox_w_out": fox_w_out}

def second_block(x, norm_g, final_g, lru_w_in, lru_conv_w, lru_conv_b, lru_wa, lru_ba,
              lru_wx, lru_bx, lru_a_param, lru_w_out, fox_w_in, fox_b_f, fox_w_out):
    for i in range(DEPTH):
        h = rms_norm_2(x, norm_g[i])
        j = i // N_MIXERS
        if i % N_MIXERS == 0:
            x = x + lru_mixer(h, lru_w_in[j], lru_conv_w[j], lru_conv_b[j], lru_wa[j], lru_ba[j],
                              lru_wx[j], lru_bx[j], lru_a_param[j], lru_w_out[j])
        else:
            x = x + fox_mixer(h, fox_w_in[j], fox_b_f[j], fox_w_out[j])
    return rms_norm_2(x, final_g)


def setup_inputs(seed=0):
    out = dict(first_inputs(seed))
    for name, value in second_inputs(seed + 1).items():
        if name != "x":
            out[name + "_2"] = value
    return out


def reference(
    x, c, positions, ada_w, ada_b, norm_g, final_g, even_w_in, even_w_out, conv_w, conv_vec,
    rwkv_mu_rkv, rwkv_mu_lora, rwkv_vec, rwkv_w_up, rwkv_a_up, rwkv_r_k, odd_w_in, odd_w_out,
    norm_g_2, final_g_2, lru_w_in_2, lru_conv_w_2, lru_conv_b_2, lru_wa_2, lru_ba_2, lru_wx_2,
    lru_bx_2, lru_a_param_2, lru_w_out_2, fox_w_in_2, fox_b_f_2, fox_w_out_2,
):
    x = first_block(
        x, c, positions, ada_w, ada_b, norm_g, final_g, even_w_in, even_w_out, conv_w, conv_vec,
        rwkv_mu_rkv, rwkv_mu_lora, rwkv_vec, rwkv_w_up, rwkv_a_up, rwkv_r_k, odd_w_in,
        odd_w_out,
    )
    return second_block(
        x, norm_g_2, final_g_2, lru_w_in_2, lru_conv_w_2, lru_conv_b_2, lru_wa_2, lru_ba_2,
        lru_wx_2, lru_bx_2, lru_a_param_2, lru_w_out_2, fox_w_in_2, fox_b_f_2, fox_w_out_2,
    )


_drawn_inputs = setup_inputs


def setup_inputs(seed=0):
    import zlib

    import numpy as np

    out = dict(_drawn_inputs(seed))
    spreads = {}
    factors = {'rwkv_mu_lora': 3.111, 'rwkv_w_up': 4.76, 'lru_ba_2': 35.212, 'lru_bx_2': 8.0}
    for name, (base, spread) in spreads.items():
        noise = np.random.default_rng([zlib.crc32(name.encode()), seed]).standard_normal(out[name].shape)
        drawn = base * np.exp(spread * noise) if base else spread * noise
        out[name] = __import__('jax').numpy.asarray(drawn.astype(out[name].dtype))
    for name, factor in factors.items():
        out[name] = (out[name] * factor).astype(out[name].dtype)
    return out
```

```python
from contextlib import ExitStack

import numpy as np

from concourse import mybir

ALU = mybir.AluOpType
ACT = mybir.ActivationFunctionType
F32 = mybir.dt.float32
F32R = mybir.dt.float32r
I32 = mybir.dt.int32

P = 128
T = 512
D = 1024
DT = D // P
TT = T // P
TAPS = 31
RH = 64
LORA = 64
CH = P
NCH = T // CH
DECAY = float(np.exp(-0.5))
AH = 16
IH = 8
TOPK = min(256, T // 4)
LRU = 1536
LT = LRU // P
LTAPS = 4
LRU_C = 8.0
FH = 16
NEG = -1e30
TAKEN = -3e38
ROUND = 1.5 * 2.0 ** 23
NRAW, NSPLIT = 4, 2
RWKV_AHEAD = True
TWO_PI = (6.28125, 0.0019350051879882812, 3.019916050561733e-07)


def vector_columns():
    names = [("c", DT), ("ada_b0", 3 * DT), ("ada_b1", 3 * DT), ("norm_g0", DT), ("norm_g1", DT),
             ("final_g", DT), ("conv_w", DT * TAPS), ("conv_vec", 3 * DT), ("mu_rkv", 3 * DT),
             ("mu_lora", 1), ("rwkv_vec", 6 * DT), ("r_k", DT), ("inv128", 1), ("inv64", 1),
             ("norm2_g0", DT), ("norm2_g1", DT), ("final2_g", DT), ("lru_conv_w", LT * LTAPS),
             ("lru_conv_b", LT), ("lru_ba", LT), ("lru_bx", LT), ("lru_a", LT), ("fox_b", 1)]
    at, out = 0, {}
    for name, n in names:
        out[name] = (at, n)
        at += n
    return out, at


class Lane:

    def __init__(self, sem, chained=True):
        self.sem, self.chained, self.count, self.queue, self.waited = sem, chained, 0, [], {}

    def wait(self, *marks):
        for m in marks:
            if isinstance(m, list):
                self.wait(*m)
            elif m is not None and self.waited.get(m[0].name, 0) < m[1]:
                self.waited[m[0].name] = m[1]
                self.queue.append(lambda e, m=m: e.wait_ge(m[0], m[1]))

    def do(self, issue, *marks, signal=True):
        if self.chained and self.count:
            self.wait((self.sem, self.count))
        self.wait(*marks)
        if not signal:
            self.queue.append(issue)
            return None
        self.count += 1
        self.queue.append(lambda e: issue(e).then_inc(self.sem, 1))
        return (self.sem, self.count)

    def mark(self):
        return (self.sem, self.count) if self.count else None


class Slot:

    def __init__(self, buf, free=()):
        self.buf, self.free, self.wait = buf, list(free), None

    def hold(self):
        assert self.free is not None
        self.wait, self.free = self.free, None
        return self


class Ring:

    def __init__(self, slots):
        self.slots, self.at = slots, 0

    def take(self):
        for _ in self.slots:
            s = self.slots[self.at % len(self.slots)]
            self.at += 1
            if s.free is not None:
                return s.hold()
        raise AssertionError("every buffer of the ring is held")


def together(*stages):
    stages = list(stages)
    while stages:
        for g in list(stages):
            try:
                next(g)
            except StopIteration:
                stages.remove(g)
            yield


class Core:

    def __init__(self, nc, t, ctx, debug):
        self.nc, self.t, self.ctx, self.debug, self.names = nc, t, ctx, debug or (), 0
        self.PE = Lane(self.sem("pe_done"), chained=False)
        self.DVE = Lane(self.sem("dve_done"))
        self.ACTE = Lane(self.sem("act_done"))
        self.POOL = Lane(self.sem("pool_done"))
        self.SP = Lane(None, chained=False)
        self.dma_total, self.stores, self.mod_made = {}, [], {}

        banks = [ctx.enter_context(nc.psum_tensor(f"bank{i}", [P, T], F32)) for i in range(8)]
        self.acc = Ring([Slot(b) for b in banks[0:2]])
        self.work = Ring([Slot(b) for b in banks[2:7]])
        self.stat = Slot(banks[7])

        self.cols, n_cols = vector_columns()
        self.vecs = self.sb("vecs", [P, n_cols])
        self.ident = self.sb("ident", [P, P])
        self.ones = self.sb("ones", [P, P])
        self.head_ones = self.sb("head_ones", [P, P])
        self.causal = self.sb("causal", [P, P])
        self.few = self.sb("few", [P, 5])
        self.rms_eps, self.ln_eps, self.gn_eps, self.sign128, self.sign64 = (
            self.few[:, i:i + 1] for i in range(5))
        self.mods = [self.sb(f"mod{l}", [P, 3 * DT]) for l in range(2)]
        self.gains = [self.sb(f"gain{l}", [P, DT]) for l in range(2)]
        self.silu_c = self.sb("silu_c", [P, DT])
        self.h_hi = self.sb("h_hi", [P, DT, T], F32R)
        self.h_lo = self.sb("h_lo", [P, DT, T], F32R)
        self.H = [(self.h_hi[:, k, :], self.h_lo[:, k, :]) for k in range(DT)]
        self.h_marks = [None] * DT
        self.h_free = []

        self.x = self.sb("x", [P, DT, T])

        self.raw = [Slot(self.sb(f"raw{i}", [P, DT * P])) for i in range(NRAW)]
        self.raw_sems = [self.sem(f"raw{i}_in") for i in range(NRAW)]
        self.split = [Slot((self.sb(f"w_hi{i}", [P, DT * P], F32R), self.sb(f"w_lo{i}", [P, DT * P], F32R)))
                      for i in range(NSPLIT)]
        self.plan, self.loaded, self.taken, self.splits, self.ready = weight_plan(t), 0, 0, 0, {}
        self.constants()

    def sem(self, name):
        return self.ctx.enter_context(self.nc.semaphore(name))

    def sb(self, name, shape, dt=F32, scope=None):
        self.names += 1
        return (scope or self.ctx).enter_context(self.nc.sbuf_tensor(f"{name}_{self.names}", shape, dt))

    def ring(self, name, n, shape, scope, free):
        return Ring([Slot(self.sb(f"{name}{i}", shape, scope=scope), free) for i in range(n)])

    def dma(self, out, in_, semaphore, *marks):
        self.SP.wait(*marks)
        self.SP.queue.append(lambda e: e.dma_start(out, in_).then_inc(semaphore, 16))
        self.dma_total[semaphore.name] = self.dma_total.get(semaphore.name, 0) + 16
        return (semaphore, self.dma_total[semaphore.name])

    def everyone(self):
        return [x.mark() for x in (self.PE, self.DVE, self.ACTE, self.POOL)]

    def vec(self, name, i=0, n=1):
        at, count = self.cols[name]
        assert i + n <= count
        return self.vecs[:, at + i:at + i + n]

    def dump(self, name, ap):
        if name in self.debug:
            self.stores.append(self.dma(self.t["dbg_" + name], ap, self.sem(f"dump_{name}"), self.everyone()))
            for lane in (self.PE, self.DVE, self.ACTE, self.POOL):
                lane.wait(self.stores[-1])

    def act(self, out, in_, func, *marks, **kw):
        return self.ACTE.do(lambda e: e.activation(out, in_, func, **kw), *marks)

    def tt(self, out, a, b, op, *marks):
        return self.DVE.do(lambda e: e.tensor_tensor(out, a, b, op), *marks)

    def ts(self, out, a, s1, op0, s2, op1, *marks):
        if op1 is None:
            return self.DVE.do(lambda e: e.tensor_scalar(out, a, s1, None, op0), *marks)
        return self.DVE.do(lambda e: e.tensor_scalar(out, a, s1, s2, op0, op1), *marks)

    def stt(self, out, a, s, b, op0, op1, *marks):
        return self.DVE.do(lambda e: e.scalar_tensor_tensor(out, a, s, b, op0, op1), *marks)

    def copy(self, out, a, *marks):
        return self.DVE.do(lambda e: e.tensor_copy(out, a), *marks)

    def recip(self, out, a, *marks):
        return self.DVE.do(lambda e: e.reciprocal(out, a), *marks)

    def scan(self, out, a, b, *marks):
        return self.DVE.do(lambda e: e.tensor_tensor_scan(out, a, b, 0.0, ALU.mult, ALU.add), *marks)

    def ptt(self, out, a, b, op, *marks):
        return self.POOL.do(lambda e: e.tensor_tensor(out, a, b, op), *marks)

    def fill(self, ap, value, *marks):
        return self.POOL.do(lambda e: e.memset(ap, value), *marks)

    def select(self, ap, pattern, base, cm, op, value, *marks):
        return self.POOL.do(lambda e: e.affine_select(out=ap, in_=ap, pattern=pattern, compare_op=op, fill=value,
                                                      base=base, channel_multiplier=cm), *marks)

    def mm(self, out, lhsT, rhs, start, stop, *marks, signal=False):
        return self.PE.do(lambda e: e.matmul(out, lhsT, rhs, start=start, stop=stop, skip_group_check=True),
                          *marks, signal=signal)

    def tr(self, out, in_, *marks, signal=False):
        k = in_.shape[0]
        return self.PE.do(lambda e: e.transpose(out, in_, self.ident[0:k, 0:k]), self.consts_made, *marks,
                          signal=signal)

    def load_next(self):
        n = self.loaded
        _, src, kt, width, split = self.plan[n]
        self.loaded += 1
        size = kt * width
        raw = self.raw[n % NRAW].hold()
        landed = self.dma(raw.buf[:, 0:size], src, self.raw_sems[n % NRAW], raw.wait)
        if not split:
            self.ready[n] = (raw, raw.buf, None, landed)
            return
        s = self.split[self.splits % NSPLIT].hold()
        self.splits += 1
        hi, lo = s.buf
        rounded = self.act(hi[:, 0:size], raw.buf[:, 0:size], ACT.Copy, landed, s.wait)
        rest = self.ptt(lo[:, 0:size], raw.buf[:, 0:size], hi[:, 0:size].bitcast(F32), ALU.subtract,
                        landed, rounded, s.wait)
        raw.free = [rounded, rest]
        self.ready[n] = (s, hi, lo, [rounded, rest])

    def weights(self, key):
        n = self.taken
        assert self.plan[n][0] == key, (self.plan[n][0], key)
        self.taken += 1
        if n not in self.ready:
            self.load_next()
        return self.ready.pop(n) + self.plan[n][2:4]

    def look_ahead(self):
        if self.loaded < len(self.plan) and self.loaded < self.taken + NSPLIT - 1:
            self.load_next()

    def project(self, key, bank, x=None, x_marks=None, start=True, stop=True):
        x, x_marks = x or self.H, x_marks or self.h_marks
        slot, hi, lo, landed, kt, width = self.weights(key)
        out = bank.buf[0:width, :]
        for k in range(kt):
            w = slice(k * width, (k + 1) * width)
            last = k == kt - 1
            self.mm(out, hi[:, w], x[k][0], start and k == 0, False, landed, bank.wait, x_marks[k])
            self.mm(out, hi[:, w], x[k][1], False, False)
            m = self.mm(out, lo[:, w], x[k][0], False, stop and last, signal=last)
            if k == 0:
                self.look_ahead()
            elif k % 2 and not last:
                yield
        slot.free = [m]
        bank.made = m

    def project_tokens(self, key, bank):
        slot, hi, lo, landed, kt, width = self.weights(key)
        for tt in range(TT):
            out = bank.buf[:, tt * width:(tt + 1) * width]
            at = slice(tt * P, (tt + 1) * P)
            for k in range(kt):
                w = slice(k * width, (k + 1) * width)
                self.mm(out, self.H[k][0][:, at], hi[:, w], k == 0, False, landed, bank.wait, self.h_marks[k])
                self.mm(out, self.H[k][1][:, at], hi[:, w], False, False)
                m = self.mm(out, self.H[k][0][:, at], lo[:, w], False, k == kt - 1, signal=k == kt - 1)
            if tt == 0:
                self.look_ahead()
            yield
        slot.free = [m]
        bank.made = m

    def constants(self):
        self.vecs_in = self.dma(self.vecs[:, :], self.t["vecs"], self.sem("vecs_in"))
        self.fill(self.ident[:, :], 0.0)
        self.select(self.ident[:, :], [[-1, P]], 0, 1, ALU.not_equal, 1.0)
        self.fill(self.ones[:, :], 1.0)
        self.fill(self.head_ones[:, :], 0.0)
        for h in range(2):
            self.fill(self.head_ones[h * RH:(h + 1) * RH, h * RH:(h + 1) * RH], 1.0)
        self.fill(self.causal[:, :], 0.0)
        self.select(self.causal[:, :], [[-1, P]], 0, 1, ALU.is_ge, NEG)
        for ap, value in ((self.rms_eps, 1e-6), (self.ln_eps, 1e-5), (self.gn_eps, 64e-5)):
            self.fill(ap, value)
        for p0, s128, s64 in ((0, -1.0, -1.0), (32, -1.0, 1.0), (64, 1.0, -1.0), (96, 1.0, 1.0)):
            self.fill(self.few[p0:p0 + 32, 3:4], s128)
            self.fill(self.few[p0:p0 + 32, 4:5], s64)
        self.consts_made = self.POOL.mark()
        self.silu_c_made = self.act(self.silu_c[:, :], self.vec("c", 0, DT), ACT.Silu, self.vecs_in)

    def modulation(self, l, parts):
        for part in parts:
            bank = self.work.take()
            for i in range(DT):
                slot, w, _, landed, kt, width = self.weights(("ada", l, part * DT + i))
                for k in range(kt):
                    m = self.mm(bank.buf[:, i:i + 1], w[:, k * width:(k + 1) * width], self.silu_c[:, k:k + 1],
                                k == 0, k == kt - 1, landed, bank.wait, self.silu_c_made, signal=k == kt - 1)
                slot.free = [m]
                self.look_ahead()
            at = slice(part * DT, (part + 1) * DT)
            made = self.tt(self.mods[l][:, at], bank.buf[:, 0:DT], self.vec(f"ada_b{l}", part * DT, DT), ALU.add,
                           m, self.vecs_in)
            bank.free = [made]
            if part == 1:
                made = self.stt(self.gains[l][:, :], self.mods[l][:, at], 1.0, self.vec(f"norm_g{l}", 0, DT),
                                ALU.add, ALU.mult, made)
            self.mod_made[l, part] = made
            yield

    def square_sum(self, x, i, x_mark, sq):
        s = sq.take()
        a = self.act(s.buf[:, :], x, ACT.Square, x_mark, s.wait)
        m = self.mm(self.stat.buf[:, :], self.ones[:, :], s.buf[:, :], i == 0, i == DT - 1,
                    a, self.consts_made, self.stat.free if i == 0 else None, signal=True)
        s.free = [m]
        return m

    def inverse_rms(self, rms, summed, free):
        a = self.act(rms, self.stat.buf[:, :], ACT.Sqrt, summed, free, self.consts_made,
                     bias=self.rms_eps, scale=1.0 / D)
        self.stat.free = [a]
        return self.recip(rms, rms, a)

    def norm_into_h(self, x, x_marks, summed, gain, shift, *marks):
        with ExitStack() as scope:
            before = self.everyone()
            rms = self.sb("rms", [P, T], scope=scope)
            tmp = self.ring("normed", 3, [P, T], scope, before)
            inverse = self.inverse_rms(rms[:, :], summed, before)
            for k in range(DT):
                s = tmp.take()
                n = s.buf[:, :]
                v = self.tt(n, x[:, k, :], rms[:, :], ALU.mult, x_marks[k], inverse, s.wait)
                if shift is None:
                    v = self.ts(n, n, gain(k), ALU.mult, None, None, v, self.vecs_in)
                else:
                    v = self.ts(n, n, gain(k), ALU.mult, shift(k), ALU.add, v, *marks)
                a = self.act(self.h_hi[:, k, :], n, ACT.Copy, v, self.h_free)
                v = self.tt(self.h_lo[:, k, :], n, self.h_hi[:, k, :].bitcast(F32), ALU.subtract, a, self.h_free)
                s.free = [v]
                self.h_marks[k] = [a, v]
            self.h_free = []

    def out_project(self, name, src, src_marks, x, x_marks, gate=None, gate_mark=None):
        with ExitStack() as scope:
            before = self.everyone()
            n = len(src)
            half = n // 2
            own_hi = self.sb("own_hi", [P, n - half, T], F32R, scope)
            own_lo = self.sb("own_lo", [P, n - half, T], F32R, scope)
            pairs = self.H[:half] + [(own_hi[:, k, :], own_lo[:, k, :]) for k in range(n - half)]
            sq = self.ring("sq", 2, [P, T], scope, before)
            marks = []
            for k, (s, (hi, lo)) in enumerate(zip(src, pairs)):
                free = self.h_free if k < half else before
                a = self.act(hi, s, ACT.Copy, src_marks[k], free)
                marks.append([a, self.tt(lo, s, hi.bitcast(F32), ALU.subtract, a, src_marks[k], free)])
            if callable(x_marks):
                x_marks = x_marks(marks)
            new = []
            for cb in range(DT):
                bank = self.acc.take()
                for part, (a, b) in enumerate(((0, half), (half, n))):
                    for _ in self.project((name, cb, part), bank, pairs[a:b], marks[a:b], a == 0, b == n):
                        pass
                xs = x[:, cb, :]
                if gate is None:
                    v = self.tt(xs, bank.buf[:, :], xs, ALU.add, bank.made, x_marks[cb])
                else:
                    v = self.stt(xs, bank.buf[:, :], gate(cb), xs, ALU.mult, ALU.add, bank.made, x_marks[cb],
                                 gate_mark)
                bank.free = [v]
                new.append(v)
                if cb:
                    self.square_sum(x[:, cb - 1, :], cb - 1, new[cb - 1], sq)
            summed = self.square_sum(x[:, DT - 1, :], DT - 1, new[DT - 1], sq)
            self.h_free = [self.PE.mark()]
            return new, summed


def run(stage):
    for _ in stage:
        pass


def even_layer(c):
    with ExitStack() as layer:
        before = c.everyone()
        ya = c.sb("ya", [P, DT, T], scope=layer)
        ya_made = conv_mixer(c, ya, before)
        c.dump("ya", ya[:, :, :])
        yb = c.x
        yb_made = rwkv_mixer(c, yb)
        c.dump("yb", yb[:, :, :])
        run(c.modulation(0, (2,)))

        def load_x(splits):
            return [c.dma(c.x[:, k, :], c.t["x_t"][k * P:(k + 1) * P, :], c.sem(f"x_back{k}"), splits[DT + k])
                    for k in range(DT)]

        src = [ya[:, k, :] for k in range(DT)] + [yb[:, k, :] for k in range(DT)]
        return c.out_project("even_out", src, ya_made + yb_made, c.x, load_x,
                             lambda k: c.mods[0][:, 2 * DT + k:2 * DT + k + 1], c.mod_made[0, 2])


def conv_mixer(c, ya, before):
    with ExitStack() as scope:
        gate = c.sb("conv_gate", [P, DT, T], scope=scope)
        glu = c.ring("glu", 2, [P, T], scope, before)
        padded = c.ring("padded", 2, [P, TAPS - 1 + T], scope, before)
        for s in padded.slots:
            s.free = [c.fill(s.buf[:, 0:TAPS - 1], 0.0, before)]
        gate_made, made = [], []
        for k in range(DT):
            val, sig, g = c.acc.take(), None, None
            run(c.project(("even", k), val))
            b = c.acc.take()
            run(c.project(("even", DT + k), b))
            s = glu.take()
            a = c.act(s.buf[:, :], b.buf[:, :], ACT.Sigmoid, b.made, s.wait)
            b.free = [a]
            u = padded.take()
            v = c.tt(u.buf[:, TAPS - 1:], val.buf[:, :], s.buf[:, :], ALU.mult, val.made, a, u.wait)
            val.free, s.free = [v], [v]
            y = ya[:, k, :]
            w = lambda j: c.vec("conv_w", k * TAPS + j)
            v = c.ts(y, u.buf[:, 0:T], w(0), ALU.mult, c.vec("conv_vec", k), ALU.add, v, before, c.vecs_in)
            for j in range(1, TAPS):
                v = c.stt(y, u.buf[:, j:j + T], w(j), y, ALU.mult, ALU.add)
            u.free = [v]
            made.append(v)
            b = c.acc.take()
            run(c.project(("even", 2 * DT + k), b))
            a = c.act(gate[:, k, :], b.buf[:, :], ACT.Silu, b.made, before)
            b.free = [a]
            gate_made.append(a)
        mean, var = c.work.take(), c.work.take()
        for k in range(DT):
            m = c.mm(mean.buf[:, :], c.ones[:, :], ya[:, k, :], k == 0, k == DT - 1, made[k], mean.wait,
                     c.consts_made, signal=True)
        for k in range(DT):
            s = glu.take()
            v = c.stt(ya[:, k, :], mean.buf[:, :], -1.0 / D, ya[:, k, :], ALU.mult, ALU.add, m)
            a = c.act(s.buf[:, :], ya[:, k, :], ACT.Square, v, s.wait)
            n = c.mm(var.buf[:, :], c.ones[:, :], s.buf[:, :], k == 0, k == DT - 1, a, var.wait, signal=True)
            s.free = [n]
        mean.free = [v]
        s = glu.take()
        inv = s.buf[:, :]
        a = c.act(inv, var.buf[:, :], ACT.Sqrt, n, s.wait, bias=c.ln_eps, scale=1.0 / D)
        var.free = [a]
        r = c.recip(inv, inv, a)
        out = []
        for k in range(DT):
            y = ya[:, k, :]
            v = c.tt(y, y, inv, ALU.mult, r)
            a = c.act(y, y, ACT.Silu, v, scale=c.vec("conv_vec", DT + k), bias=c.vec("conv_vec", 2 * DT + k))
            out.append(c.tt(y, y, gate[:, k, :], ALU.mult, a, gate_made[k]))
        return out


def rwkv_mixer(c, yb):
    with ExitStack() as scope:
        before = c.everyone()
        sb = lambda name, shape: c.sb(name, shape, scope=scope)
        chunk_start = sb("chunk_start", [P, T])
        mask_t = sb("mask_t", [P, 4, P])
        mask_n = sb("mask_n", [P, P])
        block16 = sb("block16", [P, P])
        merges = (16, 32, 64)
        below = {s: sb(f"below{s}", [P, P]) for s in merges}
        c.fill(chunk_start[:, :], 1.0, before)
        for j in range(0, T, CH):
            c.fill(chunk_start[:, j:j + 1], 0.0)
        c.fill(mask_t[:, :, :], 1.0)
        for j in range(4):
            c.select(mask_t[:, j, :], [[1, P]], -1 + j % 2, -1, ALU.is_ge, 0.0)
        c.fill(mask_n[:, :], 1.0)
        c.select(mask_n[:, :], [[-1, P]], -1, 1, ALU.is_ge, 0.0)
        c.fill(block16[:, :], 1.0)
        v16 = block16[:, :].rearrange("p (b i) -> p b i", i=16)
        c.select(v16, [[-16, P // 16], [0, 16]], 0, 1, ALU.is_ge, 0.0)
        c.select(v16, [[16, P // 16], [0, 16]], 15, -1, ALU.is_ge, 0.0)
        for s in merges:
            v = below[s][:, :].rearrange("p (b i) -> p b i", i=s)
            v4 = below[s][:, :].rearrange("p (b h i) -> p b h i", h=2, i=s)
            c.fill(below[s][:, :], 1.0)
            c.select(v4, [[-2 * s, P // (2 * s)], [0, 2], [0, s]], -s, 1, ALU.is_ge, 0.0)
            c.select(v4, [[2 * s, P // (2 * s)], [0, 2], [0, s]], 2 * s - 1, -1, ALU.is_ge, 0.0)
            for b in range(1, P // s, 2):
                c.fill(v[:, b, :], 0.0)
        masks = c.POOL.mark()

        keep = sb("one_minus_k_a", [P, DT])
        c.ts(keep[:, :], c.vec("rwkv_vec", 3 * DT, DT), -1.0, ALU.mult, 1.0, ALU.add, before, c.vecs_in)
        up = sb("lora_up", [P, D])
        up_in = c.dma(up[:, :], c.t["lora_up"], c.sem("lora_up_in"), before)
        shifted = c.ring("shifted", 3, [P, 1 + T], scope, before)
        for s in shifted.slots:
            s.free = [c.fill(s.buf[:, 0:1], 0.0, before)]
        tmp = c.ring("tmp", 4, [P, T], scope, before)

        class Pair:
            def __init__(self, i):
                self.AR = sb(f"AR{i}", [P, NCH, 2, CH])
                self.K, self.B, self.V, self.bonus, self.gate = (
                    sb(f"{n}{i}", [P, NCH, CH]) for n in ("K", "B", "V", "bonus", "gate"))
                self.carry = sb(f"carry{i}", [P, NCH])
                self.free = before
        pairs = [Pair(0), Pair(1)] if RWKV_AHEAD else [Pair(0)]
        flat = lambda b: b[:, :, :].rearrange("p c t -> p (c t)")
        mids = sb("mids", [P, NCH])
        lora = sb("lora", [P, T])
        MM = [sb(f"MM{h}", [P, NCH, 4, CH]) for h in range(2)]
        NN = [sb(f"N{h}", [P, NCH, CH]) for h in range(2)]
        PT = [sb(f"PT{h}", [P, NCH, CH]) for h in range(2)]
        W = [[sb(f"W{h}{i}", [P, NCH, CH]) for i in range(4)] for h in range(2)]
        S = sb("S", [P, NCH, P])
        S_zero = c.fill(S[:, :, :], 0.0, before)

        def lerp(key, mu):
            bank = c.acc.take()
            yield from c.project(key, bank)
            z, d = shifted.take(), tmp.take()
            a = c.act(z.buf[:, 1:], bank.buf[:, :], ACT.Copy, bank.made, z.wait)
            bank.free = [a]
            p = c.ptt(d.buf[:, :], z.buf[:, 0:T], z.buf[:, 1:], ALU.subtract, a, d.wait)
            v = c.stt(z.buf[:, 1:], d.buf[:, :], mu, z.buf[:, 1:], ALU.mult, ALU.add, p)
            d.free = [v]
            lerp.out = z, v

        run(lerp(("even", 6 * DT), c.vec("mu_lora")))
        z, v = lerp.out
        a = c.act(lora[0:LORA, :], z.buf[0:LORA, 1:], ACT.Tanh, v, before)
        lora_made = c.act(lora[LORA:P, :], z.buf[LORA:P, 1:], ACT.Copy, v)
        z.free = [lora_made]

        def head_sum(x, *marks):
            b = c.work.take()
            b.made = c.mm(b.buf[:, :], c.head_ones[:, :], x, True, True, b.wait, c.consts_made, *marks, signal=True)
            return b

        def prepare(p, pair):
            free = pair.free
            vv = lambda i: c.vec("rwkv_vec", i * DT + p)
            at = slice(p * P, (p + 1) * P)
            b = c.work.take()
            m = c.mm(b.buf[:, :], up[0:LORA, at], lora[0:LORA, :], True, True, b.wait, up_in, lora_made, signal=True)
            sg, cum, ex = tmp.take(), tmp.take(), tmp.take()
            a = c.act(sg.buf[:, :], b.buf[:, :], ACT.Sigmoid, m, sg.wait, bias=vv(0))
            b.free = [a]
            v = c.scan(cum.buf[:, :], chunk_start[:, :], sg.buf[:, :], a, masks, cum.wait)
            c3 = cum.buf[:, :].rearrange("p (c t) -> p c t", t=CH)
            mid = c3[:, :, CH // 2 - 1:CH // 2]
            a = c.act(mids[:, :], mid.rearrange("p c o -> p (c o)"), ACT.Exp, v, scale=-DECAY)
            e3 = ex.buf[:, :].rearrange("p (c t) -> p c t", t=CH)
            v = c.tt(e3, c3, mid.to_broadcast([P, NCH, CH]), ALU.subtract, v, ex.wait)
            up_to = c.act(pair.AR[:, :, 1, :], e3, ACT.Exp, v, free, scale=-DECAY)
            w = c.tt(pair.carry[:, 0:NCH - 1], pair.AR[:, 0:NCH - 1, 1, CH - 1], mids[:, 1:], ALU.mult, up_to, free)
            over = c.act(pair.K[:, :, :], e3, ACT.Exp, v, free, scale=DECAY)
            p1 = c.ptt(ex.buf[:, :], ex.buf[:, :], sg.buf[:, :], ALU.subtract, over, up_to)
            before_t = c.act(pair.AR[:, :, 0, :], e3, ACT.Exp, p1, scale=-DECAY)
            for s in (sg, cum, ex):
                s.free = [before_t, c.DVE.mark()]
            b = c.work.take()
            m = c.mm(b.buf[:, :], up[LORA:P, at], lora[LORA:P, :], True, True, b.wait, signal=True)
            rate = tmp.take()
            a = c.act(rate.buf[:, :], b.buf[:, :], ACT.Sigmoid, m, rate.wait, bias=vv(1))
            b.free = [a]
            rate_made = a
            yield
            yield from lerp(("even", 4 * DT + p), c.vec("mu_rkv", DT + p))
            k, k_made = lerp.out
            kz = k.buf[:, 1:]
            kk, sq = tmp.take(), tmp.take()
            v = c.ts(kk.buf[:, :], kz, vv(2), ALU.mult, None, None, k_made, kk.wait)
            a = c.act(sq.buf[:, :], kk.buf[:, :], ACT.Square, v, sq.wait)
            b = head_sum(sq.buf[:, :], a)
            a = c.act(sq.buf[:, :], b.buf[:, :], ACT.Sqrt, b.made)
            b.free = [a]
            v = c.ts(sq.buf[:, :], sq.buf[:, :], 1e-12, ALU.max, None, None, a)
            v = c.recip(sq.buf[:, :], sq.buf[:, :])
            v = c.tt(kk.buf[:, :], kk.buf[:, :], sq.buf[:, :], ALU.mult)
            yield
            r3 = lambda s: s.buf[:, :].rearrange("p (c t) -> p c t", t=CH)
            v = c.stt(pair.AR[:, :, 0, :], r3(kk), -1.0, pair.AR[:, :, 0, :], ALU.mult, ALU.mult, before_t)
            v = c.tt(kk.buf[:, :], kk.buf[:, :], rate.buf[:, :], ALU.mult, rate_made)
            v = c.tt(pair.B[:, :, :], r3(kk), pair.K[:, :, :], ALU.mult, over, free)
            v = c.ts(rate.buf[:, :], rate.buf[:, :], vv(3), ALU.mult, keep[:, p:p + 1], ALU.add)
            v = c.tt(kz, kz, rate.buf[:, :], ALU.mult)
            k2 = v
            v = c.tt(flat(pair.K), kz, flat(pair.K), ALU.mult)
            for s in (kk, sq, rate):
                s.free = [v]
            yield from lerp(("even", 3 * DT + p), c.vec("mu_rkv", p))
            r, r_made = lerp.out
            rz = r.buf[:, 1:]
            r33 = rz.rearrange("p (c t) -> p c t", t=CH)
            v = c.tt(pair.AR[:, :, 1, :], r33, pair.AR[:, :, 1, :], ALU.mult, r_made, up_to)
            v = c.stt(rz, rz, c.vec("r_k", p), kz, ALU.mult, ALU.mult)
            k.free = [v]
            bonus = head_sum(rz, v)
            r.free = [bonus.made]
            yield from lerp(("even", 5 * DT + p), c.vec("mu_rkv", 2 * DT + p))
            z, v = lerp.out
            a = c.act(flat(pair.V), z.buf[:, 1:], ACT.Copy, v, free)
            v = c.tt(flat(pair.bonus), bonus.buf[:, :], z.buf[:, 1:], ALU.mult, bonus.made, free)
            z.free, bonus.free = [a, v], [v]
            b = c.acc.take()
            yield from c.project(("even", 6 * DT + 1 + p), b)
            a = c.act(flat(pair.gate), b.buf[:, :], ACT.Silu, b.made, free)
            b.free = [a]
            pair.made = [v, a]

        def four(lhsT, rhs, *marks):
            b = c.work.take()
            for j in range(NCH):
                m = c.mm(b.buf[:, j * CH:(j + 1) * CH], lhsT[:, j, :], rhs[:, j, :], True, True, b.wait, *marks,
                         signal=j == NCH - 1)
            b.made = m
            return b

        def three(b):
            return b.buf[:, :].rearrange("p (c t) -> p c t", t=CH)

        def every_chunk(mask):
            return mask[:, :].unsqueeze(1).to_broadcast([P, NCH, CH])

        def to_sbuf(dst, b, act):
            m = c.act(dst, three(b), ACT.Copy, b.made) if act else c.copy(dst, three(b), b.made)
            b.free = [m]
            return m

        def matrices(h, pair):
            hs = slice(h * RH, (h + 1) * RH)
            for j in range(NCH):
                b = c.work.take()
                ar = pair.AR[hs, j, :, :].rearrange("p a t -> p (a t)")
                c.mm(b.buf[:, 0:2 * CH], pair.K[hs, j, :], ar, True, True, b.wait, pair.made)
                m = c.mm(b.buf[:, 2 * CH:], pair.B[hs, j, :], ar, True, True, signal=True)
                v = c.tt(MM[h][:, j, :, :], b.buf[:, :].rearrange("p (a t) -> p a t", t=CH), mask_t[:, :, :],
                         ALU.mult, m, masks, before, solved)
                b.free = [v]
                yield
            b = c.work.take()
            for j in range(NCH):
                m = c.mm(b.buf[:, j * CH:(j + 1) * CH], pair.AR[hs, j, 0, :], pair.B[hs, j, :], True, True, b.wait,
                         signal=j == NCH - 1)
            v = c.tt(NN[h][:, :, :], three(b), every_chunk(mask_n), ALU.mult, m)
            b.free = [v]
            matrices.made[h] = v
            yield
        matrices.made = {}

        def add_to_inverse(h, b):
            v = c.tt(PT[h][:, :, :], three(b), PT[h][:, :, :], ALU.add, b.made)
            b.free = [v]
            return v

        def invert(h, pair):
            yield from matrices(h, pair)
            w = W[h]
            p1 = c.ptt(w[0][:, :, :], NN[h][:, :, :], every_chunk(block16), ALU.mult, matrices.made[h])
            p2 = c.tt(w[1][:, :, :], MM[h][:, :, 2, :], every_chunk(block16), ALU.mult)
            pt = c.tt(PT[h][:, :, :], w[1][:, :, :], every_chunk(c.ident), ALU.add, p2)
            b1, b2 = four(w[1], w[0], p1, p2), four(w[0], w[1], p1, p2)
            m1 = to_sbuf(w[2][:, :, :], b1, True)
            m2 = to_sbuf(w[3][:, :, :], b2, False)
            yield
            b1, b3, b2 = four(w[3], w[2], m1, m2), four(w[2], PT[h], m1, pt), four(w[2], w[3], m1, m2)
            m1 = to_sbuf(w[0][:, :, :], b1, True)
            pt = add_to_inverse(h, b3)
            m2 = to_sbuf(w[1][:, :, :], b2, False)
            yield
            b1, b2 = four(w[1], w[0], m1, m2), four(w[0], PT[h], m1, pt)
            m1 = to_sbuf(w[2][:, :, :], b1, True)
            pt = add_to_inverse(h, b2)
            yield
            pt = add_to_inverse(h, four(w[2], PT[h], m1, pt))
            yield
            for s in merges:
                b = c.work.take()
                for j in range(NCH):
                    m = c.tr(b.buf[:, j * CH:(j + 1) * CH], PT[h][:, j, :], pt, b.wait, signal=j == NCH - 1)
                b.made = m
                off = c.ptt(w[1][:, :, :], NN[h][:, :, :], every_chunk(below[s]), ALU.mult, c.PE.mark())
                p = to_sbuf(w[0][:, :, :], b, True)
                b = four(w[1], PT[h], off, pt)
                m = to_sbuf(w[2][:, :, :], b, False)
                yield
                pt = add_to_inverse(h, four(w[0], w[2], p, m))
                yield
            invert.made[h] = pt
        invert.made = {}

        def solve(p, pair):
            yield from together(invert(0, pair), invert(1, pair))
            inv = [invert.made[0], invert.made[1]]
            A_t, V_t, K_t, B_t = W[0]
            Z, U0, PA, U = W[1]
            turned = []
            for i, (dst, src) in enumerate(((A_t, lambda j: pair.AR[:, j, 0, :]), (V_t, lambda j: pair.V[:, j, :]),
                                            (K_t, lambda j: pair.K[:, j, :]), (B_t, lambda j: pair.B[:, j, :]))):
                b = c.work.take()
                for j in range(NCH):
                    m = c.tr(b.buf[:, j * CH:(j + 1) * CH], src(j), b.wait, inv, pair.made, signal=j == NCH - 1)
                b.made = m
                turned.append(to_sbuf(dst[:, :, :], b, i % 2 == 0))
                yield
            heads = [(h, slice(h * RH, (h + 1) * RH)) for h in range(2)]
            b = c.work.take()
            for j in range(NCH):
                for h, hs in heads:
                    m = c.mm(three(b)[:, j, hs], MM[h][:, j, 0, :], V_t[:, j, hs], True, True, b.wait, turned,
                             signal=j == NCH - 1 and h == 1)
            b.made = m
            z = to_sbuf(Z[:, :, :], b, True)
            b = c.work.take()
            for j in range(NCH):
                for h, hs in heads:
                    m = c.mm(three(b)[hs, j, :], A_t[:, j, hs], PT[h][:, j, :], True, True, b.wait,
                             signal=j == NCH - 1 and h == 1)
            b.made = m
            pa = to_sbuf(PA[:, :, :], b, False)
            yield
            b = c.work.take()
            for j in range(NCH):
                for h, hs in heads:
                    m = c.mm(three(b)[:, j, hs], PT[h][:, j, :], Z[:, j, hs], True, True, b.wait, z,
                             signal=j == NCH - 1 and h == 1)
            b.made = m
            u0 = to_sbuf(U0[:, :, :], b, True)
            yield
            y = c.work.take()
            u, s_made = u0, S_zero
            for j in range(NCH):
                Uj = U0 if j == 0 else U
                if j:
                    b = c.work.take()
                    m = c.mm(b.buf[:, 0:P], PA[:, j, :], S[:, j, :], True, True, b.wait, pa, s_made, signal=True)
                    u = c.tt(U[:, j, :], b.buf[:, 0:P], U0[:, j, :], ALU.add, m, u0)
                    b.free = [u]
                if j < NCH - 1:
                    b = c.work.take()
                    w = pair.carry[:, j:j + 1]
                    m = c.mm(b.buf[:, 0:P], K_t[:, j, :], V_t[:, j, :], True, False, b.wait)
                    m = c.mm(b.buf[:, 0:P], B_t[:, j, :], Uj[:, j, :], False, True, u, signal=True)
                    for h, hs in heads:
                        if j == 0:
                            v = c.ts(S[hs, 1, hs], b.buf[hs, hs], w[hs], ALU.mult, None, None, m, S_free[0])
                        else:
                            v = c.tt(S[hs, j + 1, hs], b.buf[hs, hs], S[hs, j, hs], ALU.add, m, S_free[0])
                            v = c.ts(S[hs, j + 1, hs], S[hs, j + 1, hs], w[hs], ALU.mult, None, None, v)
                    b.free, s_next = [v], v
                if j:
                    c.mm(three(y)[:, j, :], S[:, j, :], pair.AR[:, j, 1, :], True, False, y.wait)
                for h, hs in heads:
                    c.mm(three(y)[hs, j, :], V_t[:, j, hs], MM[h][:, j, 1, :], j == 0, False, y.wait)
                    m = c.mm(three(y)[hs, j, :], Uj[:, j, hs], MM[h][:, j, 3, :], False, True, u, signal=True)
                s_made = s_next
                yield
            S_free[0] = m
            solved[:] = [m]
            t1, t2 = post.take(), post.take()
            a = c.act(t1.buf[:, :], y.buf[:, :], ACT.Copy, m, t1.wait)
            y.free = [a]
            b = head_sum(t1.buf[:, :], a)
            v = c.stt(t1.buf[:, :], b.buf[:, :], -1.0 / RH, t1.buf[:, :], ALU.mult, ALU.add, b.made)
            b.free = [v]
            a = c.act(t2.buf[:, :], t1.buf[:, :], ACT.Square, v, t2.wait)
            b = head_sum(t2.buf[:, :], a)
            a = c.act(t2.buf[:, :], b.buf[:, :], ACT.Sqrt, b.made, bias=c.gn_eps, scale=1.0 / RH)
            b.free = [a]
            v = c.recip(t2.buf[:, :], t2.buf[:, :], a)
            v = c.tt(t1.buf[:, :], t1.buf[:, :], t2.buf[:, :], ALU.mult)
            v = c.ts(t1.buf[:, :], t1.buf[:, :], c.vec("rwkv_vec", 4 * DT + p), ALU.mult,
                     c.vec("rwkv_vec", 5 * DT + p), ALU.add)
            v = c.tt(t1.buf[:, :], t1.buf[:, :], flat(pair.bonus), ALU.add)
            v = c.tt(yb[:, p, :], t1.buf[:, :], flat(pair.gate), ALU.mult, before)
            t1.free, t2.free = [v], [v]
            pair.free = [m, v]
            made.append(v)

        post = c.ring("post", 2, [P, T], scope, before)
        made, solved, S_free = [], [], [S_zero]
        run(prepare(0, pairs[0]))
        for p in range(DT):
            if len(pairs) == 1:
                run(solve(p, pairs[0]))
                if p + 1 < DT:
                    run(prepare(p + 1, pairs[0]))
            else:
                stages = [solve(p, pairs[p % 2])]
                if p + 1 < DT:
                    stages.append(prepare(p + 1, pairs[(p + 1) % 2]))
                run(together(*stages))
        return made


def rope_tables(c, scope, name, inv, sign, positions, angle, turns, before):
    out = []
    c.ts(angle[:, :], positions[:, :], inv, ALU.mult, None, None, before, c.vecs_in)
    for i, quarter in enumerate((0.25, 0.0)):
        r = c.sb(f"{'sin' if i else 'cos'}_{name}", [P, T], scope=scope)
        c.ts(turns[:, :], angle[:, :], float(0.5 / np.pi), ALU.mult, quarter, ALU.add)
        c.ts(turns[:, :], turns[:, :], ROUND, ALU.add, ROUND, ALU.subtract)
        c.stt(r[:, :], turns[:, :], -TWO_PI[0], angle[:, :], ALU.mult, ALU.add)
        for part in TWO_PI[1:]:
            c.stt(r[:, :], turns[:, :], -part, r[:, :], ALU.mult, ALU.add)
        if not i:
            c.ts(r[:, :], r[:, :], float(np.pi / 2), ALU.add, None, None)
        v = c.ts(r[:, :], r[:, :], 3.1415925, ALU.min, -3.1415925, ALU.max)
        a = c.act(r[:, :], r[:, :], ACT.Sin, v)
        out.append(r)
    made = c.ts(r[:, :], r[:, :], sign, ALU.mult, None, None, a, c.consts_made)
    return out[0], out[1], made


def odd_layer(c, x_marks):
    with ExitStack() as layer:
        before = c.everyone()
        sb = lambda name, shape, dt=F32: c.sb(name, shape, dt, scope=layer)
        Q = sb("q", [P, AH, T])
        keys = sb("keys", [P, T])
        values = sb("values", [P, TT, P])
        bias = sb("bias", [P, TT, T])
        tmp = c.ring("attn_tmp", 5, [P, T], layer, before)
        probs = c.ring("probs", 3, [P, T], layer, before)
        PT = c.ring("probs_t", 2, [P, TT, T], layer, before)
        small = sb("small", [P, 3 * AH * TT])
        with ExitStack() as index:
            isb = lambda name, shape, dt=F32: c.sb(name, shape, dt, scope=index)
            score = isb("score", [P, TT, T])
            pos_i, chunk_i = isb("pos_i", [P, T], I32), isb("chunk_i", [P, T], I32)
            pos_q, chunk_q = isb("pos_q", [P, TT], I32), isb("chunk_q", [P, TT], I32)
            pos, chunk_k, chunk_qf = isb("pos", [P, T]), isb("chunk_k", [P, T]), isb("chunk_qf", [P, TT])
            loaded = [c.dma(pos_i[:, :], c.t["pos"].to_broadcast([P, T]), c.sem("pos_in"), before),
                      c.dma(pos_q[:, :], c.t["pos_q"], c.sem("pos_q_in"), before)]
            c.copy(pos[:, :], pos_i[:, :], before, loaded)
            for dst, src, out in ((chunk_i, pos_i, chunk_k), (chunk_q, pos_q, chunk_qf)):
                c.DVE.do(lambda e, d=dst, s=src: e.tensor_scalar(d[:, :], s[:, :], 6, None, ALU.arith_shift_right))
                c.copy(out[:, :], dst[:, :])
            angle, turns = isb("angle", [P, T]), isb("turns", [P, T])
            cos128, sin128, rope128 = rope_tables(c, index, "128", c.vec("inv128"), c.sign128, pos, angle, turns, before)
            cos64, sin64, rope64 = rope_tables(c, index, "64", c.vec("inv64"), c.sign64, pos, angle, turns, before)
            for t in range(TT):
                adm = c.ts(bias[:, t, :], chunk_k[:, :], chunk_qf[:, t:t + 1], ALU.is_gt, NEG, ALU.mult)

            def rotate(key, half, cos, sin, rope_made, out, *marks):
                b = c.acc.take()
                yield from c.project(key, b)
                swapped, plain = tmp.take(), tmp.take()
                for r in range(0, P, half):
                    o = r ^ half
                    a = c.act(swapped.buf[r:r + half, :], b.buf[o:o + half, :], ACT.Copy, b.made, swapped.wait)
                p = c.ptt(swapped.buf[:, :], swapped.buf[:, :], sin[:, :], ALU.mult, a, rope_made)
                v = c.tt(plain.buf[:, :], b.buf[:, :], cos[:, :], ALU.mult, a, rope_made, plain.wait)
                b.free = [a, v]
                v = c.tt(out, plain.buf[:, :], swapped.buf[:, :], ALU.add, p, *marks)
                swapped.free, plain.free = [v], [v]
                rotate.made = v
                yield

            ki, qi, wi = isb("ki", [P, T]), isb("qi", [P, IH // 2, T]), isb("wi", [P, TT, IH])
            run(rotate(("ki", 0), 32, cos64, sin64, rope64, ki[:, :], before))
            b = c.acc.take()
            run(c.project_tokens(("wi", 0), b))
            wi_made = c.ts(wi[:, :, :], b.buf[:, 0:TT * IH].rearrange("p (t h) -> p t h", h=IH),
                           float(IH ** -0.5), ALU.mult, None, None, b.made)
            b.free = [wi_made]
            qi_made = []
            for i in range(IH // 2):
                run(rotate(("qi", i), 32, cos64, sin64, rope64, qi[:, i, :], before))
                qi_made.append(rotate.made)

            def scores():
                for t in range(TT):
                    for h in range(IH):
                        hs = slice(h % 2 * 64, h % 2 * 64 + 64)
                        b = c.work.take()
                        m = c.mm(b.buf[:, :], qi[hs, h // 2, t * P:(t + 1) * P], ki[hs, :], True, True, b.wait,
                                 qi_made[h // 2], signal=True)
                        s = probs.take()
                        a = c.act(s.buf[:, :], b.buf[:, :], ACT.Relu, m, s.wait, scale=0.125)
                        b.free = [a]
                        v = c.stt(score[:, t, :], s.buf[:, :], wi[:, t, h:h + 1],
                                  bias[:, t, :] if h == 0 else score[:, t, :], ALU.mult, ALU.add, a, wi_made, adm)
                        s.free = [v]
                        yield
                best = isb("best", [P, 8])
                for t in range(TT):
                    for _ in range(TOPK // 8):
                        c.DVE.do(lambda e, t=t: e.max(best[:, :], score[:, t, :]))
                        c.DVE.do(lambda e, t=t: e.match_replace(score[:, t, :], best[:, :], score[:, t, :], TAKEN))
                        yield
                    c.ts(score[:, t, :], score[:, t, :], -2e38, ALU.is_le, -NEG, ALU.mult)
                    scores.made = c.stt(bias[:, t, :], score[:, t, :], NEG, bias[:, t, :], ALU.add, ALU.add)
                    yield

            q_made = [None] * AH

            def main():
                yield from rotate(("k", 0), 64, cos128, sin128, rope128, keys[:, :], before)
                main.keys = rotate.made
                b = c.acc.take()
                yield from c.project_tokens(("v", 0), b)
                main.values = c.act(values[:, :, :], b.buf[:, :].rearrange("p (t d) -> p t d", d=P), ACT.Copy,
                                    b.made, before)
                b.free = [main.values]
                for h in range(AH):
                    yield from rotate(("q", h), 64, cos128, sin128, rope128, Q[:, h, :], before)
                    q_made[h] = rotate.made

            run(together(main(), scores()))
            c.dump("bias", bias[:, :, :])
            c.dump("q", Q[:, :, :])
        gates = c.ring("gate", 2, [P, T], layer, c.everyone())
        scale = float(P ** -0.5)
        out_made = []
        run_gates = {}

        def gate(h):
            b = c.acc.take()
            yield from c.project(("g", h), b)
            g = gates.take()
            g.made = c.act(g.buf[:, :], b.buf[:, :], ACT.Silu, b.made, g.wait)
            b.free = [g.made]
            run_gates[h] = g

        def head(h):
            pt = PT.take()
            marks = []
            for t in range(TT):
                b = c.work.take()
                m = c.mm(b.buf[:, :], Q[:, h, t * P:(t + 1) * P], keys[:, :], True, True, b.wait, q_made[h],
                         main.keys, signal=True)
                marks.append(softmax_tile(c, b, m, bias[:, t, :], probs.take(), small, h * TT + t, scale,
                                          TT, pt, t, scores.made))
                yield
            o = c.work.take()
            for j in range(TT):
                m = c.mm(o.buf[:, :], values[:, j, :], pt.buf[:, j, :], j == 0, j == TT - 1, o.wait, marks,
                         main.values, signal=j == TT - 1)
            pt.free = [m]
            g = run_gates[h]
            v = c.tt(Q[:, h, :], o.buf[:, :], g.buf[:, :], ALU.mult, m, g.made)
            o.free, g.free = [v], [v]
            out_made.append(v)

        run(gate(0))
        for h in range(AH):
            run(together(head(h), *([gate(h + 1)] if h + 1 < AH else [])))
        c.dump("og", Q[:, :, :])
        c.x_gate = lambda k: c.mods[1][:, 2 * DT + k:2 * DT + k + 1]
        own = [Q[:, h, :] for h in range(AH)]
        c.pending = (own, out_made)
        return c.out_project("odd_out", own, out_made, c.x, x_marks, c.x_gate, c.mod_made[1, 2])


def softmax_tile(c, bank, logits, bias, prob, small, i, scale, width, pt, t, *marks):
    n = width * P
    mx, total, inv = (small[:, 3 * i + j:3 * i + j + 1] for j in range(3))
    p = prob.buf[:, 0:n]
    v = c.DVE.do(lambda e: e.tensor_tensor_reduce(p, bank.buf[:, 0:n], bias, 1.0, 3 * NEG, ALU.add, ALU.max, mx),
                 logits, prob.wait, *marks)
    bank.free = [v]
    v = c.ts(mx, mx, -scale, ALU.mult, None, None, v)
    a = c.act(p, p, ACT.Exp, v, bias=mx, scale=scale, accum_out=total)
    v = c.recip(inv, total, a)
    v = c.ts(p, p, inv, ALU.mult, None, None, v)
    b = c.work.take()
    for j in range(width):
        m = c.tr(b.buf[:, j * P:(j + 1) * P], p[:, j * P:(j + 1) * P], v, b.wait, signal=j == width - 1)
    prob.free = [m]
    dst = pt.buf[:, 0:width, t * P:(t + 1) * P]
    src = b.buf[:, 0:n].rearrange("p (j q) -> p j q", q=P)
    done = c.act(dst, src, ACT.Copy, m, pt.wait) if t % 2 else c.copy(dst, src, m, pt.wait)
    b.free = [done]
    return done


def softplus_of_minus(c, x, u, z, tmp, *marks):
    a = c.act(u, x, ACT.Abs, *marks)
    a = c.act(u, u, ACT.Exp, a, scale=-1.0)
    v = c.ts(z, u, 2.0, ALU.add, None, None, a)
    v = c.recip(z, z)
    v = c.tt(z, z, u, ALU.mult)
    v = c.tt(u, z, z, ALU.mult)
    v = c.ts(tmp, u, 2.0 / 19, ALU.mult, 2.0 / 17, ALU.add)
    for k in range(15, -1, -2):
        v = c.tt(tmp, tmp, u, ALU.mult)
        v = c.ts(tmp, tmp, 2.0 / k, ALU.add, None, None)
    v = c.tt(tmp, tmp, z, ALU.mult)
    v = c.ts(x, x, -1.0, ALU.mult, 0.0, ALU.max)
    return c.tt(x, x, tmp, ALU.add)


def lru_layer(c, x_marks):
    with ExitStack() as layer:
        before = c.everyone()
        sb = lambda name, shape: c.sb(name, shape, scope=layer)
        Y = sb("lru_y", [P, LT, T])
        with ExitStack() as scope:
            gates_w = c.sb("lru_gates_w", [P, 2, LRU], scope=scope)
            w_in = c.dma(gates_w[:, :, :], c.t["lru_gates"], c.sem("lru_gates_in"), before)
            padded = c.ring("lru_padded", 3, [P, LTAPS - 1 + T], scope, before)
            for s in padded.slots:
                s.free = [c.fill(s.buf[:, 0:LTAPS - 1], 0.0, before)]
            tmp = c.ring("lru_tmp", 12, [P, T], scope, before)
            rate = c.sb("lru_rate", [P, 2, LT], scope=scope)
            aux = c.sb("lru_aux", [P, 3, LT], scope=scope)
            v = c.copy(rate[:, 0, :], c.vec("lru_a", 0, LT), before, c.vecs_in)
            v = softplus_of_minus(c, rate[:, 0, :], aux[:, 0, :], aux[:, 1, :], aux[:, 2, :], v)
            c.ts(rate[:, 1, :], rate[:, 0, :], LRU_C, ALU.mult, None, None)
            rate_made = c.ts(rate[:, 0, :], rate[:, 0, :], -LRU_C, ALU.mult, None, None)
            made = []

            def block(n):
                b = c.acc.take()
                yield from c.project(("lru", n), b)
                xp = padded.take()
                a = c.act(xp.buf[:, LTAPS - 1:], b.buf[:, :], ACT.Copy, b.made, xp.wait)
                b.free = [a]
                xc = tmp.take()
                w = lambda j: c.vec("lru_conv_w", j * LT + n)
                v = c.ts(xc.buf[:, :], xp.buf[:, 0:T], w(0), ALU.mult, c.vec("lru_conv_b", n), ALU.add, a, xc.wait)
                for j in range(1, LTAPS):
                    v = c.stt(xc.buf[:, :], xp.buf[:, j:j + T], w(j), xc.buf[:, :], ALU.mult, ALU.add)
                xp.free = [v]
                b = c.acc.take()
                yield from c.project(("lru", LT + n), b)
                sg = tmp.take()
                silu = c.act(sg.buf[:, :], b.buf[:, :], ACT.Silu, b.made, sg.wait)
                b.free = [silu]
                yield
                g = []
                for i in range(2):
                    b = c.work.take()
                    m = c.mm(b.buf[:, :], gates_w[:, i, n * P:(n + 1) * P], xc.buf[:, :], True, True, b.wait, v,
                             w_in, signal=True)
                    s = tmp.take()
                    s.made = c.act(s.buf[:, :], b.buf[:, :], ACT.Sigmoid, m, s.wait, c.vecs_in,
                                   bias=c.vec(("lru_ba", "lru_bx")[i], n))
                    b.free = [s.made]
                    g.append(s)
                r, i = g
                decay, root = tmp.take(), tmp.take()
                a = c.act(decay.buf[:, :], r.buf[:, :], ACT.Exp, rate_made, decay.wait, scale=rate[:, 0, n:n + 1])
                th = c.act(r.buf[:, :], r.buf[:, :], ACT.Tanh, scale=rate[:, 1, n:n + 1])
                p = c.ptt(root.buf[:, :], decay.buf[:, :], decay.buf[:, :], ALU.mult, a, root.wait)
                ix = c.ptt(i.buf[:, :], i.buf[:, :], xc.buf[:, :], ALU.mult, i.made, v)
                v = c.stt(root.buf[:, :], root.buf[:, :], 1.0, r.buf[:, :], ALU.add, ALU.mult, p, th)
                a = c.act(root.buf[:, :], root.buf[:, :], ACT.Sqrt, v)
                v = c.tt(root.buf[:, :], root.buf[:, :], i.buf[:, :], ALU.mult, a, ix)
                v = c.scan(r.buf[:, :], decay.buf[:, :], root.buf[:, :])
                v = c.tt(Y[:, n, :], r.buf[:, :], sg.buf[:, :], ALU.mult, silu, before)
                for s in (xc, sg, r, i, decay, root):
                    s.free = [v]
                made.append(v)

            for n in range(LT):
                run(block(n))
        c.dump("lru_y", Y[:, 0:8, :])
        return c.out_project("lru_out", [Y[:, n, :] for n in range(LT)], made, c.x, x_marks)


def fox_layer(c, x_marks):
    with ExitStack() as layer:
        before = c.everyone()
        sb = lambda name, shape: c.sb(name, shape, scope=layer)
        G = sb("fox_gate", [P, DT, T])
        with ExitStack() as scope:
            sb = lambda name, shape: c.sb(name, shape, scope=scope)
            Q, K, V = sb("fox_q", [P, DT, T]), sb("fox_k", [P, DT, T]), sb("fox_v", [P, TT, D])
            probs = c.ring("fox_probs", 3, [P, T], scope, before)
            PT = c.ring("fox_probs_t", 2, [P, TT, T], scope, before)
            keybias = c.ring("fox_keybias", 2, [P, T], scope, before)
            small = sb("fox_small", [P, 3 * FH * TT])
            rows = sb("fox_rows", [FH, 4, T])
            pick = sb("fox_pick", [FH, FH, P])
            c.fill(pick[:, :, :], 0.0, before)
            picked = c.select(pick[:, :, :], [[-1, FH], [0, P]], 0, 1, ALU.not_equal, 1.0)
            b = c.acc.take()
            run(c.project(("fox_f", 0), b))
            f, u, z, tmp = (rows[:, i, :] for i in range(4))
            v = c.ts(f, b.buf[0:FH, :], c.vec("fox_b")[0:FH], ALU.add, None, None, b.made, before, c.vecs_in)
            b.free = [v]
            v = softplus_of_minus(c, f, u, z, tmp, v)
            c.DVE.do(lambda e: e.memset(u, 1.0))
            sums = c.scan(z, u, f)
            q_made, k_made, v_made, g_made = ([None] * DT for _ in range(4))

            def pair_in(p):
                for key, made, dst, func, kw in (("fox_q", q_made, Q, ACT.Copy, {"scale": 0.125}),
                                                 ("fox_k", k_made, K, ACT.Copy, {}),
                                                 ("fox_g", g_made, G, ACT.Silu, {})):
                    b = c.acc.take()
                    yield from c.project((key, p), b)
                    made[p] = c.act(dst[:, p, :], b.buf[:, :], func, b.made, before, **kw)
                    b.free = [made[p]]
                b = c.acc.take()
                yield from c.project_tokens(("fox_v", p), b)
                v_made[p] = c.copy(V[:, :, p * P:(p + 1) * P], b.buf[:, :].rearrange("p (t d) -> p t d", d=P),
                                   b.made, before)
                b.free = [v_made[p]]

            out_made = []

            def pair_out(p):
                o = c.work.take()
                for h in (2 * p, 2 * p + 1):
                    hs = slice(h % 2 * 64, h % 2 * 64 + 64)
                    b = c.work.take()
                    m = c.mm(b.buf[:, :], pick[:, h, :], z, True, True, b.wait, picked, sums, signal=True)
                    kb = keybias.take()
                    kb.made = c.act(kb.buf[:, :], b.buf[:, :], ACT.Copy, m, kb.wait)
                    b.free = [kb.made]
                    pt = PT.take()
                    marks = []
                    for t in range(TT):
                        n = (t + 1) * P
                        b = c.work.take()
                        c.mm(b.buf[:, 0:n], Q[hs, p, t * P:n], K[hs, p, 0:n], True, False, b.wait, q_made[p],
                             k_made[p])
                        m = c.mm(b.buf[:, t * P:n], c.ident[:, :], c.causal[:, :], False, True, c.consts_made,
                                 signal=True)
                        marks.append(softmax_tile(c, b, m, kb.buf[:, 0:n], probs.take(), small, h * TT + t, 1.0,
                                                  t + 1, pt, t, kb.made))
                        yield
                    kb.free = [c.DVE.mark()]
                    for j in range(TT):
                        m = c.mm(o.buf[hs, j * P:], V[:, j, p * P + hs.start:p * P + hs.stop], pt.buf[:, j, j * P:],
                                 j == 0, j == TT - 1, o.wait, marks, v_made[p], signal=j == TT - 1)
                    pt.free = [m]
                v = c.tt(G[:, p, :], o.buf[:, :], G[:, p, :], ALU.mult, m, g_made[p])
                o.free = [v]
                out_made.append(v)

            run(pair_in(0))
            for p in range(DT):
                run(together(pair_out(p), *([pair_in(p + 1)] if p + 1 < DT else [])))
        return c.out_project("fox_out", [G[:, p, :] for p in range(DT)], out_made, c.x, x_marks)


def weight_plan(t):
    plan = []

    def add(key, name, *at, split=True):
        block = t[name]
        for i in at:
            block = block[i]
        width = P if block.shape[1] % P == 0 else block.shape[1] // DT
        plan.append((key, block, block.shape[1] // width, width, split))

    def ada(l, part):
        for j in range(part * DT, (part + 1) * DT):
            add(("ada", l, j), "ada", l * 3 * DT + j, split=False)

    def out(name):
        for cb in range(DT):
            for half in range(2):
                add((name, cb, half), name, 2 * cb + half)

    ada(0, 0), ada(0, 1)
    for k in range(DT):
        for j in range(3):
            add(("even", j * DT + k), "even_in", j * DT + k)
    add(("even", 6 * DT), "even_in", 6 * DT)
    for p in range(DT):
        for j in (4, 3, 5):
            add(("even", j * DT + p), "even_in", j * DT + p)
        add(("even", 6 * DT + 1 + p), "even_in", 6 * DT + 1 + p)
    ada(0, 2)
    out("even_out")
    for part in range(3):
        ada(1, part)
    add(("ki", 0), "odd_in", 2 * AH + 2 + IH // 2)
    add(("wi", 0), "odd_wi", 0)
    for i in range(IH // 2):
        add(("qi", i), "odd_in", AH + 2 + i)
    add(("k", 0), "odd_in", AH)
    add(("v", 0), "odd_in", AH + 1)
    for h in range(AH):
        add(("q", h), "odd_in", h)
    for h in range(AH):
        add(("g", h), "odd_in", AH + 2 + IH // 2 + h)
    out("odd_out")
    for n in range(LT):
        add(("lru", n), "lru_in", n)
        add(("lru", LT + n), "lru_in", LT + n)
    out("lru_out")
    add(("fox_f", 0), "fox_in", 4 * DT)
    for p in range(DT):
        for key, j in (("fox_q", 0), ("fox_k", 1), ("fox_g", 3), ("fox_v", 2)):
            add((key, p), "fox_in", j * DT + p)
    out("fox_out")
    return plan


def build(nc, t, debug=(), layers=4):
    with ExitStack() as ctx:
        c = Core(nc, t, ctx, debug)
        x = c.x
        marks = [c.dma(x[:, k, :], t["x_t"][k * P:(k + 1) * P, :], c.sem(f"x_in{k}")) for k in range(DT)]
        with ExitStack() as scope:
            sq = c.ring("sq", 2, [P, T], scope, ())
            for k in range(DT):
                summed = c.square_sum(x[:, k, :], k, marks[k], sq)
        run(c.modulation(0, (0, 1)))
        c.norm_into_h(x, marks, summed, lambda k: c.gains[0][:, k:k + 1], lambda k: c.mods[0][:, k:k + 1],
                      c.mod_made[0, 0], c.mod_made[0, 1])
        c.dump("h_hi", c.h_hi[:, :, :].bitcast(F32))
        marks, summed = even_layer(c)
        c.dump("x0", x[:, :, :])
        if layers > 1:
            run(c.modulation(1, (0, 1, 2)))
            c.norm_into_h(x, marks, summed, lambda k: c.gains[1][:, k:k + 1], lambda k: c.mods[1][:, k:k + 1],
                          c.mod_made[1, 0], c.mod_made[1, 1])
            marks, summed = odd_layer(c, marks)
            c.dump("x1", x[:, :, :])
        if layers > 2:
            with ExitStack() as scope:
                before = c.everyone()
                rms = c.sb("rms", [P, T], scope=scope)
                sq = c.ring("sq", 2, [P, T], scope, before)
                inverse = c.inverse_rms(rms[:, :], summed, before)
                for k in range(DT):
                    v = c.tt(x[:, k, :], x[:, k, :], rms[:, :], ALU.mult, marks[k], inverse)
                    marks[k] = c.ts(x[:, k, :], x[:, k, :], c.vec("final_g", k), ALU.mult, None, None, v)
                    summed = c.square_sum(x[:, k, :], k, marks[k], sq)
            c.norm_into_h(x, marks, summed, lambda k: c.vec("norm2_g0", k), None)
            marks, summed = lru_layer(c, marks)
            c.dump("x2", x[:, :, :])
        if layers > 3:
            c.norm_into_h(x, marks, summed, lambda k: c.vec("norm2_g1", k), None)
            marks, summed = fox_layer(c, marks)
            c.dump("x3", x[:, :, :])
        with ExitStack() as scope:
            before = c.everyone()
            rms = c.sb("rms", [P, T], scope=scope)
            inverse = c.inverse_rms(rms[:, :], summed, before)
            for k in range(DT):
                v = c.tt(x[:, k, :], x[:, k, :], rms[:, :], ALU.mult, marks[k], inverse)
                v = c.ts(x[:, k, :], x[:, k, :], c.vec("final2_g", k), ALU.mult, None, None, v)
                c.stores.append(c.dma(t["out"][k * P:(k + 1) * P, :], x[:, k, :], c.sem(f"out{k}"), v))

        with nc.Block() as block:
            @block.sync
            def _(e):
                for issue in c.SP.queue:
                    issue(e)
                for semaphore, value in c.stores:
                    e.wait_ge(semaphore, value)

            @block.tensor
            def _(e):
                for issue in c.PE.queue:
                    issue(e)

            @block.vector
            def _(e):
                for issue in c.DVE.queue:
                    issue(e)

            @block.scalar
            def _(e):
                for issue in c.ACTE.queue:
                    issue(e)

            @block.gpsimd
            def _(e):
                for issue in c.POOL.queue:
                    issue(e)


def blocks(w, width=P):
    k, n = w.shape
    return np.ascontiguousarray(w.reshape(k // P, P, n // width, width).transpose(2, 1, 0, 3)).reshape(
        n // width, P, (k // P) * width)


def half_blocks(w):
    k, n = w.shape
    return np.ascontiguousarray(w.reshape(2, k // (2 * P), P, n // P, P).transpose(3, 0, 2, 1, 4)).reshape(
        2 * n // P, P, k // 2)


def columns(v):
    v = v.reshape(-1, v.shape[-1] // P, P)
    return v.transpose(2, 0, 1).reshape(P, -1)


def kernel(debug=(), layers=4, **inputs):
    import concourse.bacc as bacc
    from concourse.bass_utils import run_bass_kernel_spmd

    a = {k: np.asarray(v) for k, v in inputs.items()}
    inverse = lambda d: np.float32(10000.0) ** (-np.arange(0, d, 2, dtype=np.float32) / np.float32(d))
    conv = a["conv_w"][0, :, 0, :].reshape(TAPS, DT, P).transpose(2, 1, 0).reshape(P, DT * TAPS)
    fox_b = np.zeros((P, 1), np.float32)
    fox_b[:FH, 0] = a["fox_b_f_2"][0]
    vecs = [columns(a["c"]), columns(a["ada_b"][0]), columns(a["ada_b"][1]), columns(a["norm_g"][0]),
            columns(a["norm_g"][1]), columns(a["final_g"]), conv, columns(a["conv_vec"][0]),
            columns(a["rwkv_mu_rkv"][0]), a["rwkv_mu_lora"][0].reshape(P, 1), columns(a["rwkv_vec"][0]),
            columns(a["rwkv_r_k"][0].reshape(-1)), np.tile(inverse(128), 2).reshape(P, 1),
            np.tile(inverse(64), 4).reshape(P, 1), columns(a["norm_g_2"][0]), columns(a["norm_g_2"][1]),
            columns(a["final_g_2"]), columns(a["lru_conv_w_2"][0]), columns(a["lru_conv_b_2"][0]),
            columns(a["lru_ba_2"][0]), columns(a["lru_bx_2"][0]), columns(a["lru_a_param_2"][0]), fox_b]
    odd = a["odd_w_in"][0]
    w, at = {}, 0
    for name, n in (("q", AH * P), ("k", P), ("v", P), ("qi", IH * 64), ("ki", 64), ("wi", IH), ("g", AH * P)):
        w[name] = odd[:, at:at + n]
        at += n
    pos = a["positions"].reshape(1, T)
    fox = a["fox_w_in_2"][0]
    arrays = {
        "x_t": np.ascontiguousarray(a["x"][0].T),
        "vecs": np.ascontiguousarray(np.concatenate(vecs, axis=1)),
        "ada": np.concatenate([blocks(a["ada_w"][l]) for l in range(2)]),
        "even_in": blocks(a["even_w_in"][0]),
        "even_out": half_blocks(a["even_w_out"][0]),
        "lora_up": np.ascontiguousarray(np.concatenate([a["rwkv_w_up"][0], a["rwkv_a_up"][0]])),
        "odd_in": blocks(np.concatenate([w["q"], w["k"], w["v"], w["qi"], w["g"], w["ki"], w["ki"]], axis=1)),
        "odd_wi": blocks(w["wi"], IH),
        "odd_out": half_blocks(a["odd_w_out"][0]),
        "pos": np.ascontiguousarray(pos),
        "pos_q": np.ascontiguousarray(pos.reshape(TT, P).T),
        "lru_in": blocks(a["lru_w_in_2"][0]),
        "lru_gates": np.ascontiguousarray(np.stack(
            [a[n][0].transpose(1, 0, 2).reshape(P, LRU) for n in ("lru_wa_2", "lru_wx_2")], axis=1)),
        "lru_out": half_blocks(a["lru_w_out_2"][0]),
        "fox_in": blocks(np.concatenate([fox, np.zeros((D, P - FH), np.float32)], axis=1)),
        "fox_out": half_blocks(a["fox_w_out_2"][0]),
    }
    nc = bacc.Bacc("TRN2", target_bir_lowering=False, num_devices=1)
    t = {k: nc.dram_tensor(k, list(v.shape), I32 if v.dtype.kind == "i" else F32, kind="ExternalInput").ap()
         for k, v in arrays.items()}
    t["out"] = nc.dram_tensor("out", [D, T], F32, kind="ExternalOutput").ap()
    sizes = {"ya": DT, "yb": DT, "x0": DT, "h_hi": DT, "x1": DT, "x2": DT, "x3": DT, "q": AH, "og": AH,
             "bias": TT, "lru_y": 8}
    for name in debug:
        t["dbg_" + name] = nc.dram_tensor("dbg_" + name, [P, sizes[name], T], F32, kind="ExternalOutput").ap()
    build(nc, t, debug, layers)
    result = run_bass_kernel_spmd(nc, [arrays], core_ids=[0])
    return np.ascontiguousarray(result.results[0]["out"].T).reshape(1, T, D)
```

```python
from contextlib import ExitStack

import numpy as np

from concourse import mybir

ALU = mybir.AluOpType
ACT = mybir.ActivationFunctionType
F32 = mybir.dt.float32
F32R = mybir.dt.float32r
I32 = mybir.dt.int32

P = 128
T = 512
D = 1024
DT = D // P
TT = T // P
TAPS = 31
RH = 64
LORA = 64
CH = P
NCH = T // CH
DECAY = float(np.exp(-0.5))
AH = 16
IH = 8
TOPK = min(256, T // 4)
LRU = 1536
LT = LRU // P
LTAPS = 4
LRU_C = 8.0
FH = 16
NEG = -1e30
TAKEN = -3e38
ROUND = 1.5 * 2.0 ** 23
NRAW, NSPLIT = 3, 2
SIDE_STEPS = 1.5
SOFTMAX_LAG = 3
TWO_PI = (6.28125, 0.0019350051879882812, 3.019916050561733e-07)


def vector_columns():
    names = [("c", DT), ("ada_b0", 3 * DT), ("ada_b1", 3 * DT), ("norm_g0", DT), ("norm_g1", DT),
             ("final_g", DT), ("conv_w", DT * TAPS), ("conv_vec", 3 * DT), ("mu_rkv", 3 * DT),
             ("mu_lora", 1), ("rwkv_vec", 6 * DT), ("r_k", DT), ("inv128", 1), ("inv64", 1),
             ("norm2_g0", DT), ("norm2_g1", DT), ("final2_g", DT), ("lru_conv_w", LT * LTAPS),
             ("lru_conv_b", LT), ("lru_ba", LT), ("lru_bx", LT), ("lru_a", LT), ("fox_b", 1)]
    at, out = 0, {}
    for name, n in names:
        out[name] = (at, n)
        at += n
    return out, at


class Lane:

    def __init__(self, sem, chained=True):
        self.sem, self.chained, self.count, self.queue, self.waited = sem, chained, 0, [], {}

    def wait(self, *marks):
        for m in marks:
            if isinstance(m, list):
                self.wait(*m)
            elif m is not None and self.waited.get(m[0].name, 0) < m[1]:
                self.waited[m[0].name] = m[1]
                self.queue.append(lambda e, m=m: e.wait_ge(m[0], m[1]))

    def do(self, issue, *marks, signal=True):
        if self.chained and self.count:
            self.wait((self.sem, self.count))
        self.wait(*marks)
        if not signal:
            self.queue.append(issue)
            return None
        self.count += 1
        self.queue.append(lambda e: issue(e).then_inc(self.sem, 1))
        return (self.sem, self.count)

    def mark(self):
        return (self.sem, self.count) if self.count else None


class Slot:

    def __init__(self, buf, free=()):
        self.buf, self.free, self.wait = buf, list(free), None

    def hold(self):
        assert self.free is not None
        self.wait, self.free = self.free, None
        return self


class Ring:

    def __init__(self, slots):
        self.slots, self.at = slots, 0

    def take(self):
        for _ in self.slots:
            s = self.slots[self.at % len(self.slots)]
            self.at += 1
            if s.free is not None:
                return s.hold()
        raise AssertionError("every buffer of the ring is held")


def blend(main, side, steps):
    due = 0.0
    for _ in main:
        due += steps
        while due >= 1:
            due -= 1
            next(side, None)
        yield
    yield from side


def in_turn(*stages):
    stages = list(stages)
    while stages:
        for g in list(stages):
            try:
                next(g)
            except StopIteration:
                stages.remove(g)
            yield


def chain(*stages):
    for g in stages:
        yield from g


class Core:

    def __init__(self, nc, t, ctx, debug):
        self.nc, self.t, self.ctx, self.debug, self.names = nc, t, ctx, debug or (), 0
        self.PE = Lane(self.sem("pe_done"), chained=False)
        self.DVE = Lane(self.sem("dve_done"))
        self.ACTE = Lane(self.sem("act_done"))
        self.POOL = Lane(self.sem("pool_done"))
        self.SP = Lane(None, chained=False)
        self.dma_total, self.stores, self.mod_made = {}, [], {}

        banks = [ctx.enter_context(nc.psum_tensor(f"bank{i}", [P, T], F32)) for i in range(8)]
        self.acc = Ring([Slot(b) for b in banks[0:2]])
        self.work = Ring([Slot(b) for b in banks[2:7]])
        self.stat = Slot(banks[7])

        self.cols, n_cols = vector_columns()
        self.vecs = self.sb("vecs", [P, n_cols])
        self.ident = self.sb("ident", [P, P])
        self.ones = self.sb("ones", [P, P])
        self.head_ones = self.sb("head_ones", [P, P])
        self.causal = self.sb("causal", [P, P])
        self.few = self.sb("few", [P, 5])
        self.rms_eps, self.ln_eps, self.gn_eps, self.sign128, self.sign64 = (
            self.few[:, i:i + 1] for i in range(5))
        self.mods = [self.sb(f"mod{l}", [P, 3 * DT]) for l in range(2)]
        self.gains = [self.sb(f"gain{l}", [P, DT]) for l in range(2)]
        self.silu_c = self.sb("silu_c", [P, DT])
        self.h_hi = self.sb("h_hi", [P, DT, T], F32R)
        self.h_lo = self.sb("h_lo", [P, DT, T], F32R)
        self.H = [(self.h_hi[:, k, :], self.h_lo[:, k, :]) for k in range(DT)]
        self.h_marks = [None] * DT
        self.h_free = []

        self.x = self.sb("x", [P, DT, T])

        self.raw = [Slot(self.sb(f"raw{i}", [P, DT * P])) for i in range(NRAW)]
        self.raw_sems = [self.sem(f"raw{i}_in") for i in range(NRAW)]
        self.split = [Slot((self.sb(f"w_hi{i}", [P, DT * P], F32R), self.sb(f"w_lo{i}", [P, DT * P], F32R)))
                      for i in range(NSPLIT)]
        self.plan, self.loaded, self.taken, self.splits, self.ready = weight_plan(t), 0, 0, 0, {}
        self.constants()

    def sem(self, name):
        return self.ctx.enter_context(self.nc.semaphore(name))

    def sb(self, name, shape, dt=F32, scope=None):
        self.names += 1
        return (scope or self.ctx).enter_context(self.nc.sbuf_tensor(f"{name}_{self.names}", shape, dt))

    def ring(self, name, n, shape, scope, free):
        return Ring([Slot(self.sb(f"{name}{i}", shape, scope=scope), free) for i in range(n)])

    def dma(self, out, in_, semaphore, *marks):
        self.SP.wait(*marks)
        self.SP.queue.append(lambda e: e.dma_start(out, in_).then_inc(semaphore, 16))
        self.dma_total[semaphore.name] = self.dma_total.get(semaphore.name, 0) + 16
        return (semaphore, self.dma_total[semaphore.name])

    def everyone(self):
        return [x.mark() for x in (self.PE, self.DVE, self.ACTE, self.POOL)]

    def vec(self, name, i=0, n=1):
        at, count = self.cols[name]
        assert i + n <= count
        return self.vecs[:, at + i:at + i + n]

    def dump(self, name, ap):
        if name in self.debug:
            self.stores.append(self.dma(self.t["dbg_" + name], ap, self.sem(f"dump_{name}"), self.everyone()))
            for lane in (self.PE, self.DVE, self.ACTE, self.POOL):
                lane.wait(self.stores[-1])

    def act(self, out, in_, func, *marks, **kw):
        return self.ACTE.do(lambda e: e.activation(out, in_, func, **kw), *marks)

    def tt(self, out, a, b, op, *marks):
        return self.DVE.do(lambda e: e.tensor_tensor(out, a, b, op), *marks)

    def ts(self, out, a, s1, op0, s2, op1, *marks):
        if op1 is None:
            return self.DVE.do(lambda e: e.tensor_scalar(out, a, s1, None, op0), *marks)
        return self.DVE.do(lambda e: e.tensor_scalar(out, a, s1, s2, op0, op1), *marks)

    def stt(self, out, a, s, b, op0, op1, *marks):
        return self.DVE.do(lambda e: e.scalar_tensor_tensor(out, a, s, b, op0, op1), *marks)

    def copy(self, out, a, *marks):
        return self.DVE.do(lambda e: e.tensor_copy(out, a), *marks)

    def recip(self, out, a, *marks):
        return self.DVE.do(lambda e: e.reciprocal(out, a), *marks)

    def scan(self, out, a, b, *marks):
        return self.DVE.do(lambda e: e.tensor_tensor_scan(out, a, b, 0.0, ALU.mult, ALU.add), *marks)

    def ptt(self, out, a, b, op, *marks):
        return self.POOL.do(lambda e: e.tensor_tensor(out, a, b, op), *marks)

    def fill(self, ap, value, *marks):
        return self.POOL.do(lambda e: e.memset(ap, value), *marks)

    def select(self, ap, pattern, base, cm, op, value, *marks):
        return self.POOL.do(lambda e: e.affine_select(out=ap, in_=ap, pattern=pattern, compare_op=op, fill=value,
                                                      base=base, channel_multiplier=cm), *marks)

    def mm(self, out, lhsT, rhs, start, stop, *marks, signal=False):
        return self.PE.do(lambda e: e.matmul(out, lhsT, rhs, start=start, stop=stop, skip_group_check=True),
                          *marks, signal=signal)

    def tr(self, out, in_, *marks, signal=False):
        k = in_.shape[0]
        return self.PE.do(lambda e: e.transpose(out, in_, self.ident[0:k, 0:k]), self.consts_made, *marks,
                          signal=signal)

    def load_next(self):
        n = self.loaded
        _, src, kt, width, split = self.plan[n]
        self.loaded += 1
        size = kt * width
        raw = self.raw[n % NRAW].hold()
        landed = self.dma(raw.buf[:, 0:size], src, self.raw_sems[n % NRAW], raw.wait)
        if not split:
            self.ready[n] = (raw, raw.buf, None, landed)
            return
        s = self.split[self.splits % NSPLIT].hold()
        self.splits += 1
        hi, lo = s.buf
        rounded = self.act(hi[:, 0:size], raw.buf[:, 0:size], ACT.Copy, landed, s.wait)
        rest = self.ptt(lo[:, 0:size], raw.buf[:, 0:size], hi[:, 0:size].bitcast(F32), ALU.subtract,
                        landed, rounded, s.wait)
        raw.free = [rounded, rest]
        self.ready[n] = (s, hi, lo, [rounded, rest])

    def weights(self, key):
        n = self.taken
        assert self.plan[n][0] == key, (self.plan[n][0], key)
        self.taken += 1
        if n not in self.ready:
            self.load_next()
        return self.ready.pop(n) + self.plan[n][2:4]

    def look_ahead(self):
        if self.loaded < len(self.plan) and self.loaded < self.taken + NSPLIT - 1:
            self.load_next()

    def project(self, key, bank, x=None, x_marks=None, start=True, stop=True):
        x, x_marks = x or self.H, x_marks or self.h_marks
        slot, hi, lo, landed, kt, width = self.weights(key)
        out = bank.buf[0:width, :]
        for k in range(kt):
            w = slice(k * width, (k + 1) * width)
            last = k == kt - 1
            self.mm(out, hi[:, w], x[k][0], start and k == 0, False, landed, bank.wait, x_marks[k])
            self.mm(out, hi[:, w], x[k][1], False, False)
            m = self.mm(out, lo[:, w], x[k][0], False, stop and last, signal=last)
            if k == 0:
                self.look_ahead()
            if not last:
                yield
        slot.free = [m]
        bank.made = m

    def project_tokens(self, key, bank):
        slot, hi, lo, landed, kt, width = self.weights(key)
        for tt in range(TT):
            out = bank.buf[:, tt * width:(tt + 1) * width]
            at = slice(tt * P, (tt + 1) * P)
            for k in range(kt):
                w = slice(k * width, (k + 1) * width)
                self.mm(out, self.H[k][0][:, at], hi[:, w], k == 0, False, landed, bank.wait, self.h_marks[k])
                self.mm(out, self.H[k][1][:, at], hi[:, w], False, False)
                m = self.mm(out, self.H[k][0][:, at], lo[:, w], False, k == kt - 1, signal=k == kt - 1)
                if k == kt // 2:
                    yield
            if tt == 0:
                self.look_ahead()
            yield
        slot.free = [m]
        bank.made = m

    def constants(self):
        self.vecs_in = self.dma(self.vecs[:, :], self.t["vecs"], self.sem("vecs_in"))
        self.fill(self.ident[:, :], 0.0)
        self.select(self.ident[:, :], [[-1, P]], 0, 1, ALU.not_equal, 1.0)
        self.fill(self.ones[:, :], 1.0)
        self.fill(self.head_ones[:, :], 0.0)
        for h in range(2):
            self.fill(self.head_ones[h * RH:(h + 1) * RH, h * RH:(h + 1) * RH], 1.0)
        self.fill(self.causal[:, :], 0.0)
        self.select(self.causal[:, :], [[-1, P]], 0, 1, ALU.is_ge, NEG)
        for ap, value in ((self.rms_eps, 1e-6), (self.ln_eps, 1e-5), (self.gn_eps, 64e-5)):
            self.fill(ap, value)
        for p0, s128, s64 in ((0, -1.0, -1.0), (32, -1.0, 1.0), (64, 1.0, -1.0), (96, 1.0, 1.0)):
            self.fill(self.few[p0:p0 + 32, 3:4], s128)
            self.fill(self.few[p0:p0 + 32, 4:5], s64)
        self.consts_made = self.POOL.mark()
        self.silu_c_made = self.act(self.silu_c[:, :], self.vec("c", 0, DT), ACT.Silu, self.vecs_in)

    def modulation(self, l, js):
        for j in js:
            bank = self.work.take()
            slot, w, _, landed, kt, width = self.weights(("ada", l, j))
            for k in range(kt):
                m = self.mm(bank.buf[:, 0:1], w[:, k * width:(k + 1) * width], self.silu_c[:, k:k + 1],
                            k == 0, k == kt - 1, landed, bank.wait, self.silu_c_made, signal=k == kt - 1)
            slot.free = [m]
            self.look_ahead()
            made = self.tt(self.mods[l][:, j:j + 1], bank.buf[:, 0:1], self.vec(f"ada_b{l}", j), ALU.add, m,
                           self.vecs_in)
            bank.free = [made]
            if DT <= j < 2 * DT:
                i = j - DT
                made = self.stt(self.gains[l][:, i:i + 1], self.mods[l][:, j:j + 1], 1.0,
                                self.vec(f"norm_g{l}", i), ALU.add, ALU.mult, made)
            self.mod_made[l] = made
            yield

    def square_sum(self, x, i, x_mark, sq):
        s = sq.take()
        a = self.act(s.buf[:, :], x, ACT.Square, x_mark, s.wait)
        m = self.mm(self.stat.buf[:, :], self.ones[:, :], s.buf[:, :], i == 0, i == DT - 1,
                    a, self.consts_made, self.stat.free if i == 0 else None, signal=True)
        s.free = [m]
        return m

    def inverse_rms(self, rms, summed, free):
        a = self.act(rms, self.stat.buf[:, :], ACT.Sqrt, summed, free, self.consts_made,
                     bias=self.rms_eps, scale=1.0 / D)
        self.stat.free = [a]
        return self.recip(rms, rms, a)

    def norm_into_h(self, x, x_marks, summed, gain, shift, *marks):
        with ExitStack() as scope:
            before = self.everyone()
            rms = self.sb("rms", [P, T], scope=scope)
            tmp = self.ring("normed", 3, [P, T], scope, before)
            inverse = self.inverse_rms(rms[:, :], summed, before)
            for k in range(DT):
                s = tmp.take()
                n = s.buf[:, :]
                v = self.tt(n, x[:, k, :], rms[:, :], ALU.mult, x_marks[k], inverse, s.wait)
                if shift is None:
                    v = self.ts(n, n, gain(k), ALU.mult, None, None, v, self.vecs_in)
                else:
                    v = self.ts(n, n, gain(k), ALU.mult, shift(k), ALU.add, v, *marks)
                a = self.act(self.h_hi[:, k, :], n, ACT.Copy, v, self.h_free)
                v = self.tt(self.h_lo[:, k, :], n, self.h_hi[:, k, :].bitcast(F32), ALU.subtract, a, self.h_free)
                s.free = [v]
                self.h_marks[k] = [a, v]
            self.h_free = []

    def out_project(self, name, src, src_marks, x, x_marks, gate=None, gate_mark=None):
        with ExitStack() as scope:
            before = self.everyone()
            n = len(src)
            half = n // 2
            own_hi = self.sb("own_hi", [P, n - half, T], F32R, scope)
            own_lo = self.sb("own_lo", [P, n - half, T], F32R, scope)
            pairs = self.H[:half] + [(own_hi[:, k, :], own_lo[:, k, :]) for k in range(n - half)]
            sq = self.ring("sq", 2, [P, T], scope, before)
            marks = []
            for k, (s, (hi, lo)) in enumerate(zip(src, pairs)):
                free = self.h_free if k < half else before
                a = self.act(hi, s, ACT.Copy, src_marks[k], free)
                marks.append([a, self.tt(lo, s, hi.bitcast(F32), ALU.subtract, a, src_marks[k], free)])
            if callable(x_marks):
                x_marks = x_marks(marks)
            new = []
            for cb in range(DT):
                bank = self.acc.take()
                for part, (a, b) in enumerate(((0, half), (half, n))):
                    for _ in self.project((name, cb, part), bank, pairs[a:b], marks[a:b], a == 0, b == n):
                        pass
                xs = x[:, cb, :]
                if gate is None:
                    v = self.tt(xs, bank.buf[:, :], xs, ALU.add, bank.made, x_marks[cb])
                else:
                    v = self.stt(xs, bank.buf[:, :], gate(cb), xs, ALU.mult, ALU.add, bank.made, x_marks[cb],
                                 gate_mark)
                bank.free = [v]
                new.append(v)
                if cb:
                    self.square_sum(x[:, cb - 1, :], cb - 1, new[cb - 1], sq)
            summed = self.square_sum(x[:, DT - 1, :], DT - 1, new[DT - 1], sq)
            self.h_free = [self.PE.mark()]
            return new, summed


def run(stage):
    for _ in stage:
        pass


def even_layer(c):
    with ExitStack() as layer:
        ya = c.sb("ya", [P, DT, T], scope=layer)
        yb = c.x
        ya_made, yb_made = even_mixers(c, ya, yb)
        c.dump("ya", ya[:, :, :])
        c.dump("yb", yb[:, :, :])

        def load_x(splits):
            return [c.dma(c.x[:, k, :], c.t["x_t"][k * P:(k + 1) * P, :], c.sem(f"x_back{k}"), splits[DT + k])
                    for k in range(DT)]

        src = [ya[:, k, :] for k in range(DT)] + [yb[:, k, :] for k in range(DT)]
        return c.out_project("even_out", src, ya_made + yb_made, c.x, load_x,
                             lambda k: c.mods[0][:, 2 * DT + k:2 * DT + k + 1], c.mod_made[0])


def convolve(c, k, ya, tmp, padded, before, made):
    b = c.acc.take()
    yield from c.project(("even", DT + k), b)
    s = tmp.take()
    a = c.act(s.buf[:, :], b.buf[:, :], ACT.Sigmoid, b.made, s.wait)
    b.free = [a]
    b = c.acc.take()
    yield from c.project(("even", k), b)
    u = padded.take()
    v = c.tt(u.buf[:, TAPS - 1:], b.buf[:, :], s.buf[:, :], ALU.mult, b.made, a, u.wait)
    b.free, s.free = [v], [v]
    y = ya[:, k, :]
    w = lambda j: c.vec("conv_w", k * TAPS + j)
    v = c.ts(y, u.buf[:, 0:T], w(0), ALU.mult, c.vec("conv_vec", k), ALU.add, v, before, c.vecs_in)
    for j in range(1, TAPS):
        v = c.stt(y, u.buf[:, j:j + T], w(j), y, ALU.mult, ALU.add)
        if j % 2:
            yield
    u.free = [v]
    made.append(v)


def conv_finish(c, ya, tmp, made, out):
    mean, var = c.work.take(), c.work.take()
    for k in range(DT):
        m = c.mm(mean.buf[:, :], c.ones[:, :], ya[:, k, :], k == 0, k == DT - 1, made[k], mean.wait,
                 c.consts_made, signal=True)
        yield
    for k in range(DT):
        s = tmp.take()
        v = c.stt(ya[:, k, :], mean.buf[:, :], -1.0 / D, ya[:, k, :], ALU.mult, ALU.add, m)
        a = c.act(s.buf[:, :], ya[:, k, :], ACT.Square, v, s.wait)
        n = c.mm(var.buf[:, :], c.ones[:, :], s.buf[:, :], k == 0, k == DT - 1, a, var.wait, signal=True)
        s.free = [n]
        yield
    mean.free = [v]
    inverse = tmp.take()
    inv = inverse.buf[:, :]
    a = c.act(inv, var.buf[:, :], ACT.Sqrt, n, inverse.wait, bias=c.ln_eps, scale=1.0 / D)
    var.free = [a]
    r = c.recip(inv, inv, a)
    for k in range(DT):
        b = c.acc.take()
        yield from c.project(("even", 2 * DT + k), b)
        g = tmp.take()
        y = ya[:, k, :]
        v = c.tt(y, y, inv, ALU.mult, r)
        gate = c.act(g.buf[:, :], b.buf[:, :], ACT.Silu, b.made, g.wait)
        b.free = [gate]
        a = c.act(y, y, ACT.Silu, v, scale=c.vec("conv_vec", DT + k), bias=c.vec("conv_vec", 2 * DT + k))
        v = c.tt(y, y, g.buf[:, :], ALU.mult, a, gate)
        g.free = [v]
        out.append(v)
    inverse.free = [v]


def even_mixers(c, ya, yb):
    with ExitStack() as scope:
        before = c.everyone()
        sb = lambda name, shape: c.sb(name, shape, scope=scope)
        chunk_start = sb("chunk_start", [P, T])
        mask_t = sb("mask_t", [P, 2, P])
        mask_n = sb("mask_n", [P, P])
        block16 = sb("block16", [P, P])
        merges = (16, 32, 64)
        below = {s: sb(f"below{s}", [P, P]) for s in merges}
        c.fill(chunk_start[:, :], 1.0, before)
        for j in range(0, T, CH):
            c.fill(chunk_start[:, j:j + 1], 0.0)
        c.fill(mask_t[:, :, :], 1.0)
        for j in range(2):
            c.select(mask_t[:, j, :], [[1, P]], j - 1, -1, ALU.is_ge, 0.0)
        c.fill(mask_n[:, :], 1.0)
        c.select(mask_n[:, :], [[-1, P]], -1, 1, ALU.is_ge, 0.0)
        c.fill(block16[:, :], 1.0)
        v16 = block16[:, :].rearrange("p (b i) -> p b i", i=16)
        c.select(v16, [[-16, P // 16], [0, 16]], 0, 1, ALU.is_ge, 0.0)
        c.select(v16, [[16, P // 16], [0, 16]], 15, -1, ALU.is_ge, 0.0)
        for s in merges:
            v = below[s][:, :].rearrange("p (b i) -> p b i", i=s)
            v4 = below[s][:, :].rearrange("p (b h i) -> p b h i", h=2, i=s)
            c.fill(below[s][:, :], 1.0)
            c.select(v4, [[-2 * s, P // (2 * s)], [0, 2], [0, s]], -s, 1, ALU.is_ge, 0.0)
            c.select(v4, [[2 * s, P // (2 * s)], [0, 2], [0, s]], 2 * s - 1, -1, ALU.is_ge, 0.0)
            for b in range(1, P // s, 2):
                c.fill(v[:, b, :], 0.0)
        masks = c.POOL.mark()

        keep = sb("one_minus_k_a", [P, DT])
        c.ts(keep[:, :], c.vec("rwkv_vec", 3 * DT, DT), -1.0, ALU.mult, 1.0, ALU.add, before, c.vecs_in)
        up = sb("lora_up", [P, D])
        up_in = c.dma(up[:, :], c.t["lora_up"], c.sem("lora_up_in"), before)
        shifted = c.ring("shifted", 3, [P, 1 + T], scope, before)
        for s in shifted.slots:
            s.free = [c.fill(s.buf[:, 0:1], 0.0, before)]
        tmp = c.ring("tmp", 4, [P, T], scope, before)

        class Pair:
            def __init__(self, i):
                self.AR = sb(f"AR{i}", [P, NCH, 2, CH])
                self.K, self.B, self.V, self.bonus = (
                    sb(f"{n}{i}", [P, NCH, CH]) for n in ("K", "B", "V", "bonus"))
                self.carry = sb(f"carry{i}", [P, NCH])
                self.free = before
        pairs = [Pair(0), Pair(1)]
        flat = lambda b: b[:, :, :].rearrange("p c t -> p (c t)")
        mids = sb("mids", [P, NCH])
        lora = sb("lora", [P, T])
        MM = [sb(f"MM{h}", [P, NCH, 4, CH]) for h in range(2)]
        NN = [sb(f"N{h}", [P, NCH, CH]) for h in range(2)]
        PT = [sb(f"PT{h}", [P, NCH, CH]) for h in range(2)]
        W = [[sb(f"W{h}{i}", [P, NCH, CH]) for i in range(4)] for h in range(2)]
        S = sb("S", [P, NCH, P])
        S_zero = c.fill(S[:, :, :], 0.0, before)

        def lerp(key, mu):
            bank = c.acc.take()
            yield from c.project(key, bank)
            z, d = shifted.take(), tmp.take()
            a = c.act(z.buf[:, 1:], bank.buf[:, :], ACT.Copy, bank.made, z.wait)
            bank.free = [a]
            p = c.ptt(d.buf[:, :], z.buf[:, 0:T], z.buf[:, 1:], ALU.subtract, a, d.wait)
            v = c.stt(z.buf[:, 1:], d.buf[:, :], mu, z.buf[:, 1:], ALU.mult, ALU.add, p)
            d.free = [v]
            lerp.out = z, v

        run(lerp(("even", 6 * DT), c.vec("mu_lora")))
        z, v = lerp.out
        a = c.act(lora[0:LORA, :], z.buf[0:LORA, 1:], ACT.Tanh, v, before)
        lora_made = c.act(lora[LORA:P, :], z.buf[LORA:P, 1:], ACT.Copy, v)
        z.free = [lora_made]

        def head_sum(x, *marks):
            b = c.work.take()
            b.made = c.mm(b.buf[:, :], c.head_ones[:, :], x, True, True, b.wait, c.consts_made, *marks, signal=True)
            return b

        def prepare(p, pair):
            free = pair.free
            vv = lambda i: c.vec("rwkv_vec", i * DT + p)
            at = slice(p * P, (p + 1) * P)
            b = c.work.take()
            m = c.mm(b.buf[:, :], up[0:LORA, at], lora[0:LORA, :], True, True, b.wait, up_in, lora_made, signal=True)
            sg, cum, ex = tmp.take(), tmp.take(), tmp.take()
            a = c.act(sg.buf[:, :], b.buf[:, :], ACT.Sigmoid, m, sg.wait, bias=vv(0))
            b.free = [a]
            v = c.scan(cum.buf[:, :], chunk_start[:, :], sg.buf[:, :], a, masks, cum.wait)
            c3 = cum.buf[:, :].rearrange("p (c t) -> p c t", t=CH)
            mid = c3[:, :, CH // 2 - 1:CH // 2]
            a = c.act(mids[:, :], mid.rearrange("p c o -> p (c o)"), ACT.Exp, v, scale=-DECAY)
            e3 = ex.buf[:, :].rearrange("p (c t) -> p c t", t=CH)
            v = c.tt(e3, c3, mid.to_broadcast([P, NCH, CH]), ALU.subtract, v, ex.wait)
            up_to = c.act(pair.AR[:, :, 1, :], e3, ACT.Exp, v, free, scale=-DECAY)
            w = c.tt(pair.carry[:, 0:NCH - 1], pair.AR[:, 0:NCH - 1, 1, CH - 1], mids[:, 1:], ALU.mult, up_to, free)
            over = c.act(pair.K[:, :, :], e3, ACT.Exp, v, free, scale=DECAY)
            p1 = c.ptt(ex.buf[:, :], ex.buf[:, :], sg.buf[:, :], ALU.subtract, over, up_to)
            before_t = c.act(pair.AR[:, :, 0, :], e3, ACT.Exp, p1, scale=-DECAY)
            for s in (sg, cum, ex):
                s.free = [before_t, c.DVE.mark()]
            b = c.work.take()
            m = c.mm(b.buf[:, :], up[LORA:P, at], lora[LORA:P, :], True, True, b.wait, signal=True)
            rate = tmp.take()
            a = c.act(rate.buf[:, :], b.buf[:, :], ACT.Sigmoid, m, rate.wait, bias=vv(1))
            b.free = [a]
            rate_made = a
            yield
            yield from lerp(("even", 4 * DT + p), c.vec("mu_rkv", DT + p))
            k, k_made = lerp.out
            kz = k.buf[:, 1:]
            kk, sq = tmp.take(), tmp.take()
            v = c.ts(kk.buf[:, :], kz, vv(2), ALU.mult, None, None, k_made, kk.wait)
            a = c.act(sq.buf[:, :], kk.buf[:, :], ACT.Square, v, sq.wait)
            b = head_sum(sq.buf[:, :], a)
            a = c.act(sq.buf[:, :], b.buf[:, :], ACT.Sqrt, b.made)
            b.free = [a]
            v = c.ts(sq.buf[:, :], sq.buf[:, :], 1e-12, ALU.max, None, None, a)
            v = c.recip(sq.buf[:, :], sq.buf[:, :])
            v = c.tt(kk.buf[:, :], kk.buf[:, :], sq.buf[:, :], ALU.mult)
            yield
            r3 = lambda s: s.buf[:, :].rearrange("p (c t) -> p c t", t=CH)
            v = c.stt(pair.AR[:, :, 0, :], r3(kk), -1.0, pair.AR[:, :, 0, :], ALU.mult, ALU.mult, before_t)
            v = c.tt(kk.buf[:, :], kk.buf[:, :], rate.buf[:, :], ALU.mult, rate_made)
            v = c.tt(pair.B[:, :, :], r3(kk), pair.K[:, :, :], ALU.mult, over, free)
            v = c.ts(rate.buf[:, :], rate.buf[:, :], vv(3), ALU.mult, keep[:, p:p + 1], ALU.add)
            v = c.tt(kz, kz, rate.buf[:, :], ALU.mult)
            k2 = v
            v = c.tt(flat(pair.K), kz, flat(pair.K), ALU.mult)
            for s in (kk, sq, rate):
                s.free = [v]
            yield from lerp(("even", 3 * DT + p), c.vec("mu_rkv", p))
            r, r_made = lerp.out
            rz = r.buf[:, 1:]
            r33 = rz.rearrange("p (c t) -> p c t", t=CH)
            v = c.tt(pair.AR[:, :, 1, :], r33, pair.AR[:, :, 1, :], ALU.mult, r_made, up_to)
            v = c.stt(rz, rz, c.vec("r_k", p), kz, ALU.mult, ALU.mult)
            k.free = [v]
            bonus = head_sum(rz, v)
            r.free = [bonus.made]
            yield from lerp(("even", 5 * DT + p), c.vec("mu_rkv", 2 * DT + p))
            z, v = lerp.out
            a = c.act(flat(pair.V), z.buf[:, 1:], ACT.Copy, v, free)
            v = c.tt(flat(pair.bonus), bonus.buf[:, :], z.buf[:, 1:], ALU.mult, bonus.made, free)
            z.free, bonus.free = [a, v], [v]
            pair.made = [v, a]

        gates = c.ring("rwkv_gate", 1, [P, T], scope, before)

        def gate(p):
            b = c.acc.take()
            yield from c.project(("even", 6 * DT + 1 + p), b)
            gate.out = g = gates.take()
            g.made = c.act(g.buf[:, :], b.buf[:, :], ACT.Silu, b.made, g.wait)
            b.free = [g.made]

        def four(lhsT, rhs, *marks):
            b = c.work.take()
            for j in range(NCH):
                m = c.mm(b.buf[:, j * CH:(j + 1) * CH], lhsT[:, j, :], rhs[:, j, :], True, True, b.wait, *marks,
                         signal=j == NCH - 1)
            b.made = m
            return b

        def three(b):
            return b.buf[:, :].rearrange("p (c t) -> p c t", t=CH)

        def every_chunk(mask):
            return mask[:, :].unsqueeze(1).to_broadcast([P, NCH, CH])

        def to_sbuf(dst, b, act):
            m = c.act(dst, three(b), ACT.Copy, b.made) if act else c.copy(dst, three(b), b.made)
            b.free = [m]
            return m

        def matrices(h, pair):
            hs = slice(h * RH, (h + 1) * RH)
            for j in range(NCH):
                b = c.work.take()
                ar = pair.AR[hs, j, :, :].rearrange("p a t -> p (a t)")
                c.mm(b.buf[:, 0:2 * CH], pair.K[hs, j, :], ar, True, True, b.wait, pair.made)
                m = c.mm(b.buf[:, 2 * CH:], pair.B[hs, j, :], ar, True, True, signal=True)
                v = c.tt(MM[h][:, j, :, :].rearrange("p (x a) t -> p x (a t)", a=2),
                         b.buf[:, :].rearrange("p (x a) -> p x a", x=2),
                         mask_t[:, :, :].rearrange("p a t -> p (a t)").unsqueeze(1).to_broadcast([P, 2, 2 * CH]),
                         ALU.mult, m, masks, before, solved)
                b.free = [v]
                yield
            b = c.work.take()
            for j in range(NCH):
                m = c.mm(b.buf[:, j * CH:(j + 1) * CH], pair.AR[hs, j, 0, :], pair.B[hs, j, :], True, True, b.wait,
                         signal=j == NCH - 1)
            v = c.tt(NN[h][:, :, :], three(b), every_chunk(mask_n), ALU.mult, m)
            b.free = [v]
            matrices.made[h] = v
            yield
        matrices.made = {}

        def add_to_inverse(h, b):
            v = c.tt(PT[h][:, :, :], three(b), PT[h][:, :, :], ALU.add, b.made)
            b.free = [v]
            return v

        def invert(h, pair):
            yield from matrices(h, pair)
            w = W[h]
            p1 = c.ptt(w[0][:, :, :], NN[h][:, :, :], every_chunk(block16), ALU.mult, matrices.made[h])
            p2 = c.tt(w[1][:, :, :], MM[h][:, :, 2, :], every_chunk(block16), ALU.mult)
            pt = c.tt(PT[h][:, :, :], w[1][:, :, :], every_chunk(c.ident), ALU.add, p2)
            b1, b2 = four(w[1], w[0], p1, p2), four(w[0], w[1], p1, p2)
            m1 = to_sbuf(w[2][:, :, :], b1, True)
            m2 = to_sbuf(w[3][:, :, :], b2, False)
            yield
            b1, b3, b2 = four(w[3], w[2], m1, m2), four(w[2], PT[h], m1, pt), four(w[2], w[3], m1, m2)
            m1 = to_sbuf(w[0][:, :, :], b1, True)
            pt = add_to_inverse(h, b3)
            m2 = to_sbuf(w[1][:, :, :], b2, False)
            yield
            b1, b2 = four(w[1], w[0], m1, m2), four(w[0], PT[h], m1, pt)
            m1 = to_sbuf(w[2][:, :, :], b1, True)
            pt = add_to_inverse(h, b2)
            yield
            pt = add_to_inverse(h, four(w[2], PT[h], m1, pt))
            yield
            for s in merges:
                b = c.work.take()
                for j in range(NCH):
                    m = c.tr(b.buf[:, j * CH:(j + 1) * CH], PT[h][:, j, :], pt, b.wait, signal=j == NCH - 1)
                b.made = m
                off = c.ptt(w[1][:, :, :], NN[h][:, :, :], every_chunk(below[s]), ALU.mult, c.PE.mark())
                p = to_sbuf(w[0][:, :, :], b, True)
                b = four(w[1], PT[h], off, pt)
                m = to_sbuf(w[2][:, :, :], b, False)
                yield
                pt = add_to_inverse(h, four(w[0], w[2], p, m))
                yield
            invert.made[h] = pt
        invert.made = {}

        def solve(p, pair):
            yield from in_turn(invert(0, pair), invert(1, pair))
            inv = [invert.made[0], invert.made[1]]
            A_t, V_t, K_t, B_t = W[0]
            Z, U0, PA, U = W[1]
            turned = []
            for i, (dst, src) in enumerate(((A_t, lambda j: pair.AR[:, j, 0, :]), (V_t, lambda j: pair.V[:, j, :]),
                                            (K_t, lambda j: pair.K[:, j, :]), (B_t, lambda j: pair.B[:, j, :]))):
                b = c.work.take()
                for j in range(NCH):
                    m = c.tr(b.buf[:, j * CH:(j + 1) * CH], src(j), b.wait, inv, pair.made, signal=j == NCH - 1)
                b.made = m
                turned.append(to_sbuf(dst[:, :, :], b, i % 2 == 0))
                yield
            heads = [(h, slice(h * RH, (h + 1) * RH)) for h in range(2)]
            b = c.work.take()
            for j in range(NCH):
                for h, hs in heads:
                    m = c.mm(three(b)[:, j, hs], MM[h][:, j, 0, :], V_t[:, j, hs], True, True, b.wait, turned,
                             signal=j == NCH - 1 and h == 1)
            b.made = m
            z = to_sbuf(Z[:, :, :], b, True)
            b = c.work.take()
            for j in range(NCH):
                for h, hs in heads:
                    m = c.mm(three(b)[hs, j, :], A_t[:, j, hs], PT[h][:, j, :], True, True, b.wait,
                             signal=j == NCH - 1 and h == 1)
            b.made = m
            pa = to_sbuf(PA[:, :, :], b, False)
            yield
            b = c.work.take()
            for j in range(NCH):
                for h, hs in heads:
                    m = c.mm(three(b)[:, j, hs], PT[h][:, j, :], Z[:, j, hs], True, True, b.wait, z,
                             signal=j == NCH - 1 and h == 1)
            b.made = m
            u0 = to_sbuf(U0[:, :, :], b, True)
            yield
            y = c.work.take()
            u, s_made = u0, S_zero
            for j in range(NCH):
                Uj = U0 if j == 0 else U
                if j:
                    b = c.work.take()
                    m = c.mm(b.buf[:, 0:P], PA[:, j, :], S[:, j, :], True, True, b.wait, pa, s_made, signal=True)
                    u = c.tt(U[:, j, :], b.buf[:, 0:P], U0[:, j, :], ALU.add, m, u0)
                    b.free = [u]
                if j < NCH - 1:
                    b = c.work.take()
                    w = pair.carry[:, j:j + 1]
                    m = c.mm(b.buf[:, 0:P], K_t[:, j, :], V_t[:, j, :], True, False, b.wait)
                    m = c.mm(b.buf[:, 0:P], B_t[:, j, :], Uj[:, j, :], False, True, u, signal=True)
                    for h, hs in heads:
                        if j == 0:
                            v = c.ts(S[hs, 1, hs], b.buf[hs, hs], w[hs], ALU.mult, None, None, m, S_free[0])
                        else:
                            v = c.tt(S[hs, j + 1, hs], b.buf[hs, hs], S[hs, j, hs], ALU.add, m, S_free[0])
                            v = c.ts(S[hs, j + 1, hs], S[hs, j + 1, hs], w[hs], ALU.mult, None, None, v)
                    b.free, s_next = [v], v
                if j:
                    c.mm(three(y)[:, j, :], S[:, j, :], pair.AR[:, j, 1, :], True, False, y.wait)
                for h, hs in heads:
                    c.mm(three(y)[hs, j, :], V_t[:, j, hs], MM[h][:, j, 1, :], j == 0, False, y.wait)
                    m = c.mm(three(y)[hs, j, :], Uj[:, j, hs], MM[h][:, j, 3, :], False, True, u, signal=True)
                s_made = s_next
                yield
            S_free[0] = m
            solved[:] = [m]
            t1, t2 = post.take(), post.take()
            a = c.act(t1.buf[:, :], y.buf[:, :], ACT.Copy, m, t1.wait)
            y.free = [a]
            b = head_sum(t1.buf[:, :], a)
            v = c.stt(t1.buf[:, :], b.buf[:, :], -1.0 / RH, t1.buf[:, :], ALU.mult, ALU.add, b.made)
            b.free = [v]
            a = c.act(t2.buf[:, :], t1.buf[:, :], ACT.Square, v, t2.wait)
            b = head_sum(t2.buf[:, :], a)
            a = c.act(t2.buf[:, :], b.buf[:, :], ACT.Sqrt, b.made, bias=c.gn_eps, scale=1.0 / RH)
            b.free = [a]
            v = c.recip(t2.buf[:, :], t2.buf[:, :], a)
            v = c.tt(t1.buf[:, :], t1.buf[:, :], t2.buf[:, :], ALU.mult)
            v = c.ts(t1.buf[:, :], t1.buf[:, :], c.vec("rwkv_vec", 4 * DT + p), ALU.mult,
                     c.vec("rwkv_vec", 5 * DT + p), ALU.add)
            v = c.tt(t1.buf[:, :], t1.buf[:, :], flat(pair.bonus), ALU.add)
            g = gate.out
            v = c.tt(yb[:, p, :], t1.buf[:, :], g.buf[:, :], ALU.mult, g.made, before)
            t1.free, t2.free, g.free = [v], [v], [v]
            pair.free = [m, v]
            made.append(v)

        post = c.ring("post", 2, [P, T], scope, before)
        made, solved, S_free = [], [], [S_zero]
        padded = c.ring("padded", 2, [P, TAPS - 1 + T], scope, before)
        for s in padded.slots:
            s.free = [c.fill(s.buf[:, 0:TAPS - 1], 0.0, before)]
        convolved, ya_made = [], []
        run(prepare(0, pairs[0]))
        run(convolve(c, 0, ya, tmp, padded, before, convolved))
        for p in range(DT):
            side = [gate(p)]
            if p + 1 < DT:
                side += [prepare(p + 1, pairs[(p + 1) % 2]), convolve(c, p + 1, ya, tmp, padded, before, convolved),
                         modulations(c, p)]
            else:
                side += [conv_finish(c, ya, tmp, convolved, ya_made)]
            run(blend(solve(p, pairs[p % 2]), chain(*side), SIDE_STEPS))
        run(modulations(c, DT - 1))
        return ya_made, made


def modulations(c, p):
    yield from c.modulation(0, [2 * DT + p])
    yield from c.modulation(1, range(3 * p, 3 * p + 3))


def rope_tables(c, scope, name, inv, sign, positions, angle, turns, before):
    out = []
    c.ts(angle[:, :], positions[:, :], inv, ALU.mult, None, None, before, c.vecs_in)
    for i, quarter in enumerate((0.25, 0.0)):
        r = c.sb(f"{'sin' if i else 'cos'}_{name}", [P, T], scope=scope)
        c.ts(turns[:, :], angle[:, :], float(0.5 / np.pi), ALU.mult, quarter, ALU.add)
        c.ts(turns[:, :], turns[:, :], ROUND, ALU.add, ROUND, ALU.subtract)
        c.stt(r[:, :], turns[:, :], -TWO_PI[0], angle[:, :], ALU.mult, ALU.add)
        for part in TWO_PI[1:]:
            c.stt(r[:, :], turns[:, :], -part, r[:, :], ALU.mult, ALU.add)
        if not i:
            c.ts(r[:, :], r[:, :], float(np.pi / 2), ALU.add, None, None)
        v = c.ts(r[:, :], r[:, :], 3.1415925, ALU.min, -3.1415925, ALU.max)
        a = c.act(r[:, :], r[:, :], ACT.Sin, v)
        out.append(r)
    made = c.ts(r[:, :], r[:, :], sign, ALU.mult, None, None, a, c.consts_made)
    return out[0], out[1], made


def odd_layer(c, x_marks):
    with ExitStack() as layer:
        before = c.everyone()
        sb = lambda name, shape, dt=F32: c.sb(name, shape, dt, scope=layer)
        Q = sb("q", [P, AH, T])
        keys = sb("keys", [P, T])
        values = sb("values", [P, TT, P])
        bias = sb("bias", [P, TT, T])
        tmp = c.ring("attn_tmp", 5, [P, T], layer, before)
        probs = c.ring("probs", SOFTMAX_LAG + 2, [P, T], layer, before)
        PT = c.ring("probs_t", 2, [P, TT, T], layer, before)
        small = sb("small", [P, 3 * AH * TT])
        with ExitStack() as index:
            isb = lambda name, shape, dt=F32: c.sb(name, shape, dt, scope=index)
            score = isb("score", [P, TT, T])
            pos_i, chunk_i = isb("pos_i", [P, T], I32), isb("chunk_i", [P, T], I32)
            pos_q, chunk_q = isb("pos_q", [P, TT], I32), isb("chunk_q", [P, TT], I32)
            pos, chunk_k, chunk_qf = isb("pos", [P, T]), isb("chunk_k", [P, T]), isb("chunk_qf", [P, TT])
            loaded = [c.dma(pos_i[:, :], c.t["pos"].to_broadcast([P, T]), c.sem("pos_in"), before),
                      c.dma(pos_q[:, :], c.t["pos_q"], c.sem("pos_q_in"), before)]
            c.copy(pos[:, :], pos_i[:, :], before, loaded)
            for dst, src, out in ((chunk_i, pos_i, chunk_k), (chunk_q, pos_q, chunk_qf)):
                c.DVE.do(lambda e, d=dst, s=src: e.tensor_scalar(d[:, :], s[:, :], 6, None, ALU.arith_shift_right))
                c.copy(out[:, :], dst[:, :])
            angle, turns = isb("angle", [P, T]), isb("turns", [P, T])
            cos128, sin128, rope128 = rope_tables(c, index, "128", c.vec("inv128"), c.sign128, pos, angle, turns, before)
            cos64, sin64, rope64 = rope_tables(c, index, "64", c.vec("inv64"), c.sign64, pos, angle, turns, before)
            for t in range(TT):
                adm = c.ts(bias[:, t, :], chunk_k[:, :], chunk_qf[:, t:t + 1], ALU.is_gt, NEG, ALU.mult)

            def rotate(key, half, cos, sin, rope_made, out, *marks):
                b = c.acc.take()
                yield from c.project(key, b)
                swapped, plain = tmp.take(), tmp.take()
                for r in range(0, P, half):
                    o = r ^ half
                    a = c.act(swapped.buf[r:r + half, :], b.buf[o:o + half, :], ACT.Copy, b.made, swapped.wait)
                p = c.ptt(swapped.buf[:, :], swapped.buf[:, :], sin[:, :], ALU.mult, a, rope_made)
                v = c.tt(plain.buf[:, :], b.buf[:, :], cos[:, :], ALU.mult, a, rope_made, plain.wait)
                b.free = [a, v]
                v = c.tt(out, plain.buf[:, :], swapped.buf[:, :], ALU.add, p, *marks)
                swapped.free, plain.free = [v], [v]
                rotate.made = v
                yield

            ki, qi, wi = isb("ki", [P, T]), isb("qi", [P, IH // 2, T]), isb("wi", [P, TT, IH])
            run(rotate(("ki", 0), 32, cos64, sin64, rope64, ki[:, :], before))
            b = c.acc.take()
            run(c.project_tokens(("wi", 0), b))
            wi_made = c.ts(wi[:, :, :], b.buf[:, 0:TT * IH].rearrange("p (t h) -> p t h", h=IH),
                           float(IH ** -0.5), ALU.mult, None, None, b.made)
            b.free = [wi_made]
            qi_made = []
            for i in range(IH // 2):
                run(rotate(("qi", i), 32, cos64, sin64, rope64, qi[:, i, :], before))
                qi_made.append(rotate.made)

            def scores():
                for t in range(TT):
                    for h in range(IH):
                        hs = slice(h % 2 * 64, h % 2 * 64 + 64)
                        b = c.work.take()
                        m = c.mm(b.buf[:, :], qi[hs, h // 2, t * P:(t + 1) * P], ki[hs, :], True, True, b.wait,
                                 qi_made[h // 2], signal=True)
                        s = probs.take()
                        a = c.act(s.buf[:, :], b.buf[:, :], ACT.Relu, m, s.wait, scale=0.125)
                        b.free = [a]
                        v = c.stt(score[:, t, :], s.buf[:, :], wi[:, t, h:h + 1],
                                  bias[:, t, :] if h == 0 else score[:, t, :], ALU.mult, ALU.add, a, wi_made, adm)
                        s.free = [v]
                        yield
                best = isb("best", [P, 8])
                for t in range(TT):
                    for _ in range(TOPK // 8):
                        c.DVE.do(lambda e, t=t: e.max(best[:, :], score[:, t, :]))
                        c.DVE.do(lambda e, t=t: e.match_replace(score[:, t, :], best[:, :], score[:, t, :], TAKEN))
                        yield
                    c.ts(score[:, t, :], score[:, t, :], -2e38, ALU.is_le, -NEG, ALU.mult)
                    scores.made = c.stt(bias[:, t, :], score[:, t, :], NEG, bias[:, t, :], ALU.add, ALU.add)
                    yield

            q_made = [None] * AH

            def main():
                yield from rotate(("k", 0), 64, cos128, sin128, rope128, keys[:, :], before)
                main.keys = rotate.made
                b = c.acc.take()
                yield from c.project_tokens(("v", 0), b)
                main.values = c.act(values[:, :, :], b.buf[:, :].rearrange("p (t d) -> p t d", d=P), ACT.Copy,
                                    b.made, before)
                b.free = [main.values]
                for h in range(AH):
                    yield from rotate(("q", h), 64, cos128, sin128, rope128, Q[:, h, :], before)
                    q_made[h] = rotate.made

            run(blend(main(), scores(), 0.7))
            c.dump("bias", bias[:, :, :])
            c.dump("q", Q[:, :, :])
        gates = c.ring("gate", 2, [P, T], layer, c.everyone())
        gate_of = {}

        def gates_in():
            for h in range(AH):
                b = c.acc.take()
                yield from c.project(("g", h), b)
                g = gate_of[h] = gates.take()
                g.made = c.act(g.buf[:, :], b.buf[:, :], ACT.Silu, b.made, g.wait)
                b.free = [g.made]
                yield

        out_made = []

        def front(i):
            h, t = divmod(i, TT)
            b = c.work.take()
            m = c.mm(b.buf[:, :], Q[:, h, t * P:(t + 1) * P], keys[:, :], True, True, b.wait, q_made[h],
                     main.keys, signal=True)
            return softmax_tile(c, b, m, bias[:, t, :], probs.take(), small, i, float(P ** -0.5), scores.made)

        def back(i, prob, state):
            h, t = divmod(i, TT)
            if t == 0:
                state.pt, state.marks = PT.take(), []
            state.marks.append(turn_tile(c, prob, TT, state.pt, t))

        def finish(h, pt, marks):
            o = c.work.take()
            for j in range(TT):
                m = c.mm(o.buf[:, :], values[:, j, :], pt.buf[:, j, :], j == 0, j == TT - 1, o.wait, marks,
                         main.values, signal=j == TT - 1)
            pt.free = [m]
            g = gate_of[h]
            v = c.tt(Q[:, h, :], o.buf[:, :], g.buf[:, :], ALU.mult, m, g.made)
            o.free, g.free = [v], [v]
            out_made.append(v)

        run(blend(pipeline(AH * TT, TT, front, back, finish), gates_in(), 2))
        c.dump("og", Q[:, :, :])
        return c.out_project("odd_out", [Q[:, h, :] for h in range(AH)], out_made, c.x, x_marks,
                             lambda k: c.mods[1][:, 2 * DT + k:2 * DT + k + 1], c.mod_made[1])


def pipeline(n, per_head, front, back, finish):
    class State:
        pt = marks = None
    probs, state, due = {}, State(), None
    for i in range(n + SOFTMAX_LAG + 1):
        if i < n:
            probs[i] = front(i)
        k = i - SOFTMAX_LAG
        if 0 <= k < n:
            back(k, probs.pop(k), state)
        if due is not None:
            finish(*due)
            due = None
        if 0 <= k < n and k % per_head == per_head - 1:
            due = (k // per_head, state.pt, state.marks)
        yield


def softmax_tile(c, bank, logits, bias, prob, small, i, scale, *marks):
    n = bias.shape[-1]
    mx, total, inv = (small[:, 3 * i + j:3 * i + j + 1] for j in range(3))
    p = prob.buf[:, 0:n]
    v = c.DVE.do(lambda e: e.tensor_tensor_reduce(p, bank.buf[:, 0:n], bias, 1.0, 3 * NEG, ALU.add, ALU.max, mx),
                 logits, prob.wait, *marks)
    bank.free = [v]
    v = c.ts(mx, mx, -scale, ALU.mult, None, None, v)
    a = c.act(p, p, ACT.Exp, v, bias=mx, scale=scale, accum_out=total)
    v = c.recip(inv, total, a)
    prob.made = c.ts(p, p, inv, ALU.mult, None, None, v)
    return prob


def turn_tile(c, prob, width, pt, t):
    b = c.work.take()
    for j in range(width):
        m = c.tr(b.buf[:, j * P:(j + 1) * P], prob.buf[:, j * P:(j + 1) * P], prob.made, b.wait,
                 signal=j == width - 1)
    prob.free = [m]
    dst = pt.buf[:, 0:width, t * P:(t + 1) * P]
    src = b.buf[:, 0:width * P].rearrange("p (j q) -> p j q", q=P)
    done = c.act(dst, src, ACT.Copy, m, pt.wait) if t % 2 else c.copy(dst, src, m, pt.wait)
    b.free = [done]
    return done


def softplus_of_minus(c, x, u, z, tmp, *marks):
    a = c.act(u, x, ACT.Abs, *marks)
    a = c.act(u, u, ACT.Exp, a, scale=-1.0)
    v = c.ts(z, u, 2.0, ALU.add, None, None, a)
    v = c.recip(z, z)
    v = c.tt(z, z, u, ALU.mult)
    v = c.tt(u, z, z, ALU.mult)
    v = c.ts(tmp, u, 2.0 / 19, ALU.mult, 2.0 / 17, ALU.add)
    for k in range(15, -1, -2):
        v = c.tt(tmp, tmp, u, ALU.mult)
        v = c.ts(tmp, tmp, 2.0 / k, ALU.add, None, None)
    v = c.tt(tmp, tmp, z, ALU.mult)
    v = c.ts(x, x, -1.0, ALU.mult, 0.0, ALU.max)
    return c.tt(x, x, tmp, ALU.add)


def lru_layer(c, x_marks):
    with ExitStack() as layer:
        before = c.everyone()
        sb = lambda name, shape: c.sb(name, shape, scope=layer)
        Y = sb("lru_y", [P, LT, T])
        with ExitStack() as scope:
            gates_w = c.sb("lru_gates_w", [P, 2, LRU], scope=scope)
            w_in = c.dma(gates_w[:, :, :], c.t["lru_gates"], c.sem("lru_gates_in"), before)
            padded = c.ring("lru_padded", 3, [P, LTAPS - 1 + T], scope, before)
            for s in padded.slots:
                s.free = [c.fill(s.buf[:, 0:LTAPS - 1], 0.0, before)]
            tmp = c.ring("lru_tmp", 12, [P, T], scope, before)
            rate = c.sb("lru_rate", [P, 2, LT], scope=scope)
            aux = c.sb("lru_aux", [P, 3, LT], scope=scope)
            v = c.copy(rate[:, 0, :], c.vec("lru_a", 0, LT), before, c.vecs_in)
            v = softplus_of_minus(c, rate[:, 0, :], aux[:, 0, :], aux[:, 1, :], aux[:, 2, :], v)
            c.ts(rate[:, 1, :], rate[:, 0, :], LRU_C, ALU.mult, None, None)
            rate_made = c.ts(rate[:, 0, :], rate[:, 0, :], -LRU_C, ALU.mult, None, None)
            made = []

            def block(n):
                b = c.acc.take()
                yield from c.project(("lru", n), b)
                xp = padded.take()
                a = c.act(xp.buf[:, LTAPS - 1:], b.buf[:, :], ACT.Copy, b.made, xp.wait)
                b.free = [a]
                xc = tmp.take()
                w = lambda j: c.vec("lru_conv_w", j * LT + n)
                v = c.ts(xc.buf[:, :], xp.buf[:, 0:T], w(0), ALU.mult, c.vec("lru_conv_b", n), ALU.add, a, xc.wait)
                for j in range(1, LTAPS):
                    v = c.stt(xc.buf[:, :], xp.buf[:, j:j + T], w(j), xc.buf[:, :], ALU.mult, ALU.add)
                xp.free = [v]
                b = c.acc.take()
                yield from c.project(("lru", LT + n), b)
                sg = tmp.take()
                silu = c.act(sg.buf[:, :], b.buf[:, :], ACT.Silu, b.made, sg.wait)
                b.free = [silu]
                block.out = xc, sg, silu, v

            def recurrence(n, xc, sg, silu, v):
                g = []
                for i in range(2):
                    b = c.work.take()
                    m = c.mm(b.buf[:, :], gates_w[:, i, n * P:(n + 1) * P], xc.buf[:, :], True, True, b.wait, v,
                             w_in, signal=True)
                    s = tmp.take()
                    s.made = c.act(s.buf[:, :], b.buf[:, :], ACT.Sigmoid, m, s.wait, c.vecs_in,
                                   bias=c.vec(("lru_ba", "lru_bx")[i], n))
                    b.free = [s.made]
                    g.append(s)
                    yield
                r, i = g
                decay, root = tmp.take(), tmp.take()
                a = c.act(decay.buf[:, :], r.buf[:, :], ACT.Exp, rate_made, decay.wait, scale=rate[:, 0, n:n + 1])
                th = c.act(r.buf[:, :], r.buf[:, :], ACT.Tanh, scale=rate[:, 1, n:n + 1])
                p = c.ptt(root.buf[:, :], decay.buf[:, :], decay.buf[:, :], ALU.mult, a, root.wait)
                ix = c.ptt(i.buf[:, :], i.buf[:, :], xc.buf[:, :], ALU.mult, i.made, v)
                v = c.stt(root.buf[:, :], root.buf[:, :], 1.0, r.buf[:, :], ALU.add, ALU.mult, p, th)
                a = c.act(root.buf[:, :], root.buf[:, :], ACT.Sqrt, v)
                v = c.tt(root.buf[:, :], root.buf[:, :], i.buf[:, :], ALU.mult, a, ix)
                v = c.scan(r.buf[:, :], decay.buf[:, :], root.buf[:, :])
                v = c.tt(Y[:, n, :], r.buf[:, :], sg.buf[:, :], ALU.mult, silu, before)
                for s in (xc, sg, r, i, decay, root):
                    s.free = [v]
                made.append(v)

            last = iter(())
            for n in range(LT):
                run(blend(block(n), last, 0.3))
                last = recurrence(n, *block.out)
            run(last)
        c.dump("lru_y", Y[:, 0:8, :])
        return c.out_project("lru_out", [Y[:, n, :] for n in range(LT)], made, c.x, x_marks)


def fox_layer(c, x_marks):
    with ExitStack() as layer:
        before = c.everyone()
        sb = lambda name, shape: c.sb(name, shape, scope=layer)
        G = sb("fox_gate", [P, DT, T])
        with ExitStack() as scope:
            sb = lambda name, shape: c.sb(name, shape, scope=scope)
            Q, K, V = sb("fox_q", [P, DT, T]), sb("fox_k", [P, DT, T]), sb("fox_v", [P, TT, D])
            probs = c.ring("fox_probs", SOFTMAX_LAG + 2, [P, T], scope, before)
            PT = c.ring("fox_probs_t", 2, [P, TT, T], scope, before)
            keybias = c.ring("fox_keybias", 2, [P, T], scope, before)
            small = sb("fox_small", [P, 3 * FH * TT])
            rows = sb("fox_rows", [FH, 4, T])
            pick = sb("fox_pick", [FH, FH, P])
            c.fill(pick[:, :, :], 0.0, before)
            picked = c.select(pick[:, :, :], [[-1, FH], [0, P]], 0, 1, ALU.not_equal, 1.0)
            b = c.acc.take()
            run(c.project(("fox_f", 0), b))
            f, u, z, tmp = (rows[:, i, :] for i in range(4))
            v = c.ts(f, b.buf[0:FH, :], c.vec("fox_b")[0:FH], ALU.add, None, None, b.made, before, c.vecs_in)
            b.free = [v]
            v = softplus_of_minus(c, f, u, z, tmp, v)
            c.DVE.do(lambda e: e.memset(u, 1.0))
            sums = c.scan(z, u, f)
            q_made, k_made, v_made, g_made = ([None] * DT for _ in range(4))

            def pair_in(p):
                for key, made, dst, func, kw in (("fox_q", q_made, Q, ACT.Copy, {"scale": 0.125}),
                                                 ("fox_k", k_made, K, ACT.Copy, {}),
                                                 ("fox_g", g_made, G, ACT.Silu, {})):
                    b = c.acc.take()
                    yield from c.project((key, p), b)
                    made[p] = c.act(dst[:, p, :], b.buf[:, :], func, b.made, before, **kw)
                    b.free = [made[p]]
                b = c.acc.take()
                yield from c.project_tokens(("fox_v", p), b)
                v_made[p] = c.copy(V[:, :, p * P:(p + 1) * P], b.buf[:, :].rearrange("p (t d) -> p t d", d=P),
                                   b.made, before)
                b.free = [v_made[p]]

            out_made = []

            def pairs_in():
                for p in range(DT):
                    yield from pair_in(p)
                    loaded.append(p)
            loaded, coming = [], pairs_in()
            keybias_of, o_of = {}, {}

            def front(i):
                h, t = divmod(i, TT)
                p, hs = h // 2, slice(h % 2 * 64, h % 2 * 64 + 64)
                while p not in loaded:
                    next(coming)
                if t == 0:
                    b = c.work.take()
                    m = c.mm(b.buf[:, :], pick[:, h, :], z, True, True, b.wait, picked, sums, signal=True)
                    kb = keybias_of[h] = keybias.take()
                    kb.made = c.act(kb.buf[:, :], b.buf[:, :], ACT.Copy, m, kb.wait)
                    b.free = [kb.made]
                kb = keybias_of[h]
                n = (t + 1) * P
                b = c.work.take()
                c.mm(b.buf[:, 0:n], Q[hs, p, t * P:n], K[hs, p, 0:n], True, False, b.wait, q_made[p], k_made[p])
                m = c.mm(b.buf[:, t * P:n], c.ident[:, :], c.causal[:, :], False, True, c.consts_made, signal=True)
                prob = softmax_tile(c, b, m, kb.buf[:, 0:n], probs.take(), small, i, 1.0, kb.made)
                if t == TT - 1:
                    kb.free = [prob.made]
                return prob

            def back(i, prob, state):
                t = i % TT
                if t == 0:
                    state.pt, state.marks = PT.take(), []
                state.marks.append(turn_tile(c, prob, t + 1, state.pt, t))

            def finish(h, pt, marks):
                p, hs = h // 2, slice(h % 2 * 64, h % 2 * 64 + 64)
                if h % 2 == 0:
                    o_of[p] = c.work.take()
                o = o_of[p]
                for j in range(TT):
                    m = c.mm(o.buf[hs, j * P:], V[:, j, p * P + hs.start:p * P + hs.stop], pt.buf[:, j, j * P:],
                             j == 0, j == TT - 1, o.wait, marks, v_made[p], signal=j == TT - 1)
                pt.free = [m]
                if h % 2:
                    v = c.tt(G[:, p, :], o.buf[:, :], G[:, p, :], ALU.mult, m, g_made[p])
                    o.free = [v]
                    out_made.append(v)

            run(blend(pipeline(FH * TT, TT, front, back, finish), coming, 4))
        return c.out_project("fox_out", [G[:, p, :] for p in range(DT)], out_made, c.x, x_marks)


def weight_plan(t):
    plan = []

    def add(key, name, *at, split=True):
        block = t[name]
        for i in at:
            block = block[i]
        width = P if block.shape[1] % P == 0 else block.shape[1] // DT
        plan.append((key, block, block.shape[1] // width, width, split))

    def ada(l, js):
        for j in js:
            add(("ada", l, j), "ada", l * 3 * DT + j, split=False)

    def out(name):
        for cb in range(DT):
            for half in range(2):
                add((name, cb, half), name, 2 * cb + half)

    def even(*js):
        for j in js:
            add(("even", j), "even_in", j)

    ada(0, range(2 * DT))
    even(6 * DT, 4 * DT, 3 * DT, 5 * DT, DT, 0)
    for p in range(DT):
        even(6 * DT + 1 + p)
        if p + 1 < DT:
            even(4 * DT + p + 1, 3 * DT + p + 1, 5 * DT + p + 1, DT + p + 1, p + 1)
        else:
            even(*range(2 * DT, 3 * DT))
        ada(0, [2 * DT + p])
        ada(1, range(3 * p, 3 * p + 3))
    out("even_out")
    add(("ki", 0), "odd_in", 2 * AH + 2 + IH // 2)
    add(("wi", 0), "odd_wi", 0)
    for i in range(IH // 2):
        add(("qi", i), "odd_in", AH + 2 + i)
    add(("k", 0), "odd_in", AH)
    add(("v", 0), "odd_in", AH + 1)
    for h in range(AH):
        add(("q", h), "odd_in", h)
    for h in range(AH):
        add(("g", h), "odd_in", AH + 2 + IH // 2 + h)
    out("odd_out")
    for n in range(LT):
        add(("lru", n), "lru_in", n)
        add(("lru", LT + n), "lru_in", LT + n)
    out("lru_out")
    add(("fox_f", 0), "fox_in", 4 * DT)
    for p in range(DT):
        for key, j in (("fox_q", 0), ("fox_k", 1), ("fox_g", 3), ("fox_v", 2)):
            add((key, p), "fox_in", j * DT + p)
    out("fox_out")
    return plan


def build(nc, t, debug=(), layers=4):
    with ExitStack() as ctx:
        c = Core(nc, t, ctx, debug)
        x = c.x
        marks = [c.dma(x[:, k, :], t["x_t"][k * P:(k + 1) * P, :], c.sem(f"x_in{k}")) for k in range(DT)]
        with ExitStack() as scope:
            sq = c.ring("sq", 2, [P, T], scope, ())
            for k in range(DT):
                summed = c.square_sum(x[:, k, :], k, marks[k], sq)
        run(c.modulation(0, range(2 * DT)))
        c.norm_into_h(x, marks, summed, lambda k: c.gains[0][:, k:k + 1], lambda k: c.mods[0][:, k:k + 1],
                      c.mod_made[0])
        c.dump("h_hi", c.h_hi[:, :, :].bitcast(F32))
        marks, summed = even_layer(c)
        c.dump("x0", x[:, :, :])
        if layers > 1:
            c.norm_into_h(x, marks, summed, lambda k: c.gains[1][:, k:k + 1], lambda k: c.mods[1][:, k:k + 1],
                          c.mod_made[1])
            marks, summed = odd_layer(c, marks)
            c.dump("x1", x[:, :, :])
        if layers > 2:
            with ExitStack() as scope:
                before = c.everyone()
                rms = c.sb("rms", [P, T], scope=scope)
                sq = c.ring("sq", 2, [P, T], scope, before)
                inverse = c.inverse_rms(rms[:, :], summed, before)
                for k in range(DT):
                    v = c.tt(x[:, k, :], x[:, k, :], rms[:, :], ALU.mult, marks[k], inverse)
                    marks[k] = c.ts(x[:, k, :], x[:, k, :], c.vec("final_g", k), ALU.mult, None, None, v)
                    summed = c.square_sum(x[:, k, :], k, marks[k], sq)
            c.norm_into_h(x, marks, summed, lambda k: c.vec("norm2_g0", k), None)
            marks, summed = lru_layer(c, marks)
            c.dump("x2", x[:, :, :])
        if layers > 3:
            c.norm_into_h(x, marks, summed, lambda k: c.vec("norm2_g1", k), None)
            marks, summed = fox_layer(c, marks)
            c.dump("x3", x[:, :, :])
        with ExitStack() as scope:
            before = c.everyone()
            rms = c.sb("rms", [P, T], scope=scope)
            inverse = c.inverse_rms(rms[:, :], summed, before)
            for k in range(DT):
                v = c.tt(x[:, k, :], x[:, k, :], rms[:, :], ALU.mult, marks[k], inverse)
                v = c.ts(x[:, k, :], x[:, k, :], c.vec("final2_g", k), ALU.mult, None, None, v)
                c.stores.append(c.dma(t["out"][k * P:(k + 1) * P, :], x[:, k, :], c.sem(f"out{k}"), v))

        with nc.Block() as block:
            @block.sync
            def _(e):
                for issue in c.SP.queue:
                    issue(e)
                for semaphore, value in c.stores:
                    e.wait_ge(semaphore, value)

            @block.tensor
            def _(e):
                for issue in c.PE.queue:
                    issue(e)

            @block.vector
            def _(e):
                for issue in c.DVE.queue:
                    issue(e)

            @block.scalar
            def _(e):
                for issue in c.ACTE.queue:
                    issue(e)

            @block.gpsimd
            def _(e):
                for issue in c.POOL.queue:
                    issue(e)


def blocks(w, width=P):
    k, n = w.shape
    return np.ascontiguousarray(w.reshape(k // P, P, n // width, width).transpose(2, 1, 0, 3)).reshape(
        n // width, P, (k // P) * width)


def half_blocks(w):
    k, n = w.shape
    return np.ascontiguousarray(w.reshape(2, k // (2 * P), P, n // P, P).transpose(3, 0, 2, 1, 4)).reshape(
        2 * n // P, P, k // 2)


def columns(v):
    v = v.reshape(-1, v.shape[-1] // P, P)
    return v.transpose(2, 0, 1).reshape(P, -1)


def kernel(debug=(), layers=4, **inputs):
    import concourse.bacc as bacc
    from concourse.bass_utils import run_bass_kernel_spmd

    a = {k: np.asarray(v) for k, v in inputs.items()}
    inverse = lambda d: (10000.0 ** (-np.arange(0, d, 2) / d)).astype(np.float32)
    conv = a["conv_w"][0, :, 0, :].reshape(TAPS, DT, P).transpose(2, 1, 0).reshape(P, DT * TAPS)
    fox_b = np.zeros((P, 1), np.float32)
    fox_b[:FH, 0] = a["fox_b_f_2"][0]
    vecs = [columns(a["c"]), columns(a["ada_b"][0]), columns(a["ada_b"][1]), columns(a["norm_g"][0]),
            columns(a["norm_g"][1]), columns(a["final_g"]), conv, columns(a["conv_vec"][0]),
            columns(a["rwkv_mu_rkv"][0]), a["rwkv_mu_lora"][0].reshape(P, 1), columns(a["rwkv_vec"][0]),
            columns(a["rwkv_r_k"][0].reshape(-1)), np.tile(inverse(128), 2).reshape(P, 1),
            np.tile(inverse(64), 4).reshape(P, 1), columns(a["norm_g_2"][0]), columns(a["norm_g_2"][1]),
            columns(a["final_g_2"]), columns(a["lru_conv_w_2"][0]), columns(a["lru_conv_b_2"][0]),
            columns(a["lru_ba_2"][0]), columns(a["lru_bx_2"][0]), columns(a["lru_a_param_2"][0]), fox_b]
    odd = a["odd_w_in"][0]
    w, at = {}, 0
    for name, n in (("q", AH * P), ("k", P), ("v", P), ("qi", IH * 64), ("ki", 64), ("wi", IH), ("g", AH * P)):
        w[name] = odd[:, at:at + n]
        at += n
    pos = a["positions"].reshape(1, T)
    fox = a["fox_w_in_2"][0]
    arrays = {
        "x_t": np.ascontiguousarray(a["x"][0].T),
        "vecs": np.ascontiguousarray(np.concatenate(vecs, axis=1)),
        "ada": np.concatenate([blocks(a["ada_w"][l]) for l in range(2)]),
        "even_in": blocks(a["even_w_in"][0]),
        "even_out": half_blocks(a["even_w_out"][0]),
        "lora_up": np.ascontiguousarray(np.concatenate([a["rwkv_w_up"][0], a["rwkv_a_up"][0]])),
        "odd_in": blocks(np.concatenate([w["q"], w["k"], w["v"], w["qi"], w["g"], w["ki"], w["ki"]], axis=1)),
        "odd_wi": blocks(w["wi"], IH),
        "odd_out": half_blocks(a["odd_w_out"][0]),
        "pos": np.ascontiguousarray(pos),
        "pos_q": np.ascontiguousarray(pos.reshape(TT, P).T),
        "lru_in": blocks(a["lru_w_in_2"][0]),
        "lru_gates": np.ascontiguousarray(np.stack(
            [a[n][0].transpose(1, 0, 2).reshape(P, LRU) for n in ("lru_wa_2", "lru_wx_2")], axis=1)),
        "lru_out": half_blocks(a["lru_w_out_2"][0]),
        "fox_in": blocks(np.concatenate([fox, np.zeros((D, P - FH), np.float32)], axis=1)),
        "fox_out": half_blocks(a["fox_w_out_2"][0]),
    }
    nc = bacc.Bacc("TRN2", target_bir_lowering=False, num_devices=1)
    t = {k: nc.dram_tensor(k, list(v.shape), I32 if v.dtype.kind == "i" else F32, kind="ExternalInput").ap()
         for k, v in arrays.items()}
    t["out"] = nc.dram_tensor("out", [D, T], F32, kind="ExternalOutput").ap()
    sizes = {"ya": DT, "yb": DT, "x0": DT, "h_hi": DT, "x1": DT, "x2": DT, "x3": DT, "q": AH, "og": AH,
             "bias": TT, "lru_y": 8}
    for name in debug:
        t["dbg_" + name] = nc.dram_tensor("dbg_" + name, [P, sizes[name], T], F32, kind="ExternalOutput").ap()
    build(nc, t, debug, layers)
    result = run_bass_kernel_spmd(nc, [arrays], core_ids=[0])
    return np.ascontiguousarray(result.results[0]["out"].T).reshape(1, T, D)
```

```python
from contextlib import ExitStack

import numpy as np

from concourse import mybir

ALU = mybir.AluOpType
ACT = mybir.ActivationFunctionType
F32 = mybir.dt.float32
F32R = mybir.dt.float32r
I32 = mybir.dt.int32

P = 128
T = 512
D = 1024
DT = D // P
TT = T // P
TAPS = 31
RH = 64
LORA = 64
CH = P
NCH = T // CH
DECAY = float(np.exp(-0.5))
AH = 16
IH = 8
MERGES = (16, 32, 64)
TOPK = min(256, T // 4)
LRU = 1536
LT = LRU // P
LTAPS = 4
LRU_C = 8.0
FH = 16
NEG = -1e30
TAKEN = -3e38
ROUND = 1.5 * 2.0 ** 23
NRAW, NSPLIT = 3, 2
SOLVE_STEPS, PREPARE_STEPS, FINISH_STEPS, TAP_DELAY = 51, 94, 64, 22
SOFTMAX_LAG = 3
TWO_PI = (6.28125, 0.0019350051879882812, 3.019916050561733e-07)


def vector_columns():
    names = [("ada_b0", 3 * DT), ("ada_b1", 3 * DT), ("norm_g0", DT), ("norm_g1", DT),
             ("final_g", DT), ("conv_w", DT * TAPS), ("conv_vec", 3 * DT), ("mu_rkv", 3 * DT),
             ("mu_lora", 1), ("rwkv_vec", 6 * DT), ("r_k", DT), ("inv128", 1), ("inv64", 1),
             ("norm2_g0", DT), ("norm2_g1", DT), ("final2_g", DT), ("lru_conv_w", LT * LTAPS),
             ("lru_conv_b", LT), ("lru_bias", 2 * LT), ("lru_a", LT), ("fox_b", 1)]
    at, out = 0, {}
    for name, n in names:
        out[name] = (at, n)
        at += n
    return out, at


class Lane:

    def __init__(self, sem, chained=True):
        self.sem, self.chained, self.count, self.queue, self.waited = sem, chained, 0, [], {}

    def wait(self, *marks):
        for m in marks:
            if isinstance(m, list):
                self.wait(*m)
            elif m is not None and self.waited.get(m[0].name, 0) < m[1]:
                self.waited[m[0].name] = m[1]
                self.queue.append(lambda e, m=m: e.wait_ge(m[0], m[1]))

    def do(self, issue, *marks, signal=True, chained=True):
        if self.chained and chained and self.count:
            self.wait((self.sem, self.count))
        self.wait(*marks)
        if not signal:
            self.queue.append(issue)
            return None
        self.count += 1
        self.queue.append(lambda e: issue(e).then_inc(self.sem, 1))
        return (self.sem, self.count)

    def mark(self):
        return (self.sem, self.count) if self.count else None


class Slot:

    def __init__(self, buf, free=()):
        self.buf, self.free, self.wait = buf, list(free), None

    def hold(self):
        assert self.free is not None
        self.wait, self.free = self.free, None
        return self


class Ring:

    def __init__(self, slots):
        self.slots, self.at = slots, 0

    def take(self):
        for _ in self.slots:
            s = self.slots[self.at % len(self.slots)]
            self.at += 1
            if s.free is not None:
                return s.hold()
        raise AssertionError("every buffer of the ring is held")


def blend(main, side, steps):
    due = 0.0
    for _ in main:
        due += steps
        while due >= 1:
            due -= 1
            next(side, None)
        yield
    yield from side


def in_turn(*stages):
    stages = list(stages)
    while stages:
        for g in list(stages):
            try:
                next(g)
            except StopIteration:
                stages.remove(g)
            yield


def weave(*parts):
    parts = [[0.0, 1.0 / steps, stage] for stage, steps in parts]
    while parts:
        part = min(parts, key=lambda x: x[0])
        part[0] += part[1]
        try:
            next(part[2])
        except StopIteration:
            parts.remove(part)
            continue
        yield


def idle(steps):
    for _ in range(steps):
        yield


def chain(*stages):
    for g in stages:
        yield from g


class Core:

    def __init__(self, nc, t, ctx, debug):
        self.nc, self.t, self.ctx, self.debug, self.names = nc, t, ctx, debug or (), 0
        self.PE = Lane(self.sem("pe_done"), chained=False)
        self.DVE = Lane(self.sem("dve_done"))
        self.ACTE = Lane(self.sem("act_done"))
        self.POOL = Lane(self.sem("pool_done"))
        self.SP = Lane(None, chained=False)
        self.dma_total, self.stores, self.mod_made = {}, [], {}

        banks = [ctx.enter_context(nc.psum_tensor(f"bank{i}", [P, T], F32)) for i in range(8)]
        self.acc = Ring([Slot(b) for b in banks[0:2]])
        self.work = Ring([Slot(b) for b in banks[2:7]])
        self.stat = Slot(banks[7])

        self.cols, n_cols = vector_columns()
        self.vecs = self.sb("vecs", [P, n_cols])
        self.ident = self.sb("ident", [P, P])
        self.ones = self.sb("ones", [P, P])
        self.head_ones = self.sb("head_ones", [P, P])
        self.causal = self.sb("causal", [P, P])
        self.few = self.sb("few", [P, 5])
        self.rms_eps, self.ln_eps, self.gn_eps, self.sign128, self.sign64 = (
            self.few[:, i:i + 1] for i in range(5))
        self.mods = [self.sb(f"mod{l}", [P, 3 * DT]) for l in range(2)]
        self.gains = [self.sb(f"gain{l}", [P, DT]) for l in range(2)]
        self.rms = self.sb("rms", [P, 3, TT])
        self.squares, self.squares_free = self.sb("squares", [P, 2, T]), [[], []]
        self.rms_free = []
        self.silu_c = self.sb("silu_c", [P, D])
        self.h_hi = self.sb("h_hi", [P, DT, T], F32R)
        self.h_lo = self.sb("h_lo", [P, DT, T], F32R)
        self.H = [(self.h_hi[:, k, :], self.h_lo[:, k, :]) for k in range(DT)]
        self.h_marks = [None] * DT
        self.x = self.sb("x", [P, DT, T])

        self.raw = [Slot(self.sb(f"raw{i}", [P, DT * P])) for i in range(NRAW)]
        self.raw_sems = [self.sem(f"raw{i}_in") for i in range(NRAW)]
        self.split = [Slot((self.sb(f"w_hi{i}", [P, DT * P], F32R), self.sb(f"w_lo{i}", [P, DT * P], F32R)))
                      for i in range(NSPLIT)]
        self.plan, self.ready = weight_plan(t), {}
        self.fetched = self.prepared = self.taken = self.splits = 0
        self.constants()

    def sem(self, name):
        return self.ctx.enter_context(self.nc.semaphore(name))

    def sb(self, name, shape, dt=F32, scope=None):
        self.names += 1
        return (scope or self.ctx).enter_context(self.nc.sbuf_tensor(f"{name}_{self.names}", shape, dt))

    def ring(self, name, n, shape, scope, free):
        return Ring([Slot(self.sb(f"{name}{i}", shape, scope=scope), free) for i in range(n)])

    def dma(self, out, in_, semaphore, *marks):
        self.SP.wait(*marks)
        self.SP.queue.append(lambda e: e.dma_start(out, in_).then_inc(semaphore, 16))
        self.dma_total[semaphore.name] = self.dma_total.get(semaphore.name, 0) + 16
        return (semaphore, self.dma_total[semaphore.name])

    def everyone(self):
        return [x.mark() for x in (self.PE, self.DVE, self.ACTE, self.POOL)]

    def vec(self, name, i=0, n=1):
        at, count = self.cols[name]
        assert i + n <= count
        return self.vecs[:, at + i:at + i + n]

    def dump(self, name, ap):
        if name in self.debug:
            self.stores.append(self.dma(self.t["dbg_" + name], ap, self.sem(f"dump_{name}"), self.everyone()))
            for lane in (self.PE, self.DVE, self.ACTE, self.POOL):
                lane.wait(self.stores[-1])

    def act(self, out, in_, func, *marks, **kw):
        return self.ACTE.do(lambda e: e.activation(out, in_, func, **kw), *marks)

    def tt(self, out, a, b, op, *marks):
        return self.DVE.do(lambda e: e.tensor_tensor(out, a, b, op), *marks)

    def ts(self, out, a, s1, op0, s2, op1, *marks):
        if op1 is None:
            return self.DVE.do(lambda e: e.tensor_scalar(out, a, s1, None, op0), *marks)
        return self.DVE.do(lambda e: e.tensor_scalar(out, a, s1, s2, op0, op1), *marks)

    def stt(self, out, a, s, b, op0, op1, *marks):
        return self.DVE.do(lambda e: e.scalar_tensor_tensor(out, a, s, b, op0, op1), *marks)

    def silu_twice(self, out, in_, *marks):
        a = self.act(out, in_, ACT.Tanh, *marks, scale=0.5)
        return self.stt(out, out, 1.0, in_, ALU.add, ALU.mult, a)

    def copy(self, out, a, *marks):
        return self.DVE.do(lambda e: e.tensor_copy(out, a), *marks)

    def recip(self, out, a, *marks):
        return self.DVE.do(lambda e: e.reciprocal(out, a), *marks)

    def scan(self, out, a, b, *marks):
        return self.DVE.do(lambda e: e.tensor_tensor_scan(out, a, b, 0.0, ALU.mult, ALU.add), *marks)

    def ptt(self, out, a, b, op, *marks):
        return self.POOL.do(lambda e: e.tensor_tensor(out, a, b, op), *marks)

    def fill(self, ap, value, *marks):
        return self.POOL.do(lambda e: e.memset(ap, value), *marks)

    def select(self, ap, pattern, base, cm, op, value, *marks):
        return self.POOL.do(lambda e: e.affine_select(out=ap, in_=ap, pattern=pattern, compare_op=op, fill=value,
                                                      base=base, channel_multiplier=cm), *marks)

    def mm(self, out, lhsT, rhs, start, stop, *marks, signal=False):
        return self.PE.do(lambda e: e.matmul(out, lhsT, rhs, start=start, stop=stop, skip_group_check=True),
                          *marks, signal=signal)

    def tr(self, out, in_, *marks, signal=False):
        k = in_.shape[0]
        return self.PE.do(lambda e: e.transpose(out, in_, self.ident[0:k, 0:k]), self.consts_made, *marks,
                          signal=signal)

    def fetch(self):
        while self.fetched < len(self.plan):
            n = self.fetched
            raw = self.raw[n % NRAW]
            if raw.free is None:
                return
            _, src, kt, width, _ = self.plan[n]
            raw.hold()
            raw.landed = self.dma(raw.buf[:, 0:kt * width], src, self.raw_sems[n % NRAW], raw.wait)
            self.fetched += 1

    def split_next(self):
        n = self.prepared
        _, src, kt, width, split = self.plan[n]
        self.prepared += 1
        size = kt * width
        raw = self.raw[n % NRAW]
        if not split:
            self.ready[n] = (raw, raw.buf, None, raw.landed)
            return
        s = self.split[self.splits % NSPLIT].hold()
        self.splits += 1
        hi, lo = s.buf
        made = []
        for half in (slice(0, size // 2), slice(size // 2, size)):
            rounded = self.act(hi[:, half], raw.buf[:, half], ACT.Copy, raw.landed, s.wait)
            rest = self.ptt(lo[:, half], raw.buf[:, half], hi[:, half].bitcast(F32), ALU.subtract,
                            raw.landed, rounded, s.wait)
            made.append([rounded, rest])
        raw.free = made[1]
        self.ready[n] = (s, hi, lo, made)

    def weights(self, key):
        n = self.taken
        assert self.plan[n][0] == key, (self.plan[n][0], key)
        self.taken += 1
        self.fetch()
        while n not in self.ready:
            self.split_next()
        return self.ready.pop(n) + self.plan[n][2:4]

    def look_ahead(self):
        self.fetch()
        while self.prepared < self.fetched and (
                not self.plan[self.prepared][4] or self.split[self.splits % NSPLIT].free is not None):
            split = self.plan[self.prepared][4]
            self.split_next()
            if split:
                self.fetch()
                return

    def project(self, key, bank, x=None, x_marks=None, start=True, stop=True):
        x, x_marks = x or self.H, x_marks or self.h_marks
        slot, hi, lo, landed, kt, width = self.weights(key)
        out = bank.buf[0:width, :]
        for k in range(kt):
            w = slice(k * width, (k + 1) * width)
            last = k == kt - 1
            self.mm(out, hi[:, w], x[k][0], start and k == 0, False, landed[2 * k // kt], bank.wait, x_marks[k])
            self.mm(out, hi[:, w], x[k][1], False, False)
            m = self.mm(out, lo[:, w], x[k][0], False, stop and last, signal=last)
            if k == 2:
                self.look_ahead()
            if not last:
                yield
        slot.free = [m]
        bank.made = m

    def project_tokens(self, key, bank):
        slot, hi, lo, landed, kt, width = self.weights(key)
        for tt in range(TT):
            out = bank.buf[:, tt * width:(tt + 1) * width]
            at = slice(tt * P, (tt + 1) * P)
            for k in range(kt):
                w = slice(k * width, (k + 1) * width)
                self.mm(out, self.H[k][0][:, at], hi[:, w], k == 0, False, landed[2 * k // kt], bank.wait,
                        self.h_marks[k])
                self.mm(out, self.H[k][1][:, at], hi[:, w], False, False)
                m = self.mm(out, self.H[k][0][:, at], lo[:, w], False, k == kt - 1, signal=k == kt - 1)
                if k == kt // 2:
                    yield
            if tt == 0:
                self.look_ahead()
            yield
        slot.free = [m]
        bank.made = m

    def constants(self):
        self.vecs_in = self.dma(self.vecs[:, :], self.t["vecs"], self.sem("vecs_in"))
        self.fill(self.ident[:, :], 0.0)
        self.select(self.ident[:, :], [[-1, P]], 0, 1, ALU.not_equal, 1.0)
        self.fill(self.ones[:, :], 1.0)
        self.fill(self.head_ones[:, :], 0.0)
        for h in range(2):
            self.fill(self.head_ones[h * RH:(h + 1) * RH, h * RH:(h + 1) * RH], 1.0)
        self.fill(self.causal[:, :], 0.0)
        self.select(self.causal[:, :], [[-1, P]], 0, 1, ALU.is_ge, NEG)
        for ap, value in ((self.rms_eps, 1e-6), (self.ln_eps, 1e-5), (self.gn_eps, 64e-5)):
            self.fill(ap, value)
        for p0, s128, s64 in ((0, -1.0, -1.0), (32, -1.0, 1.0), (64, 1.0, -1.0), (96, 1.0, 1.0)):
            self.fill(self.few[p0:p0 + 32, 3:4], s128)
            self.fill(self.few[p0:p0 + 32, 4:5], s64)
        self.consts_made = self.POOL.mark()
        self.gain_product = self.sb("gain_product", [P, DT])
        self.tt(self.gain_product[:, :], self.vec("final_g", 0, DT), self.vec("norm2_g0", 0, DT), ALU.mult,
                self.vecs_in)
        self.half_bias = self.sb("half_bias", [P, 2 * DT + 2 * LT])
        self.ts(self.half_bias[:, 0:2 * DT], self.vec("rwkv_vec", 0, 2 * DT), 0.5, ALU.mult, None, None, self.vecs_in)
        self.half_bias_made = self.ts(self.half_bias[:, 2 * DT:], self.vec("lru_bias", 0, 2 * LT), 0.5, ALU.mult,
                                      None, None)
        c_in = self.dma(self.silu_c[:, :], self.t["c"].to_broadcast([P, D]), self.sem("c_in"))
        self.silu_c_made = self.act(self.silu_c[:, :], self.silu_c[:, :], ACT.Silu, c_in)

    def modulation(self, l, js):
        for j in js:
            slot, w, _, landed, _, _ = self.weights(("ada", l, j))
            slot.free = [self.modulation_block(l, j, w[:, :], landed)]
            self.look_ahead()
            yield

    def modulation_block(self, l, j, w, landed):
        col = self.mods[l][:, j:j + 1]
        used = self.DVE.do(lambda e: e.tensor_tensor_reduce(w, w, self.silu_c[:, :], 1.0, 0.0, ALU.mult, ALU.add,
                                                            col), landed, self.silu_c_made)
        made = self.tt(col, col, self.vec(f"ada_b{l}", j), ALU.add, self.vecs_in)
        if DT <= j < 2 * DT:
            i = j - DT
            made = self.stt(self.gains[l][:, i:i + 1], col, 1.0, self.vec(f"norm_g{l}", i), ALU.add, ALU.mult)
        self.mod_made[l] = made
        return used

    def square_sum(self, x, i, x_mark, sq, gain=None, which=0):
        total = self.squares[:, which, :]
        kw = {} if gain is None else {"scale": gain(i)}
        if i == 0:
            return self.act(total, x, ACT.Square, x_mark, self.squares_free[which], self.vecs_in, **kw)
        s = sq.take()
        a = self.act(s.buf[:, :], x, ACT.Square, x_mark, s.wait, **kw)
        v = self.tt(total, total, s.buf[:, :], ALU.add, a)
        s.free = [v]
        if i < DT - 1:
            return v
        for j in range(TT):
            at = which * TT + j
            m = self.mm(self.stat.buf[:, at:at + 1], self.squares[:, which, j * P:(j + 1) * P], self.ones[:, 0:1],
                        at == 0, True, v, self.consts_made, self.stat.free, signal=j == TT - 1)
        self.squares_free[which] = [m]
        return m

    def inverse_rms(self, summed, scaled=False):
        one, two, root = (self.rms[:, i, :] for i in range(3))
        a = self.act(one, self.stat.buf[:, 0:TT], ACT.Sqrt, summed, self.rms_free, self.consts_made,
                     bias=self.rms_eps, scale=1.0 / D)
        r = self.recip(one, one, a)
        self.stat.free = [a]
        banks = [self.work.take()]
        banks[0].made = self.spread(banks[0], lambda j: one[:, j:j + 1].to_broadcast([P, P]), r)
        if scaled:
            v = self.tt(root, self.stat.buf[:, TT:2 * TT], one, ALU.mult, summed)
            self.stat.free = [v]
            v = self.tt(root, root, one, ALU.mult)
            a = self.act(root, root, ACT.Sqrt, v, bias=self.rms_eps, scale=1.0 / D)
            v = self.recip(root, root, a)
            r = self.tt(two, root, one, ALU.mult)
            banks.append(self.work.take())
            banks[1].made = self.spread(banks[1], lambda j: two[:, j:j + 1].to_broadcast([P, P]), r)
        self.rms_free = [banks[-1].made]
        return banks

    def spread(self, bank, column, *marks):
        for j in range(TT):
            m = self.mm(bank.buf[:, j * P:(j + 1) * P], column(j), self.ident[:, :], True, True, bank.wait,
                        self.consts_made, *marks, signal=j == TT - 1)
        return m

    def norm_into_h(self, x, x_marks, inverse, gain, shift, *marks):
        with ExitStack() as scope:
            before = self.everyone()
            tmp = self.ring("normed", 4, [P, T], scope, before)
            rms = inverse.buf[:, :]
            rounded = {}

            def rest(k):
                if k >= 0:
                    s, a = rounded[k]
                    lo = self.tt if k % 2 == 0 else self.ptt
                    r = lo(self.h_lo[:, k, :], s.buf[:, :], self.h_hi[:, k, :].bitcast(F32), ALU.subtract, a, before)
                    s.free = [r]
                    self.h_marks[k] = [a, r]

            for k in range(DT):
                s = tmp.take()
                n = s.buf[:, :]
                if shift is None:
                    v = self.stt(n, x[:, k, :], gain(k), rms, ALU.mult, ALU.mult, x_marks[k], inverse.made, s.wait,
                                 self.vecs_in)
                else:
                    v = self.tt(n, x[:, k, :], rms, ALU.mult, x_marks[k], inverse.made, s.wait)
                    v = self.ts(n, n, gain(k), ALU.mult, shift(k), ALU.add, v, *marks)
                rest(k - 1)
                a = self.act(self.h_hi[:, k, :], n, ACT.Copy, v, before)
                rounded[k] = s, a
            rest(DT - 1)
            inverse.free = [v]

    def out_project(self, name, src, src_marks, x, x_marks, gate=None, gate_mark=None, last=iter(()), beside=None,
                    next_gain=None):
        with ExitStack() as scope:
            before = self.everyone()
            n = len(src)
            half = n // 2
            own_hi = self.sb("own_hi", [P, n - half, T], F32R, scope)
            own_lo = self.sb("own_lo", [P, n - half, T], F32R, scope)
            pairs = self.H[:half] + [(own_hi[:, k, :], own_lo[:, k, :]) for k in range(n - half)]
            sq = self.ring("sq", 2, [P, T], scope, before)
            beside = beside(scope, before) if beside else iter(())
            marks = []

            def split(k):
                s, (hi, lo) = src[k], pairs[k]
                rest = self.tt if k % 3 else self.ptt
                a = self.act(hi, s, ACT.Copy, src_marks[k], before)
                marks.append([a, rest(lo, s, hi.bitcast(F32), ALU.subtract, a, src_marks[k], before)])

            for k in range(n - 1):
                split(k)
            new, bank_of, steps = [], {}, 0
            for cb, part in out_order():
                if part == 0:
                    bank_of[cb] = self.acc.take()
                if (cb, part) == (0, 1):
                    run(last)
                    split(n - 1)
                    if callable(x_marks):
                        x_marks = x_marks(marks)
                bank = bank_of[cb]
                a, b = (0, half) if part == 0 else (half, n)
                for _ in self.project((name, cb, part), bank, pairs[a:b], marks[a:b], a == 0, b == n):
                    next(last, None)
                    steps += 1
                    if cb and steps % 4 == 0:
                        next(beside, None)
                if part == 0:
                    continue
                xs = x[:, cb, :]
                if gate is None:
                    v = self.tt(xs, bank.buf[:, :], xs, ALU.add, bank.made, x_marks[cb])
                else:
                    v = self.stt(xs, bank.buf[:, :], gate(cb), xs, ALU.mult, ALU.add, bank.made, x_marks[cb],
                                 gate_mark)
                bank.free = [v]
                new.append(v)
                if cb == DT - 1:
                    run(beside)
                    self.act(self.rms[:, 0, :], self.ones[:, 0:TT], ACT.Sqrt, self.rms_free, self.consts_made)
                for k in range(max(cb - 1, 0), cb if cb < DT - 1 else DT):
                    summed = self.square_sum(x[:, k, :], k, new[k], sq)
                    if next_gain:
                        summed = self.square_sum(x[:, k, :], k, new[k], sq, next_gain, 1)
            return new, summed


def out_order():
    return [(0, 0), (1, 0), (0, 1), (1, 1)] + [(cb, part) for cb in range(2, DT) for part in range(2)]


def run(stage):
    for _ in stage:
        pass


def even_layer(c, masks):
    with ExitStack() as layer:
        before = c.everyone()
        ya = c.sb("ya", [P, DT, T], scope=layer)
        yb = c.x
        posts = c.ring("post", 2, [P, T], layer, before)
        gates = c.ring("rwkv_gate", 1, [P, T], layer, before)
        bonus = [c.sb(f"bonus{i}", [P, NCH, CH], scope=layer) for i in range(2)]
        ya_made, yb_made, last = even_mixers(c, ya, yb, masks, posts, gates, bonus)

        def load_x(splits):
            return [c.dma(c.x[:, k, :], c.t["x_t"][k * P:(k + 1) * P, :], c.sem(f"x_back{k}"), splits[DT + k])
                    for k in range(DT)]

        src_made = ya_made + yb_made

        def last_pair():
            yield from last
            src_made.append(yb_made[-1])

        src = [ya[:, k, :] for k in range(DT)] + [yb[:, k, :] for k in range(DT)]
        return c.out_project("even_out", src, src_made, c.x, load_x,
                             lambda k: c.mods[0][:, 2 * DT + k:2 * DT + k + 1], c.mod_made[0], last_pair(),
                             lambda scope, before: rotary(c, scope, before))


def glu(c, k, tmp, padded):
    b = c.acc.take()
    yield from c.project(("even", DT + k), b)
    s = tmp.take()
    a = c.act(s.buf[:, :], b.buf[:, :], ACT.Tanh, b.made, s.wait, scale=0.5)
    b.free = [a]
    c.ts(s.buf[:, :], s.buf[:, :], 0.5, ALU.mult, 0.5, ALU.add, a)
    b = c.acc.take()
    yield from c.project(("even", k), b)
    u = padded.take()
    v = c.tt(u.buf[:, TAPS - 1:], b.buf[:, :], s.buf[:, :], ALU.mult, b.made, a, u.wait)
    b.free, s.free = [v], [v]
    glu.out = u, v


def convolve(c, k, ya, u, u_made, before, made):
    y = ya[:, k, :]
    w = lambda j: c.vec("conv_w", k * TAPS + j)
    v = c.ts(y, u.buf[:, 0:T], w(0), ALU.mult, c.vec("conv_vec", k), ALU.add, u_made, before, c.vecs_in)
    for j in range(1, TAPS):
        v = c.stt(y, u.buf[:, j:j + T], w(j), y, ALU.mult, ALU.add)
        yield
    u.free = [v]
    made.append(v)


def conv_gate(c, k, gates):
    b = c.acc.take()
    yield from c.project(("even", 2 * DT + k), b)
    g = gates.of[k] = gates.ring.take()
    g.made = c.silu_twice(g.buf, b.buf[:, :], b.made, g.wait)
    b.free = [g.made]


def conv_finish(c, ya, tmp, gates, made, out):
    mean, var = c.work.take(), c.work.take()
    for k in range(DT):
        m = c.mm(mean.buf[:, :], c.ones[:, :], ya[:, k, :], k == 0, k == DT - 1, made[k], mean.wait,
                 c.consts_made, signal=True)
        yield
    for k in range(DT):
        s = tmp.take()
        v = c.stt(ya[:, k, :], mean.buf[:, :], -1.0 / D, ya[:, k, :], ALU.mult, ALU.add, m)
        a = c.act(s.buf[:, :], ya[:, k, :], ACT.Square, v, s.wait)
        n = c.mm(var.buf[:, :], c.ones[:, :], s.buf[:, :], k == 0, k == DT - 1, a, var.wait, signal=True)
        s.free = [n]
        yield
    mean.free = [v]
    inverse = tmp.take()
    inv = inverse.buf[:, :]
    a = c.act(inv, var.buf[:, :], ACT.Sqrt, n, inverse.wait, bias=c.ln_eps, scale=1.0 / D)
    var.free = [a]
    r = c.recip(inv, inv, a)
    for k in range(DT):
        g = gates.of[k]
        y = ya[:, k, :]
        v = c.tt(y, y, inv, ALU.mult, r)
        a = c.act(y, y, ACT.Silu, v, scale=c.vec("conv_vec", DT + k), bias=c.vec("conv_vec", 2 * DT + k))
        v = c.stt(y, y, 0.5, g.buf, ALU.mult, ALU.mult, a, g.made)
        g.free = [v]
        out.append(v)
        if len(gates.of) < DT:
            yield from conv_gate(c, len(gates.of), gates)
        yield
    inverse.free = [v]


def rwkv_masks(c, scope):
    sb = lambda name, shape: c.sb(name, shape, scope=scope)
    chunk_start = sb("chunk_start", [P, T])
    mask_t = sb("mask_t", [P, 2, P])
    mask_n = sb("mask_n", [P, P])
    block16 = sb("block16", [P, P])
    below = {s: sb(f"below{s}", [P, P]) for s in MERGES}
    c.fill(chunk_start[:, :], 1.0)
    for j in range(0, T, CH):
        c.fill(chunk_start[:, j:j + 1], 0.0)
    c.fill(mask_t[:, :, :], 1.0)
    for j in range(2):
        c.select(mask_t[:, j, :], [[1, P]], j - 1, -1, ALU.is_ge, 0.0)
    c.fill(mask_n[:, :], 1.0)
    c.select(mask_n[:, :], [[-1, P]], -1, 1, ALU.is_ge, 0.0)
    c.fill(block16[:, :], 1.0)
    v16 = block16[:, :].rearrange("p (b i) -> p b i", i=16)
    c.select(v16, [[-16, P // 16], [0, 16]], 0, 1, ALU.is_ge, 0.0)
    c.select(v16, [[16, P // 16], [0, 16]], 15, -1, ALU.is_ge, 0.0)
    for s in MERGES:
        v = below[s][:, :].rearrange("p (b i) -> p b i", i=s)
        v4 = below[s][:, :].rearrange("p (b h i) -> p b h i", h=2, i=s)
        c.fill(below[s][:, :], 1.0)
        c.select(v4, [[-2 * s, P // (2 * s)], [0, 2], [0, s]], -s, 1, ALU.is_ge, 0.0)
        c.select(v4, [[2 * s, P // (2 * s)], [0, 2], [0, s]], 2 * s - 1, -1, ALU.is_ge, 0.0)
        for b in range(1, P // s, 2):
            c.fill(v[:, b, :], 0.0)
    return chunk_start, mask_t, mask_n, block16, below, c.POOL.mark()


def even_mixers(c, ya, yb, masks_made, posts, gates, bonus):
    with ExitStack() as scope:
        before = c.everyone()
        sb = lambda name, shape: c.sb(name, shape, scope=scope)
        chunk_start, mask_t, mask_n, block16, below, masks = masks_made
        keep = sb("one_minus_k_a", [P, DT])
        c.ts(keep[:, :], c.vec("rwkv_vec", 3 * DT, DT), -1.0, ALU.mult, 1.0, ALU.add, before, c.vecs_in)
        up = sb("lora_up", [P, D])
        up_in = c.dma(up[:, :], c.t["lora_up"], c.sem("lora_up_in"), before)
        shifted = c.ring("shifted", 3, [P, 1 + T], scope, before)
        for s in shifted.slots:
            s.free = [c.fill(s.buf[:, 0:1], 0.0, before)]
        tmp = Ring([Slot(c.tables[:, i, :]) for i in range(5)])

        class Pair:
            def __init__(self, i):
                self.AR = sb(f"AR{i}", [P, NCH, 2, CH])
                self.K, self.B, self.V = (sb(f"{n}{i}", [P, NCH, CH]) for n in ("K", "B", "V"))
                self.bonus = bonus[i]
                self.carry = sb(f"carry{i}", [P, NCH])
                self.free = self.bonus_free = before
        pairs = [Pair(0), Pair(1)]
        flat = lambda b: b[:, :, :].rearrange("p c t -> p (c t)")
        mids = sb("mids", [P, NCH])
        lora = c.squares[:, 0, :]
        MM = [sb(f"MM{h}", [P, NCH, 4, CH]) for h in range(2)]
        NN = [sb(f"N{h}", [P, NCH, CH]) for h in range(2)]
        PT = [sb(f"PT{h}", [P, NCH, CH]) for h in range(2)]
        W = [[sb(f"W{h}{i}", [P, NCH, CH]) for i in range(4)] for h in range(2)]
        S = sb("S", [P, NCH, P])
        S_zero = c.fill(S[:, :, :], 0.0, before)

        def lerp(key, mu):
            bank = c.acc.take()
            yield from c.project(key, bank)
            z, d = shifted.take(), tmp.take()
            a = c.act(z.buf[:, 1:], bank.buf[:, :], ACT.Copy, bank.made, z.wait)
            bank.free = [a]
            yield
            p = c.ptt(d.buf[:, :], z.buf[:, 0:T], z.buf[:, 1:], ALU.subtract, a, d.wait)
            yield
            v = c.stt(z.buf[:, 1:], d.buf[:, :], mu, z.buf[:, 1:], ALU.mult, ALU.add, p)
            d.free = [v]
            lerp.out = z, v

        run(lerp(("even", 6 * DT), c.vec("mu_lora")))
        z, v = lerp.out
        a = c.act(lora[0:LORA, :], z.buf[0:LORA, 1:], ACT.Tanh, v, before)
        lora_made = c.act(lora[LORA:P, :], z.buf[LORA:P, 1:], ACT.Copy, v)
        z.free = [lora_made]

        def head_sum(x, *marks):
            b = c.work.take()
            b.made = c.mm(b.buf[:, :], c.head_ones[:, :], x, True, True, b.wait, c.consts_made, *marks, signal=True)
            return b

        def reciprocal(x):
            for j in range(0, T, CH):
                c.recip(x[:, j:j + CH], x[:, j:j + CH])
                yield

        def prepare(p, pair, between=iter(())):
            free = pair.free
            vv = lambda i: c.vec("rwkv_vec", i * DT + p)
            at = slice(p * P, (p + 1) * P)
            b = c.work.take()
            m = c.mm(b.buf[:, :], up[0:LORA, at], lora[0:LORA, :], True, True, b.wait, up_in, lora_made, signal=True)
            yield
            sg, cum, ex = tmp.take(), tmp.take(), tmp.take()
            a = c.act(sg.buf[:, :], b.buf[:, :], ACT.Tanh, m, sg.wait, c.half_bias_made,
                      bias=c.half_bias[:, p:p + 1], scale=0.5)
            b.free = [a]
            yield
            a = c.ts(sg.buf[:, :], sg.buf[:, :], 0.5, ALU.mult, 0.5, ALU.add, a)
            v = c.scan(cum.buf[:, :], chunk_start[:, :], sg.buf[:, :], a, masks, cum.wait)
            c3 = cum.buf[:, :].rearrange("p (c t) -> p c t", t=CH)
            mid = c3[:, :, CH // 2 - 1:CH // 2]
            a = c.act(mids[:, :], mid.rearrange("p c o -> p (c o)"), ACT.Exp, v, scale=-DECAY)
            e3 = ex.buf[:, :].rearrange("p (c t) -> p c t", t=CH)
            v = c.tt(e3, c3, mid.to_broadcast([P, NCH, CH]), ALU.subtract, v, ex.wait)
            yield
            up_to = c.act(pair.AR[:, :, 1, :], e3, ACT.Exp, v, free, scale=-DECAY)
            w = c.tt(pair.carry[:, 0:NCH - 1], pair.AR[:, 0:NCH - 1, 1, CH - 1], mids[:, 1:], ALU.mult, up_to, free)
            over = c.act(pair.K[:, :, :], e3, ACT.Exp, v, free, scale=DECAY)
            yield
            p1 = c.ptt(ex.buf[:, :], ex.buf[:, :], sg.buf[:, :], ALU.subtract, over, up_to)
            yield
            before_t = c.act(pair.AR[:, :, 0, :], e3, ACT.Exp, p1, scale=-DECAY)
            for s in (sg, cum, ex):
                s.free = [before_t, c.DVE.mark()]
            yield
            b = c.work.take()
            m = c.mm(b.buf[:, :], up[LORA:P, at], lora[LORA:P, :], True, True, b.wait, signal=True)
            rate = tmp.take()
            a = c.act(rate.buf[:, :], b.buf[:, :], ACT.Tanh, m, rate.wait, bias=c.half_bias[:, DT + p:DT + p + 1],
                      scale=0.5)
            b.free = [a]
            rate_made = c.ts(rate.buf[:, :], rate.buf[:, :], 0.5, ALU.mult, 0.5, ALU.add, a)
            yield
            yield from lerp(("even", 4 * DT + p), c.vec("mu_rkv", DT + p))
            k, k_made = lerp.out
            next(between, None)
            kz = k.buf[:, 1:]
            kk, sq = tmp.take(), tmp.take()
            v = c.ts(kk.buf[:, :], kz, vv(2), ALU.mult, None, None, k_made, kk.wait)
            yield
            a = c.act(sq.buf[:, :], kk.buf[:, :], ACT.Square, v, sq.wait)
            yield
            yield
            yield
            b = head_sum(sq.buf[:, :], a)
            yield
            a = c.act(sq.buf[:, :], b.buf[:, :], ACT.Sqrt, b.made)
            b.free = [a]
            yield
            v = c.ts(sq.buf[:, :], sq.buf[:, :], 1e-12, ALU.max, None, None, a)
            yield from reciprocal(sq.buf)
            v = c.tt(kk.buf[:, :], kk.buf[:, :], sq.buf[:, :], ALU.mult)
            yield
            r3 = lambda s: s.buf[:, :].rearrange("p (c t) -> p c t", t=CH)
            v = c.stt(pair.AR[:, :, 0, :], r3(kk), -1.0, pair.AR[:, :, 0, :], ALU.mult, ALU.mult, before_t)
            v = c.tt(kk.buf[:, :], kk.buf[:, :], rate.buf[:, :], ALU.mult, rate_made)
            yield
            v = c.tt(pair.B[:, :, :], r3(kk), pair.K[:, :, :], ALU.mult, over, free)
            yield
            v = c.ts(rate.buf[:, :], rate.buf[:, :], vv(3), ALU.mult, keep[:, p:p + 1], ALU.add)
            v = c.tt(kz, kz, rate.buf[:, :], ALU.mult)
            v = c.tt(flat(pair.K), kz, flat(pair.K), ALU.mult)
            for s in (kk, sq, rate):
                s.free = [v]
            yield from lerp(("even", 3 * DT + p), c.vec("mu_rkv", p))
            r, r_made = lerp.out
            next(between, None)
            rz = r.buf[:, 1:]
            r33 = rz.rearrange("p (c t) -> p c t", t=CH)
            v = c.tt(pair.AR[:, :, 1, :], r33, pair.AR[:, :, 1, :], ALU.mult, r_made, up_to)
            yield
            v = c.stt(rz, rz, c.vec("r_k", p), kz, ALU.mult, ALU.mult)
            k.free = [v]
            yield
            yield
            bonus = head_sum(rz, v)
            r.free = [bonus.made]
            yield from lerp(("even", 5 * DT + p), c.vec("mu_rkv", 2 * DT + p))
            z, v = lerp.out
            a = c.act(flat(pair.V), z.buf[:, 1:], ACT.Copy, v, free)
            v = c.tt(flat(pair.bonus), bonus.buf[:, :], z.buf[:, 1:], ALU.mult, bonus.made, free, pair.bonus_free)
            z.free, bonus.free = [a, v], [v]
            pair.made = [v, a]
            yield from between

        def gate(p):
            b = c.acc.take()
            yield from c.project(("even", 6 * DT + 1 + p), b)
            gate.out = g = gates.take()
            g.made = c.act(g.buf[:, :], b.buf[:, :], ACT.Silu, b.made, g.wait)
            b.free = [g.made]

        def four(lhsT, rhs, *marks):
            b = c.work.take()
            for j in range(NCH):
                m = c.mm(b.buf[:, j * CH:(j + 1) * CH], lhsT[:, j, :], rhs[:, j, :], True, True, b.wait, *marks,
                         signal=j == NCH - 1)
            b.made = m
            return b

        def three(b):
            return b.buf[:, :].rearrange("p (c t) -> p c t", t=CH)

        def every_chunk(mask):
            return mask[:, :].unsqueeze(1).to_broadcast([P, NCH, CH])

        def to_sbuf(dst, b, act):
            m = c.act(dst, three(b), ACT.Copy, b.made) if act else c.copy(dst, three(b), b.made)
            b.free = [m]
            return m

        def matrices(h, pair):
            hs = slice(h * RH, (h + 1) * RH)
            for j in range(NCH):
                b = c.work.take()
                ar = pair.AR[hs, j, :, :].rearrange("p a t -> p (a t)")
                c.mm(b.buf[:, 0:2 * CH], pair.K[hs, j, :], ar, True, True, b.wait, pair.made)
                m = c.mm(b.buf[:, 2 * CH:], pair.B[hs, j, :], ar, True, True, signal=True)
                v = c.tt(MM[h][:, j, :, :].rearrange("p (x a) t -> p x (a t)", a=2),
                         b.buf[:, :].rearrange("p (x a) -> p x a", x=2),
                         mask_t[:, :, :].rearrange("p a t -> p (a t)").unsqueeze(1).to_broadcast([P, 2, 2 * CH]),
                         ALU.mult, m, masks, before, solved)
                b.free = [v]
                yield
            b = c.work.take()
            for j in range(NCH):
                m = c.mm(b.buf[:, j * CH:(j + 1) * CH], pair.AR[hs, j, 0, :], pair.B[hs, j, :], True, True, b.wait,
                         signal=j == NCH - 1)
            v = c.tt(NN[h][:, :, :], three(b), every_chunk(mask_n), ALU.mult, m)
            b.free = [v]
            matrices.made[h] = v
            yield
        matrices.made = {}

        def add_to_inverse(h, b):
            v = c.tt(PT[h][:, :, :], three(b), PT[h][:, :, :], ALU.add, b.made)
            b.free = [v]
            return v

        def invert(h, pair):
            yield from matrices(h, pair)
            w = W[h]
            p1 = c.ptt(w[0][:, :, :], NN[h][:, :, :], every_chunk(block16), ALU.mult, matrices.made[h], solved)
            yield
            p2 = c.tt(w[1][:, :, :], MM[h][:, :, 2, :], every_chunk(block16), ALU.mult)
            pt = c.ptt(PT[h][:, :, :], w[1][:, :, :], every_chunk(c.ident), ALU.add, p2, solved)
            yield
            b1, b2 = four(w[1], w[0], p1, p2), four(w[0], w[1], p1, p2)
            m1 = to_sbuf(w[2][:, :, :], b1, True)
            m2 = to_sbuf(w[3][:, :, :], b2, False)
            yield
            b1, b3, b2 = four(w[3], w[2], m1, m2), four(w[2], PT[h], m1, pt), four(w[2], w[3], m1, m2)
            m1 = to_sbuf(w[0][:, :, :], b1, True)
            pt = add_to_inverse(h, b3)
            m2 = to_sbuf(w[1][:, :, :], b2, False)
            yield
            part = lambda i, at: c.ptt(w[at][:, :, :], NN[h][:, :, :], every_chunk(below[MERGES[i]]), ALU.mult,
                                       c.PE.mark(), matrices.made[h])
            off = part(0, 3)
            b1, b2 = four(w[1], w[0], m1, m2), four(w[0], PT[h], m1, pt)
            m1 = to_sbuf(w[2][:, :, :], b1, True)
            pt = add_to_inverse(h, b2)
            yield
            pt = add_to_inverse(h, four(w[2], PT[h], m1, pt))
            yield
            for i in range(len(MERGES)):
                b = c.work.take()
                for j in range(NCH):
                    m = c.tr(b.buf[:, j * CH:(j + 1) * CH], PT[h][:, j, :], pt, b.wait, signal=j == NCH - 1)
                b.made = m
                this, at = off, 3 - 2 * (i % 2)
                if i + 1 < len(MERGES):
                    off = part(i + 1, 4 - at)
                p = to_sbuf(w[0][:, :, :], b, False)
                b = four(w[at], PT[h], this, pt)
                m = to_sbuf(w[2][:, :, :], b, True)
                yield
                pt = add_to_inverse(h, four(w[0], w[2], p, m))
                yield
            invert.made[h] = pt
        invert.made = {}

        def solve(p, pair):
            yield from in_turn(invert(0, pair), invert(1, pair))
            inv = [invert.made[0], invert.made[1]]
            A_t, V_t, K_t, B_t = W[0]
            Z, U0, PA, U = W[1]
            turned = []
            for i, (dst, src) in enumerate(((A_t, lambda j: pair.AR[:, j, 0, :]), (V_t, lambda j: pair.V[:, j, :]),
                                            (K_t, lambda j: pair.K[:, j, :]), (B_t, lambda j: pair.B[:, j, :]))):
                b = c.work.take()
                for j in range(NCH):
                    m = c.tr(b.buf[:, j * CH:(j + 1) * CH], src(j), b.wait, inv, pair.made, signal=j == NCH - 1)
                b.made = m
                turned.append(to_sbuf(dst[:, :, :], b, i % 2 == 0))
                yield
            heads = [(h, slice(h * RH, (h + 1) * RH)) for h in range(2)]
            b = c.work.take()
            for j in range(NCH):
                for h, hs in heads:
                    m = c.mm(three(b)[:, j, hs], MM[h][:, j, 0, :], V_t[:, j, hs], True, True, b.wait, turned[:2],
                             signal=j == NCH - 1 and h == 1)
            b.made = m
            z = to_sbuf(Z[:, :, :], b, True)
            b = c.work.take()
            for j in range(NCH):
                for h, hs in heads:
                    m = c.mm(three(b)[hs, j, :], A_t[:, j, hs], PT[h][:, j, :], True, True, b.wait,
                             signal=j == NCH - 1 and h == 1)
            b.made = m
            pa = to_sbuf(PA[:, :, :], b, False)
            yield
            b = c.work.take()
            for j in range(NCH):
                for h, hs in heads:
                    m = c.mm(three(b)[:, j, hs], PT[h][:, j, :], Z[:, j, hs], True, True, b.wait, z,
                             signal=j == NCH - 1 and h == 1)
            b.made = m
            u0 = to_sbuf(U0[:, :, :], b, True)
            yield
            y = c.work.take()
            u, s_made = u0, S_zero
            for j in range(NCH):
                Uj = U0 if j == 0 else U
                if j:
                    b = c.work.take()
                    m = c.mm(b.buf[:, 0:P], PA[:, j, :], S[:, j, :], True, True, b.wait, pa, s_made, signal=True)
                    u = c.tt(U[:, j, :], b.buf[:, 0:P], U0[:, j, :], ALU.add, m, u0)
                    b.free = [u]
                if j < NCH - 1:
                    b = c.work.take()
                    c.mm(b.buf[:, 0:P], K_t[:, j, :], V_t[:, j, :], True, False, b.wait, turned)
                if j:
                    c.mm(three(y)[:, j, :], S[:, j, :], pair.AR[:, j, 1, :], True, False, y.wait)
                for h, hs in heads:
                    c.mm(three(y)[hs, j, :], V_t[:, j, hs], MM[h][:, j, 1, :], j == 0, False, y.wait)
                yield
                if j < NCH - 1:
                    w = pair.carry[:, j:j + 1]
                    m = c.mm(b.buf[:, 0:P], B_t[:, j, :], Uj[:, j, :], False, True, u, signal=True)
                    for h, hs in heads:
                        if j == 0:
                            v = c.ts(S[hs, 1, hs], b.buf[hs, hs], w[hs], ALU.mult, None, None, m, S_free[0])
                        else:
                            v = c.tt(S[hs, j + 1, hs], b.buf[hs, hs], S[hs, j, hs], ALU.add, m, S_free[0])
                            v = c.ts(S[hs, j + 1, hs], S[hs, j + 1, hs], w[hs], ALU.mult, None, None, v)
                    b.free, s_made = [v], v
                for h, hs in heads:
                    m = c.mm(three(y)[hs, j, :], Uj[:, j, hs], MM[h][:, j, 3, :], False, True, u, signal=True)
                yield
            S_free[0] = m
            solved[:] = [m]
            pair.free = [m]
            t1 = posts.take()
            t1.made = c.act(t1.buf[:, :], y.buf[:, :], ACT.Copy, m, t1.wait)
            y.free = [t1.made]
            solve.out = t1

        def finish(p, pair, t1):
            t2 = posts.take()
            b = head_sum(t1.buf[:, :], t1.made)
            yield
            v = c.stt(t1.buf[:, :], b.buf[:, :], -1.0 / RH, t1.buf[:, :], ALU.mult, ALU.add, b.made)
            b.free = [v]
            yield
            a = c.act(t2.buf[:, :], t1.buf[:, :], ACT.Square, v, t2.wait)
            yield
            b = head_sum(t2.buf[:, :], a)
            yield
            a = c.act(t2.buf[:, :], b.buf[:, :], ACT.Sqrt, b.made, bias=c.gn_eps, scale=1.0 / RH)
            b.free = [a]
            yield
            c.DVE.wait(a)
            yield from reciprocal(t2.buf)
            v = c.tt(t1.buf[:, :], t1.buf[:, :], t2.buf[:, :], ALU.mult)
            yield
            v = c.ts(t1.buf[:, :], t1.buf[:, :], c.vec("rwkv_vec", 4 * DT + p), ALU.mult,
                     c.vec("rwkv_vec", 5 * DT + p), ALU.add)
            v = c.tt(t1.buf[:, :], t1.buf[:, :], flat(pair.bonus), ALU.add)
            pair.bonus_free = [v]
            g = gate.out
            v = c.tt(yb[:, p, :], t1.buf[:, :], g.buf[:, :], ALU.mult, g.made, before)
            t1.free, t2.free, g.free = [v], [v], [v]
            made.append(v)

        made, solved, S_free = [], [], [S_zero]
        padded = c.ring("padded", 2, [P, TAPS - 1 + T], scope, before)
        for s in padded.slots:
            s.free = [c.fill(s.buf[:, 0:TAPS - 1], 0.0, before)]
        convolved, ya_made = [], []

        class conv_gates:
            of, ring = {}, None
        c.work.slots.append(c.stat)
        run(prepare(0, pairs[0]))
        run(glu(c, 0, tmp, padded))
        finishing = iter(())
        for p in range(DT):
            u, u_made = glu.out
            taps = convolve(c, p, ya, u, u_made, before, convolved)
            if p + 1 < DT:
                side = chain(finishing, prepare(p + 1, pairs[(p + 1) % 2], modulations(c, p)),
                             glu(c, p + 1, tmp, padded), gate(p))
                run(weave((solve(p, pairs[p % 2]), SOLVE_STEPS), (side, PREPARE_STEPS),
                          (chain(idle(TAP_DELAY), taps), TAPS + TAP_DELAY)))
            else:
                spare = pairs[(p + 1) % 2]
                in_two = spare.AR[:, :, :, :].rearrange("p (i c) a t -> p i (c a t)", i=2)
                conv_gates.ring = Ring([Slot(b, spare.free) for b in (
                    in_two[:, 0, :], in_two[:, 1, :], flat(spare.K), flat(spare.B), flat(spare.V))])
                side = chain(finishing, gate(p), modulations(c, p),
                             weave((taps, TAPS), (chain(*(conv_gate(c, k, conv_gates) for k in range(5))), 40)),
                             conv_finish(c, ya, tmp, conv_gates, convolved, ya_made))
                run(weave((solve(p, pairs[p % 2]), SOLVE_STEPS), (side, FINISH_STEPS)))
            finishing = finish(p, pairs[p % 2], solve.out)
        c.work.slots.remove(c.stat)
        c.squares_free[0] = c.everyone()
        return ya_made, made, finishing


def modulations(c, p):
    yield from c.modulation(0, [2 * DT + p])
    yield from c.modulation(1, range(3 * p, 3 * p + 3))


def rotary(c, scope, before):
    pos_i, chunk_i = c.sb("pos_i", [P, T], I32, scope), c.sb("chunk_i", [P, T], I32, scope)
    pos_q, chunk_q = c.sb("pos_q", [P, TT], I32, scope), c.sb("chunk_q", [P, TT], I32, scope)
    pos, angle, turns = (c.sb(name, [P, T], scope=scope) for name in ("pos", "angle", "turns"))
    loaded = [c.dma(pos_i[:, :], c.t["pos"].to_broadcast([P, T]), c.sem("pos_in"), before),
              c.dma(pos_q[:, :], c.t["pos_q"], c.sem("pos_q_in"), before)]
    yield
    c.copy(pos[:, :], pos_i[:, :], before, loaded)
    for dst, src, out in ((chunk_i, pos_i, c.tables[:, 4, :]), (chunk_q, pos_q, c.chunk_q[:, :])):
        c.DVE.do(lambda e, d=dst, s=src: e.tensor_scalar(d[:, :], s[:, :], 6, None, ALU.arith_shift_right))
        rotary.chunks = c.copy(out, dst[:, :])
        yield
    for i, (inv, sign) in enumerate(((c.vec("inv128"), c.sign128), (c.vec("inv64"), c.sign64))):
        c.ts(angle[:, :], pos[:, :], inv, ALU.mult, None, None, c.vecs_in)
        for j, quarter in enumerate((0.25, 0.0)):
            r = c.tables[:, 2 * i + j, :]
            c.ts(turns[:, :], angle[:, :], float(0.5 / np.pi), ALU.mult, quarter, ALU.add)
            c.ts(turns[:, :], turns[:, :], ROUND, ALU.add, ROUND, ALU.subtract)
            yield
            c.stt(r, turns[:, :], -TWO_PI[0], angle[:, :], ALU.mult, ALU.add)
            for part in TWO_PI[1:]:
                c.stt(r, turns[:, :], -part, r, ALU.mult, ALU.add)
            yield
            if j == 0:
                c.ts(r, r, float(np.pi / 2), ALU.add, None, None)
            v = c.ts(r, r, 3.1415925, ALU.min, -3.1415925, ALU.max)
            yield
            a = c.act(r, r, ACT.Sin, v)
            yield
        rotary.made = c.ts(r, r, sign, ALU.mult, None, None, a, c.consts_made)
        yield


def odd_layer(c, x_marks):
    with ExitStack() as layer:
        before = c.everyone()
        Q = c.sb("q", [P, AH, T], scope=layer)
        attn = layer.enter_context(ExitStack())
        sb = lambda name, shape, dt=F32: c.sb(name, shape, dt, scope=attn)
        keys = sb("keys", [P, T])
        values = sb("values", [P, TT, P])
        bias = sb("bias", [P, TT, T])
        probs = c.ring("probs", SOFTMAX_LAG + 2, [P, T], attn, before)
        gates = c.ring("gate", 4, [P, T], attn, before)
        small = sb("small", [P, 3 * AH * TT])
        with ExitStack() as index:
            isb = lambda name, shape, dt=F32: c.sb(name, shape, dt, scope=index)
            tmp = c.ring("attn_tmp", 5, [P, T], index, before)
            score = isb("score", [P, TT, T])
            cos128, sin128, cos64, sin64, chunk_k = (c.tables[:, i, :] for i in range(5))
            rope_made = rotary.made
            for t in range(TT):
                adm = c.ts(bias[:, t, :], chunk_k, c.chunk_q[:, t:t + 1], ALU.is_gt, NEG, ALU.mult, before)

            def rotate(key, half, cos, sin, out, *marks):
                b = c.acc.take()
                yield from c.project(key, b)
                swapped, plain = tmp.take(), tmp.take()
                for r in range(0, P, half):
                    o = r ^ half
                    a = c.act(swapped.buf[r:r + half, :], b.buf[o:o + half, :], ACT.Copy, b.made, swapped.wait)
                p = c.ptt(swapped.buf[:, :], swapped.buf[:, :], sin, ALU.mult, a, rope_made)
                v = c.tt(plain.buf[:, :], b.buf[:, :], cos, ALU.mult, a, rope_made, plain.wait)
                b.free = [a, v]
                v = c.ptt(out, plain.buf[:, :], swapped.buf[:, :], ALU.add, v, *marks)
                swapped.free, plain.free = [v], [v]
                rotate.made = v
                yield

            ki, qi, wi = isb("ki", [P, T]), isb("qi", [P, IH // 2, T]), isb("wi", [P, TT, IH])
            run(rotate(("ki", 0), 32, cos64, sin64, ki[:, :], before))
            acc = c.acc.take()
            run(c.project(("wi", 0), acc))
            s = tmp.take()
            a = c.act(s.buf[0:IH, :], acc.buf[0:IH, :], ACT.Copy, acc.made, s.wait)
            acc.free = [a]
            b = c.work.take()
            for t in range(TT):
                m = c.tr(b.buf[:, t * IH:(t + 1) * IH], s.buf[0:IH, t * P:(t + 1) * P], a, b.wait, signal=t == TT - 1)
            s.free = b.made = [m]
            wi_made = c.ts(wi[:, :, :], b.buf[:, 0:TT * IH].rearrange("p (t h) -> p t h", h=IH),
                           float(IH ** -0.5), ALU.mult, None, None, b.made)
            b.free = [wi_made]
            qi_made = []
            for i in range(IH // 2):
                run(rotate(("qi", i), 32, cos64, sin64, qi[:, i, :], before))
                qi_made.append(rotate.made)

            def scores():
                for t in range(TT):
                    for h in range(IH):
                        hs = slice(h % 2 * 64, h % 2 * 64 + 64)
                        b = c.work.take()
                        m = c.mm(b.buf[:, :], qi[hs, h // 2, t * P:(t + 1) * P], ki[hs, :], True, True, b.wait,
                                 qi_made[h // 2], signal=True)
                        s = probs.take()
                        a = c.act(s.buf[:, :], b.buf[:, :], ACT.Relu, m, s.wait, scale=0.125)
                        b.free = [a]
                        v = c.stt(score[:, t, :], s.buf[:, :], wi[:, t, h:h + 1],
                                  bias[:, t, :] if h == 0 else score[:, t, :], ALU.mult, ALU.add, a, wi_made, adm)
                        s.free = [v]
                        if h % 2:
                            yield
                best = isb("best", [P, 2, 8])
                made = [c.DVE.mark()] * 2
                for t0 in range(0, TT, 2):
                    for _ in range(TOPK // 8):
                        for i in range(2):
                            made[i] = c.DVE.do(lambda e, i=i, t=t0 + i: e.max(best[:, i, :], score[:, t, :]),
                                               made[i], chained=False)
                        for i in range(2):
                            made[i] = c.DVE.do(lambda e, i=i, t=t0 + i: e.match_replace(
                                score[:, t, :], best[:, i, :], score[:, t, :], TAKEN), made[i], chained=False)
                        yield
                    for t in range(t0, t0 + 2):
                        c.ts(score[:, t, :], score[:, t, :], -2e38, ALU.is_le, -NEG, ALU.mult)
                        scores.made = c.stt(bias[:, t, :], score[:, t, :], NEG, bias[:, t, :], ALU.add, ALU.add)
                    yield

            q_made = [None] * AH
            gate_of = {}

            def gates_in():
                for h in range(AH):
                    b = c.acc.take()
                    yield from c.project(("g", h), b)
                    g = gate_of[h] = gates.take()
                    g.made = c.silu_twice(g.buf[:, :], b.buf[:, :], b.made, g.wait)
                    b.free = [g.made]
                    yield
            gates_coming = gates_in()

            def main():
                yield from rotate(("k", 0), 64, cos128, sin128, keys[:, :], before)
                main.keys = rotate.made
                b = c.acc.take()
                yield from c.project_tokens(("v", 0), b)
                main.values = c.act(values[:, :, :], b.buf[:, :].rearrange("p (t d) -> p t d", d=P), ACT.Copy,
                                    b.made, before)
                b.free = [main.values]
                for h in range(AH):
                    yield from rotate(("q", h), 64, cos128, sin128, Q[:, h, :], before)
                    q_made[h] = rotate.made
                while len(gate_of) < 3:
                    next(gates_coming)
                    yield

            run(blend(main(), scores(), 0.3))
            c.dump("bias", bias[:, :, :])
            c.dump("q", Q[:, :, :])
        PT = c.ring("probs_t", 2, [P, TT, T], attn, c.everyone())
        out_made = []

        def front(i):
            h, t = divmod(i, TT)
            b = c.work.take()
            m = c.mm(b.buf[:, :], Q[:, h, t * P:(t + 1) * P], keys[:, :], True, True, b.wait, q_made[h],
                     main.keys, signal=True)
            return softmax_tile(c, b, m, bias[:, t, :], probs.take(), small, i, float(P ** -0.5), scores.made)

        def back(i, prob, state):
            h, t = divmod(i, TT)
            if t == 0:
                state.pt, state.marks = PT.take(), []
            state.marks.append(turn_tile(c, prob, TT, state.pt, t))

        def finish(h, pt, marks):
            o = c.work.take()
            for j in range(TT):
                m = c.mm(o.buf[:, :], values[:, j, :], pt.buf[:, j, :], j == 0, j == TT - 1, o.wait, marks,
                         main.values, signal=j == TT - 1)
            pt.free = [m]
            g = gate_of[h]
            v = c.stt(Q[:, h, :], o.buf[:, :], 0.5, g.buf[:, :], ALU.mult, ALU.mult, m, g.made)
            o.free, g.free = [v], [v]
            out_made.append(v)

        run(blend(pipeline(AH * TT, TT, front, back, finish), gates_coming, 1.75))
        c.dump("og", Q[:, :, :])
        attn.close()
        return c.out_project("odd_out", [Q[:, h, :] for h in range(AH)], out_made, c.x, x_marks,
                             lambda k: c.mods[1][:, 2 * DT + k:2 * DT + k + 1], c.mod_made[1],
                             next_gain=lambda k: c.vec("final_g", k))


def pipeline(n, per_head, front, back, finish):
    class State:
        pt = marks = None
    probs, state, due = {}, State(), None
    for i in range(n + SOFTMAX_LAG + 1):
        if i < n:
            probs[i] = front(i)
        k = i - SOFTMAX_LAG
        if 0 <= k < n:
            back(k, probs.pop(k), state)
        if due is not None:
            finish(*due)
            due = None
        if 0 <= k < n and k % per_head == per_head - 1:
            due = (k // per_head, state.pt, state.marks)
        yield


def softmax_tile(c, bank, logits, bias, prob, small, i, scale, *marks):
    n = bias.shape[-1]
    mx, total, inv = (small[:, 3 * i + j:3 * i + j + 1] for j in range(3))
    p = prob.buf[:, 0:n]
    v = c.DVE.do(lambda e: e.tensor_tensor_reduce(p, bank.buf[:, 0:n], bias, 1.0, 3 * NEG, ALU.add, ALU.max, mx),
                 logits, prob.wait, *marks)
    bank.free = [v]
    v = c.ts(mx, mx, -scale, ALU.mult, None, None, v)
    a = c.act(p, p, ACT.Exp, v, bias=mx, scale=scale, accum_out=total)
    v = c.recip(inv, total, a)
    prob.made = c.ts(p, p, inv, ALU.mult, None, None, v)
    return prob


def turn_tile(c, prob, width, pt, t):
    b = c.work.take()
    for j in range(width):
        m = c.tr(b.buf[:, j * P:(j + 1) * P], prob.buf[:, j * P:(j + 1) * P], prob.made, b.wait,
                 signal=j == width - 1)
    prob.free = [m]
    dst = pt.buf[:, 0:width, t * P:(t + 1) * P]
    src = b.buf[:, 0:width * P].rearrange("p (j q) -> p j q", q=P)
    done = c.act(dst, src, ACT.Copy, m, pt.wait) if t % 2 else c.copy(dst, src, m, pt.wait)
    b.free = [done]
    return done


def softplus_of_minus(c, x, u, z, tmp, *marks):
    a = c.act(u, x, ACT.Abs, *marks)
    a = c.act(u, u, ACT.Exp, a, scale=-1.0)
    v = c.ts(z, u, 2.0, ALU.add, None, None, a)
    v = c.recip(z, z)
    v = c.tt(z, z, u, ALU.mult)
    v = c.tt(u, z, z, ALU.mult)
    v = c.ts(tmp, u, 2.0 / 19, ALU.mult, 2.0 / 17, ALU.add)
    for k in range(15, -1, -2):
        v = c.tt(tmp, tmp, u, ALU.mult)
        v = c.ts(tmp, tmp, 2.0 / k, ALU.add, None, None)
    v = c.tt(tmp, tmp, z, ALU.mult)
    v = c.ts(x, x, -1.0, ALU.mult, 0.0, ALU.max)
    return c.tt(x, x, tmp, ALU.add)


def lru_layer(c, x_marks):
    with ExitStack() as layer:
        before = c.everyone()
        sb = lambda name, shape: c.sb(name, shape, scope=layer)
        Y = sb("lru_y", [P, LT, T])
        with ExitStack() as scope:
            gates_w = c.sb("lru_gates_w", [P, 2, LRU], scope=scope)
            w_in = c.dma(gates_w[:, :, :], c.t["lru_gates"], c.sem("lru_gates_in"), before)
            padded = c.ring("lru_padded", 3, [P, LTAPS - 1 + T], scope, before)
            for s in padded.slots:
                s.free = [c.fill(s.buf[:, 0:LTAPS - 1], 0.0, before)]
            tmp = c.ring("lru_tmp", 12, [P, T], scope, before)
            rate = c.sb("lru_rate", [P, 2, LT], scope=scope)
            aux = c.sb("lru_aux", [P, 3, LT], scope=scope)
            v = c.copy(rate[:, 0, :], c.vec("lru_a", 0, LT), before, c.vecs_in)
            v = softplus_of_minus(c, rate[:, 0, :], aux[:, 0, :], aux[:, 1, :], aux[:, 2, :], v)
            c.ts(rate[:, 1, :], rate[:, 0, :], LRU_C / 2, ALU.mult, None, None)
            rate_made = c.ts(rate[:, 0, :], rate[:, 0, :], -LRU_C / 2, ALU.mult, None, None)
            made = []

            def block(n):
                b = c.acc.take()
                yield from c.project(("lru", n), b)
                xp = padded.take()
                a = c.act(xp.buf[:, LTAPS - 1:], b.buf[:, :], ACT.Copy, b.made, xp.wait)
                b.free = [a]
                xc = tmp.take()
                w = lambda j: c.vec("lru_conv_w", j * LT + n)
                v = c.ts(xc.buf[:, :], xp.buf[:, 0:T], w(0), ALU.mult, c.vec("lru_conv_b", n), ALU.add, a, xc.wait)
                for j in range(1, LTAPS):
                    v = c.stt(xc.buf[:, :], xp.buf[:, j:j + T], w(j), xc.buf[:, :], ALU.mult, ALU.add)
                xp.free = [v]
                b = c.acc.take()
                yield from c.project(("lru", LT + n), b)
                sg = tmp.take()
                silu = c.silu_twice(sg.buf[:, :], b.buf[:, :], b.made, sg.wait)
                b.free = [silu]
                block.out = xc, sg, silu, v

            def recurrence(n, xc, sg, silu, v):
                g = []
                for i in range(2):
                    b = c.work.take()
                    m = c.mm(b.buf[:, :], gates_w[:, i, n * P:(n + 1) * P], xc.buf[:, :], True, True, b.wait, v,
                             w_in, signal=True)
                    s = tmp.take()
                    at = 2 * DT + i * LT + n
                    s.made = c.act(s.buf[:, :], b.buf[:, :], ACT.Tanh, m, s.wait, c.half_bias_made,
                                   bias=c.half_bias[:, at:at + 1], scale=0.5)
                    b.free = [s.made]
                    g.append(s)
                    yield
                r, i = g
                decay, root = tmp.take(), tmp.take()
                a = c.act(decay.buf[:, :], r.buf[:, :], ACT.Exp, rate_made, decay.wait, scale=rate[:, 0, n:n + 1],
                          bias=rate[:, 0, n:n + 1])
                yield
                th = c.act(r.buf[:, :], r.buf[:, :], ACT.Tanh, scale=rate[:, 1, n:n + 1], bias=rate[:, 1, n:n + 1])
                p = c.ptt(root.buf[:, :], decay.buf[:, :], decay.buf[:, :], ALU.mult, a, root.wait)
                c.stt(i.buf[:, :], i.buf[:, :], 1.0, xc.buf[:, :], ALU.add, ALU.mult, i.made)
                yield
                v = c.stt(root.buf[:, :], root.buf[:, :], 1.0, r.buf[:, :], ALU.add, ALU.mult, p, th)
                yield
                a = c.act(root.buf[:, :], root.buf[:, :], ACT.Sqrt, v)
                yield
                v = c.stt(root.buf[:, :], root.buf[:, :], 0.5, i.buf[:, :], ALU.mult, ALU.mult, a)
                v = c.scan(r.buf[:, :], decay.buf[:, :], root.buf[:, :])
                v = c.stt(Y[:, n, :], r.buf[:, :], 0.5, sg.buf[:, :], ALU.mult, ALU.mult, silu, before)
                for s in (xc, sg, r, i, decay, root):
                    s.free = [v]
                made.append(v)

            last = iter(())
            for n in range(LT):
                run(blend(block(n), last, 0.8))
                last = recurrence(n, *block.out)
            return c.out_project("lru_out", [Y[:, n, :] for n in range(LT)], made, c.x, x_marks, last=last)


def fox_layer(c, x_marks):
    with ExitStack() as layer:
        before = c.everyone()
        sb = lambda name, shape: c.sb(name, shape, scope=layer)
        G = sb("fox_gate", [P, DT, T])
        with ExitStack() as scope:
            sb = lambda name, shape: c.sb(name, shape, scope=scope)
            Q, K, V = sb("fox_q", [P, DT, T]), sb("fox_k", [P, DT, T]), sb("fox_v", [P, TT, D])
            probs = c.ring("fox_probs", SOFTMAX_LAG + 2, [P, T], scope, before)
            PT = c.ring("fox_probs_t", 2, [P, TT, T], scope, before)
            keybias = c.ring("fox_keybias", 2, [P, T], scope, before)
            small = sb("fox_small", [P, 3 * FH * TT])
            rows = sb("fox_rows", [FH, 4, T])
            pick = sb("fox_pick", [FH, FH, P])
            c.fill(pick[:, :, :], 0.0, before)
            picked = c.select(pick[:, :, :], [[-1, FH], [0, P]], 0, 1, ALU.not_equal, 1.0)
            b = c.acc.take()
            run(c.project(("fox_f", 0), b))
            f, u, z, tmp = (rows[:, i, :] for i in range(4))
            v = c.ts(f, b.buf[0:FH, :], c.vec("fox_b")[0:FH], ALU.add, None, None, b.made, before, c.vecs_in)
            b.free = [v]
            v = softplus_of_minus(c, f, u, z, tmp, v)
            c.DVE.do(lambda e: e.memset(u, 1.0))
            sums = c.scan(z, u, f)
            q_made, k_made, v_made, g_made = ([None] * DT for _ in range(4))

            def pair_in(p):
                for key, made, dst, func, kw in (("fox_q", q_made, Q, ACT.Copy, {"scale": 0.125}),
                                                 ("fox_k", k_made, K, ACT.Copy, {}),
                                                 ("fox_g", g_made, G, None, {})):
                    b = c.acc.take()
                    yield from c.project((key, p), b)
                    made[p] = (c.act(dst[:, p, :], b.buf[:, :], func, b.made, before, **kw) if func else
                               c.silu_twice(dst[:, p, :], b.buf[:, :], b.made, before))
                    b.free = [made[p]]
                b = c.acc.take()
                yield from c.project_tokens(("fox_v", p), b)
                v_made[p] = c.copy(V[:, :, p * P:(p + 1) * P], b.buf[:, :].rearrange("p (t d) -> p t d", d=P),
                                   b.made, before)
                b.free = [v_made[p]]

            out_made = []

            def pairs_in():
                for p in range(DT):
                    yield from pair_in(p)
                    loaded.append(p)
            loaded, coming = [], pairs_in()
            keybias_of, o_of = {}, {}

            def front(i):
                h, t = divmod(i, TT)
                p, hs = h // 2, slice(h % 2 * 64, h % 2 * 64 + 64)
                while p not in loaded:
                    next(coming)
                if t == 0:
                    b = c.work.take()
                    m = c.mm(b.buf[:, :], pick[:, h, :], z, True, True, b.wait, picked, sums, signal=True)
                    kb = keybias_of[h] = keybias.take()
                    kb.made = c.act(kb.buf[:, :], b.buf[:, :], ACT.Copy, m, kb.wait)
                    b.free = [kb.made]
                kb = keybias_of[h]
                n = (t + 1) * P
                b = c.work.take()
                c.mm(b.buf[:, 0:n], Q[hs, p, t * P:n], K[hs, p, 0:n], True, False, b.wait, q_made[p], k_made[p])
                m = c.mm(b.buf[:, t * P:n], c.ident[:, :], c.causal[:, :], False, True, c.consts_made, signal=True)
                prob = softmax_tile(c, b, m, kb.buf[:, 0:n], probs.take(), small, i, 1.0, kb.made)
                if t == TT - 1:
                    kb.free = [prob.made]
                return prob

            def back(i, prob, state):
                t = i % TT
                if t == 0:
                    state.pt, state.marks = PT.take(), []
                state.marks.append(turn_tile(c, prob, t + 1, state.pt, t))

            def finish(h, pt, marks):
                p, hs = h // 2, slice(h % 2 * 64, h % 2 * 64 + 64)
                if h % 2 == 0:
                    o_of[p] = c.work.take()
                o = o_of[p]
                for j in range(TT):
                    m = c.mm(o.buf[hs, j * P:], V[:, j, p * P + hs.start:p * P + hs.stop], pt.buf[:, j, j * P:],
                             j == 0, j == TT - 1, o.wait, marks, v_made[p], signal=j == TT - 1)
                pt.free = [m]
                if h % 2:
                    v = c.stt(G[:, p, :], o.buf[:, :], 0.5, G[:, p, :], ALU.mult, ALU.mult, m, g_made[p])
                    o.free = [v]
                    out_made.append(v)

            run(blend(pipeline(FH * TT, TT, front, back, finish), coming, 3.6))
        return c.out_project("fox_out", [G[:, p, :] for p in range(DT)], out_made, c.x, x_marks)


def weight_plan(t):
    plan = []

    def add(key, name, *at, split=True):
        block = t[name]
        for i in at:
            block = block[i]
        width = P if block.shape[1] % P == 0 else block.shape[1] // DT
        plan.append((key, block, block.shape[1] // width, width, split))

    def ada(l, js):
        for j in js:
            add(("ada", l, j), "ada", l * 3 * DT + j, split=False)

    def out(name):
        for cb, part in out_order():
            add((name, cb, part), name, 2 * cb + part)

    def even(*js):
        for j in js:
            add(("even", j), "even_in", j)

    even(6 * DT, 4 * DT, 3 * DT, 5 * DT, DT, 0)
    for p in range(DT):
        if p + 1 < DT:
            even(4 * DT + p + 1)
            ada(0, [2 * DT + p])
            even(3 * DT + p + 1)
            ada(1, [3 * p])
            even(5 * DT + p + 1)
            ada(1, range(3 * p + 1, 3 * p + 3))
            even(DT + p + 1, p + 1)
            even(6 * DT + 1 + p)
        else:
            even(6 * DT + 1 + p)
            ada(0, [2 * DT + p])
            ada(1, range(3 * p, 3 * p + 3))
    even(*range(2 * DT, 3 * DT))
    out("even_out")
    add(("ki", 0), "odd_in", 2 * AH + 2 + IH // 2)
    add(("wi", 0), "odd_wi", 0)
    for i in range(IH // 2):
        add(("qi", i), "odd_in", AH + 2 + i)
    add(("k", 0), "odd_in", AH)
    add(("v", 0), "odd_in", AH + 1)
    for h in range(AH):
        add(("q", h), "odd_in", h)
    for h in range(AH):
        add(("g", h), "odd_in", AH + 2 + IH // 2 + h)
    out("odd_out")
    for n in range(LT):
        add(("lru", n), "lru_in", n)
        add(("lru", LT + n), "lru_in", LT + n)
    out("lru_out")
    add(("fox_f", 0), "fox_in", 4 * DT)
    for p in range(DT):
        for key, j in (("fox_q", 0), ("fox_k", 1), ("fox_g", 3), ("fox_v", 2)):
            add((key, p), "fox_in", j * DT + p)
    out("fox_out")
    return plan


def build(nc, t, debug=(), layers=4):
    with ExitStack() as ctx:
        c = Core(nc, t, ctx, debug)
        x = c.x
        marks = [c.dma(x[:, k, :], t["x_t"][k * P:(k + 1) * P, :], c.sem(f"x_in{k}")) for k in range(DT)]
        tables_scope = ctx.enter_context(ExitStack())
        c.tables = c.sb("tables", [P, 5, T], scope=tables_scope)
        c.chunk_q = c.sb("chunk_q_f", [P, TT], scope=tables_scope)
        even_scope = tables_scope.enter_context(ExitStack())
        masks = rwkv_masks(c, even_scope)
        with ExitStack() as scope:
            sq = c.ring("sq", 2, [P, T], scope, ())
            first = c.sb("ada_first", [P, 2 * DT, D], scope=scope)
            landed = [c.dma(first[:, j, :], t["ada"][j], c.sem(f"ada_in{j}")) for j in range(2 * DT)]
            for k in range(DT):
                summed = c.square_sum(x[:, k, :], k, marks[k], sq)
            c.look_ahead()
            for j in range(2 * DT):
                c.modulation_block(0, j, first[:, j, :], landed[j])
        c.norm_into_h(x, marks, c.inverse_rms(summed)[0], lambda k: c.gains[0][:, k:k + 1],
                      lambda k: c.mods[0][:, k:k + 1], c.mod_made[0])
        c.dump("h_hi", c.h_hi[:, :, :].bitcast(F32))
        marks, summed = even_layer(c, masks)
        even_scope.close()
        c.dump("x0", x[:, :, :])
        if layers > 1:
            c.norm_into_h(x, marks, c.inverse_rms(summed)[0], lambda k: c.gains[1][:, k:k + 1],
                          lambda k: c.mods[1][:, k:k + 1], c.mod_made[1])
            marks, summed = odd_layer(c, marks)
            c.dump("x1", x[:, :, :])
        tables_scope.close()
        if layers > 2:
            final, both = c.inverse_rms(summed, scaled=True)
            c.norm_into_h(x, marks, both, lambda k: c.gain_product[:, k:k + 1], None)
            for k in range(DT):
                marks[k] = c.stt(x[:, k, :], x[:, k, :], c.vec("final_g", k), final.buf[:, :], ALU.mult, ALU.mult,
                                 marks[k], final.made)
            final.free = [marks[DT - 1]]
            marks, summed = lru_layer(c, marks)
            c.dump("x2", x[:, :, :])
        if layers > 3:
            c.norm_into_h(x, marks, c.inverse_rms(summed)[0], lambda k: c.vec("norm2_g1", k), None)
            marks, summed = fox_layer(c, marks)
            c.dump("x3", x[:, :, :])
        inverse = c.inverse_rms(summed)[0]
        for k in range(DT):
            v = c.stt(x[:, k, :], x[:, k, :], c.vec("final2_g", k), inverse.buf[:, :], ALU.mult, ALU.mult, marks[k],
                      inverse.made)
            c.stores.append(c.dma(t["out"][k * P:(k + 1) * P, :], x[:, k, :], c.sem(f"out{k}"), v))

        with nc.Block() as block:
            @block.sync
            def _(e):
                for issue in c.SP.queue:
                    issue(e)
                for semaphore, value in c.stores:
                    e.wait_ge(semaphore, value)

            @block.tensor
            def _(e):
                for issue in c.PE.queue:
                    issue(e)

            @block.vector
            def _(e):
                for issue in c.DVE.queue:
                    issue(e)

            @block.scalar
            def _(e):
                for issue in c.ACTE.queue:
                    issue(e)

            @block.gpsimd
            def _(e):
                for issue in c.POOL.queue:
                    issue(e)


def blocks(w, width=P):
    k, n = w.shape
    return np.ascontiguousarray(w.reshape(k // P, P, n // width, width).transpose(2, 1, 0, 3)).reshape(
        n // width, P, (k // P) * width)


def half_blocks(w):
    k, n = w.shape
    return np.ascontiguousarray(w.reshape(2, k // (2 * P), P, n // P, P).transpose(3, 0, 2, 1, 4)).reshape(
        2 * n // P, P, k // 2)


def columns(v):
    v = v.reshape(-1, v.shape[-1] // P, P)
    return v.transpose(2, 0, 1).reshape(P, -1)


def kernel(debug=(), layers=4, **inputs):
    import concourse.bacc as bacc
    from concourse.bass_utils import run_bass_kernel_spmd

    a = {k: np.asarray(v) for k, v in inputs.items()}
    inverse = lambda d: (10000.0 ** (-np.arange(0, d, 2) / d)).astype(np.float32)
    conv = a["conv_w"][0, :, 0, :].reshape(TAPS, DT, P).transpose(2, 1, 0).reshape(P, DT * TAPS)
    fox_b = np.zeros((P, 1), np.float32)
    fox_b[:FH, 0] = a["fox_b_f_2"][0]
    vecs = [columns(a["ada_b"][0]), columns(a["ada_b"][1]), columns(a["norm_g"][0]),
            columns(a["norm_g"][1]), columns(a["final_g"]), conv, columns(a["conv_vec"][0]),
            columns(a["rwkv_mu_rkv"][0]), a["rwkv_mu_lora"][0].reshape(P, 1), columns(a["rwkv_vec"][0]),
            columns(a["rwkv_r_k"][0].reshape(-1)), np.tile(inverse(128), 2).reshape(P, 1),
            np.tile(inverse(64), 4).reshape(P, 1), columns(a["norm_g_2"][0]), columns(a["norm_g_2"][1]),
            columns(a["final_g_2"]), columns(a["lru_conv_w_2"][0]), columns(a["lru_conv_b_2"][0]),
            columns(a["lru_ba_2"][0]), columns(a["lru_bx_2"][0]), columns(a["lru_a_param_2"][0]), fox_b]
    odd = a["odd_w_in"][0]
    w, at = {}, 0
    for name, n in (("q", AH * P), ("k", P), ("v", P), ("qi", IH * 64), ("ki", 64), ("wi", IH), ("g", AH * P)):
        w[name] = odd[:, at:at + n]
        at += n
    pos = a["positions"].reshape(1, T)
    fox = a["fox_w_in_2"][0]
    arrays = {
        "x_t": np.ascontiguousarray(a["x"][0].T),
        "vecs": np.ascontiguousarray(np.concatenate(vecs, axis=1)),
        "c": np.ascontiguousarray(a["c"].reshape(1, D)),
        "ada": np.ascontiguousarray(a["ada_w"].transpose(0, 2, 1)).reshape(2 * 3 * DT, P, D),
        "even_in": blocks(a["even_w_in"][0]),
        "even_out": half_blocks(a["even_w_out"][0]),
        "lora_up": np.ascontiguousarray(np.concatenate([a["rwkv_w_up"][0], a["rwkv_a_up"][0]])),
        "odd_in": blocks(np.concatenate([w["q"], w["k"], w["v"], w["qi"], w["g"], w["ki"], w["ki"]], axis=1)),
        "odd_wi": blocks(np.concatenate([w["wi"], np.zeros((D, P - IH), np.float32)], axis=1)),
        "odd_out": half_blocks(a["odd_w_out"][0]),
        "pos": np.ascontiguousarray(pos),
        "pos_q": np.ascontiguousarray(pos.reshape(TT, P).T),
        "lru_in": blocks(a["lru_w_in_2"][0]),
        "lru_gates": np.ascontiguousarray(np.stack(
            [a[n][0].transpose(1, 0, 2).reshape(P, LRU) for n in ("lru_wa_2", "lru_wx_2")], axis=1)),
        "lru_out": half_blocks(a["lru_w_out_2"][0]),
        "fox_in": blocks(np.concatenate([fox, np.zeros((D, P - FH), np.float32)], axis=1)),
        "fox_out": half_blocks(a["fox_w_out_2"][0]),
    }
    nc = bacc.Bacc("TRN2", target_bir_lowering=False, num_devices=1)
    t = {k: nc.dram_tensor(k, list(v.shape), I32 if v.dtype.kind == "i" else F32, kind="ExternalInput").ap()
         for k, v in arrays.items()}
    t["out"] = nc.dram_tensor("out", [D, T], F32, kind="ExternalOutput").ap()
    sizes = {"ya": DT, "yb": DT, "x0": DT, "h_hi": DT, "x1": DT, "x2": DT, "x3": DT, "q": AH, "og": AH,
             "bias": TT, "lru_y": 8}
    for name in debug:
        t["dbg_" + name] = nc.dram_tensor("dbg_" + name, [P, sizes[name], T], F32, kind="ExternalOutput").ap()
    build(nc, t, debug, layers)
    result = run_bass_kernel_spmd(nc, [arrays], core_ids=[0])
    return np.ascontiguousarray(result.results[0]["out"].T).reshape(1, T, D)
```
